# Optimizing a Trainium2 kernel written in Bass

```python
import math
import jax, jax.numpy as jnp
from jax import lax
import numpy as np

D_MODEL = 1024
BATCH = 1
SEQ = 1024
DEPTH = 1
DEC_BATCH = 1
DEC_SEQ = 64
PAST_LEN = 128

CHUNK = 64
RET_HEADS = 4
RET_DK = 128
RET_DV = 256
SB_HEADS = 4
SB_D = 128
Q_BLOCK = 128
N_KEYS = 128
N_EXPERTS = N_KEYS * N_KEYS
PEER_HEADS = 8
PEER_DKEY = 256
PEER_HALF = PEER_DKEY // 2
PEER_TOPK = 16
PEER_BLOCK = 128
ROPE_BASE = 10000.0
EPS = 1e-6
N_BRANCH = 2
RET_QK_W = RET_HEADS * RET_DK
RET_V_W = RET_HEADS * RET_DV
SB_W = SB_HEADS * SB_D
SPLITS = [RET_QK_W, RET_QK_W, RET_V_W, RET_V_W, SB_W, SB_W, SB_W, N_BRANCH * D_MODEL]
IN_W = sum(SPLITS)

kernel_name = "retention_stickbreak_peer_stream_step"

F32 = jnp.float32

def rms_norm(x, g):
    xf = x.astype(F32)
    y = xf * lax.rsqrt(jnp.mean(xf * xf, axis=-1, keepdims=True) + EPS)
    return (y * g.astype(F32)).astype(x.dtype)

def rotary(x, pos):
    d = x.shape[-1]
    inv = ROPE_BASE ** (-jnp.arange(0, d, 2, dtype=F32) / d)
    ang = pos.astype(F32)[:, None] * inv[None, :]
    cos = jnp.cos(ang)[None, :, None, :]
    sin = jnp.sin(ang)[None, :, None, :]
    xf = x.astype(F32)
    x1, x2 = xf[..., : d // 2], xf[..., d // 2:]
    return jnp.concatenate([x1 * cos - x2 * sin, x1 * sin + x2 * cos], axis=-1).astype(x.dtype)

def retention_log_decay():
    return jnp.log(1.0 - 2.0 ** (-5.0 - jnp.arange(RET_HEADS, dtype=F32)))

def retention_chunk(S, q, k, v):
    q = q.astype(F32)
    k = k.astype(F32)
    v = v.astype(F32)
    S = S.astype(F32)
    T = q.shape[1]
    log_g = retention_log_decay()
    i = jnp.arange(T, dtype=F32)
    dist = jnp.abs(i[:, None] - i[None, :])
    dmat = jnp.exp(dist[None] * log_g[:, None, None])
    scores = jnp.einsum('bqhd,bkhd->bhqk', q, k) * dmat[None]
    o = jnp.einsum('bhqk,bkhe->bqhe', scores, v)
    inter = jnp.exp((i[:, None] + 1.0) * log_g[None, :])
    o = o + jnp.einsum('bqhd,bhde->bqhe', q, S) * inter[None, :, :, None]
    kdec = jnp.exp((T - 1.0 - i)[:, None] * log_g[None, :])
    S_new = jnp.exp(T * log_g)[None, :, None, None] * S + jnp.einsum('bkhd,kh,bkhe->bhde', k, kdec, v)
    return o, S_new

def sb_attend(q, k, v, q_pos, k_pos):
    z = jnp.einsum('bqhd,bkhd->bhqk', q, k).astype(F32) * (SB_D ** -0.5)
    mask = (k_pos[None, :] < q_pos[:, None])[None, None]
    log_fail = jnp.where(mask, jax.nn.log_sigmoid(-z), 0.0)
    after = lax.cumsum(log_fail, axis=3, reverse=True) - log_fail
    w = jnp.where(mask, jnp.exp(jax.nn.log_sigmoid(z) + after), 0.0)
    return jnp.einsum('bhqk,bkhd->bqhd', w.astype(v.dtype), v)

def project_inputs(h, w_in, pos):
    B, T, _ = h.shape
    p = h @ w_in
    offs = np.cumsum(SPLITS)[:-1].tolist()
    rq, rk, rv, rg, sq, sk, sv, gt = jnp.split(p, offs, axis=-1)
    rq = rotary(rq.reshape(B, T, RET_HEADS, RET_DK), pos)
    rk = rotary(rk.reshape(B, T, RET_HEADS, RET_DK), pos) * (RET_DK ** -0.5)
    rv = rv.reshape(B, T, RET_HEADS, RET_DV)
    sq = sq.reshape(B, T, SB_HEADS, SB_D)
    sk = sk.reshape(B, T, SB_HEADS, SB_D)
    sv = sv.reshape(B, T, SB_HEADS, SB_D)
    gates = jax.nn.sigmoid(gt.reshape(B, T, N_BRANCH, D_MODEL).astype(F32)).astype(h.dtype)
    return rq, rk, rv, rg, sq, sk, sv, gates

def peer_ffn(h, w_pq, pk_keys, peer_u, peer_v):
    B, T, D = h.shape
    x = h.reshape(-1, D)
    n = x.shape[0]
    n_pad = (-n) % PEER_BLOCK
    xb_all = jnp.pad(x, ((0, n_pad), (0, 0))).reshape(-1, PEER_BLOCK, D)

    def block(xb):
        q = (xb @ w_pq).reshape(PEER_BLOCK, PEER_HEADS, 2, PEER_HALF)
        s = jnp.einsum('nhpc,phkc->nhpk', q, pk_keys).astype(F32)
        v1, i1 = lax.top_k(s[:, :, 0], PEER_TOPK)
        v2, i2 = lax.top_k(s[:, :, 1], PEER_TOPK)
        cand = (v1[..., :, None] + v2[..., None, :]).reshape(PEER_BLOCK, PEER_HEADS, PEER_TOPK * PEER_TOPK)
        cidx = (i1[..., :, None] * N_KEYS + i2[..., None, :]).reshape(PEER_BLOCK, PEER_HEADS, PEER_TOPK * PEER_TOPK)
        sc, sel = lax.top_k(cand, PEER_TOPK)
        eidx = jnp.take_along_axis(cidx, sel, axis=-1)
        g = jax.nn.softmax(sc, axis=-1)
        u = peer_u[eidx]
        a = jax.nn.gelu(jnp.einsum('nhkd,nd->nhk', u, xb).astype(F32))
        coef = (g * a).astype(peer_v.dtype)
        return jnp.einsum('nhk,nhkd->nd', coef, peer_v[eidx])

    out = lax.map(block, xb_all).reshape(-1, D)[:n]
    return out.reshape(B, T, D).astype(h.dtype)

def merge_and_channel_mix(x, ret_o, rg, sb_o, gates, ret_gn_w, w_ret_o, w_sb_o, w_out,
                          norm2_w, w_pq, pk_keys, peer_u, peer_v):
    B, T, _ = x.shape
    mu = jnp.mean(ret_o, axis=-1, keepdims=True)
    var = jnp.mean((ret_o - mu) ** 2, axis=-1, keepdims=True)
    r = ((ret_o - mu) * lax.rsqrt(var + EPS)).reshape(B, T, RET_V_W) * ret_gn_w.astype(F32)
    r = (jax.nn.silu(rg.astype(F32)) * r).astype(x.dtype)
    ret_branch = r @ w_ret_o
    sb_branch = sb_o.reshape(B, T, SB_W).astype(x.dtype) @ w_sb_o
    mixed = gates[:, :, 0] * ret_branch + gates[:, :, 1] * sb_branch
    x = x + mixed @ w_out
    x = x + peer_ffn(rms_norm(x, norm2_w), w_pq, pk_keys, peer_u, peer_v)
    return x

def prompt_layer(x, norm1_w, w_in, ret_gn_w, w_ret_o, w_sb_o, w_out, norm2_w, w_pq, pk_keys, peer_u, peer_v):
    B, T, _ = x.shape
    pos = jnp.arange(T, dtype=jnp.int32)
    h = rms_norm(x, norm1_w)
    rq, rk, rv, rg, sq, sk, sv, gates = project_inputs(h, w_in, pos)
    nc = T // CHUNK

    def to_chunks(a):
        return a.reshape(B, nc, CHUNK, *a.shape[2:]).swapaxes(0, 1)

    def step(S, qkv):
        o, S_new = retention_chunk(S, *qkv)
        return S_new, o

    S0 = jnp.zeros((B, RET_HEADS, RET_DK, RET_DV), F32)
    S_fin, ret_o = lax.scan(step, S0, (to_chunks(rq), to_chunks(rk), to_chunks(rv)))
    ret_o = ret_o.swapaxes(0, 1).reshape(B, T, RET_HEADS, RET_DV)
    nb = T // Q_BLOCK
    qb = sq.reshape(B, nb, Q_BLOCK, SB_HEADS, SB_D).swapaxes(0, 1)
    pb = pos.reshape(nb, Q_BLOCK)
    sb_o = lax.map(lambda a: sb_attend(a[0], sk, sv, a[1], pos), (qb, pb))
    sb_o = sb_o.swapaxes(0, 1).reshape(B, T, SB_HEADS, SB_D)
    y = merge_and_channel_mix(x, ret_o, rg, sb_o, gates, ret_gn_w, w_ret_o, w_sb_o, w_out,
                              norm2_w, w_pq, pk_keys, peer_u, peer_v)
    return y, sk, sv, S_fin.astype(x.dtype)

def sample_layer(x, past_k, past_v, S_past, norm1_w, w_in, ret_gn_w, w_ret_o, w_sb_o, w_out,
                 norm2_w, w_pq, pk_keys, peer_u, peer_v):
    B, T, _ = x.shape
    P = past_k.shape[1]
    pos = P + jnp.arange(T, dtype=jnp.int32)
    h = rms_norm(x, norm1_w)
    rq, rk, rv, rg, sq, sk, sv, gates = project_inputs(h, w_in, pos)
    ret_o, S_new = retention_chunk(S_past, rq, rk, rv)
    k_all = jnp.concatenate([past_k.astype(sk.dtype), sk], axis=1)
    v_all = jnp.concatenate([past_v.astype(sv.dtype), sv], axis=1)
    k_pos = jnp.arange(P + T, dtype=jnp.int32)
    sb_o = sb_attend(sq, k_all, v_all, pos, k_pos)
    y = merge_and_channel_mix(x, ret_o, rg, sb_o, gates, ret_gn_w, w_ret_o, w_sb_o, w_out,
                              norm2_w, w_pq, pk_keys, peer_u, peer_v)
    return y, sk, sv, S_new.astype(S_past.dtype)

def setup_inputs(seed: int = 0) -> dict:
    key = jax.random.key(seed)
    ks = jax.random.split(key, 20)
    nrm = jax.random.normal
    D = D_MODEL
    return {
        "x_prompt": nrm(ks[0], (BATCH, SEQ, D), F32),
        "x_sample": nrm(ks[1], (DEC_BATCH, DEC_SEQ, D), F32),
        "cache_sb_k": nrm(ks[2], (DEPTH, DEC_BATCH, PAST_LEN, SB_HEADS, SB_D), F32),
        "cache_sb_v": nrm(ks[3], (DEPTH, DEC_BATCH, PAST_LEN, SB_HEADS, SB_D), F32),
        "state_ret": 0.1 * nrm(ks[4], (DEPTH, DEC_BATCH, RET_HEADS, RET_DK, RET_DV), F32),
        "norm1_w": 1.0 + 0.01 * nrm(ks[5], (DEPTH, D), F32),
        "w_in": nrm(ks[6], (DEPTH, D, IN_W), F32) * D ** -0.5,
        "ret_gn_w": 1.0 + 0.01 * nrm(ks[7], (DEPTH, RET_V_W), F32),
        "w_ret_o": nrm(ks[8], (DEPTH, RET_V_W, D), F32) * RET_V_W ** -0.5,
        "w_sb_o": nrm(ks[9], (DEPTH, SB_W, D), F32) * SB_W ** -0.5,
        "w_out": nrm(ks[10], (DEPTH, D, D), F32) * D ** -0.5,
        "norm2_w": 1.0 + 0.01 * nrm(ks[11], (DEPTH, D), F32),
        "w_pq": nrm(ks[12], (DEPTH, D, PEER_HEADS * PEER_DKEY), F32) * D ** -0.5,
        "pk_keys": nrm(ks[13], (DEPTH, 2, PEER_HEADS, N_KEYS, PEER_HALF), F32) * PEER_HALF ** -0.5,
        "peer_u": nrm(ks[14], (DEPTH, N_EXPERTS, D), F32) * D ** -0.5,
        "peer_v": nrm(ks[15], (DEPTH, N_EXPERTS, D), F32) * PEER_HEADS ** -0.5,
        "norm_f_w": 1.0 + 0.01 * nrm(ks[16], (D,), F32),
    }

def reference(x_prompt, x_sample, cache_sb_k, cache_sb_v, state_ret, norm1_w, w_in, ret_gn_w,
              w_ret_o, w_sb_o, w_out, norm2_w, w_pq, pk_keys, peer_u, peer_v, norm_f_w):
    xp = x_prompt
    xs = x_sample
    pk_list, pv_list, ps_list = [], [], []
    sk_list, sv_list, ss_list = [], [], []
    for l in range(DEPTH):
        xp, kp, vp, Sp = prompt_layer(xp, norm1_w[l], w_in[l], ret_gn_w[l], w_ret_o[l], w_sb_o[l],
                                      w_out[l], norm2_w[l], w_pq[l], pk_keys[l], peer_u[l], peer_v[l])
        xs, ksn, vsn, Ss = sample_layer(xs, cache_sb_k[l], cache_sb_v[l], state_ret[l], norm1_w[l], w_in[l],
                                        ret_gn_w[l], w_ret_o[l], w_sb_o[l], w_out[l], norm2_w[l],
                                        w_pq[l], pk_keys[l], peer_u[l], peer_v[l])
        pk_list.append(kp)
        pv_list.append(vp)
        ps_list.append(Sp)
        sk_list.append(ksn)
        sv_list.append(vsn)
        ss_list.append(Ss)
    y_prompt = rms_norm(xp, norm_f_w)
    y_sample = rms_norm(xs, norm_f_w)
    prompt_sb_k = jnp.stack(pk_list)
    prompt_sb_v = jnp.stack(pv_list)
    prompt_ret_state = jnp.stack(ps_list)
    sample_sb_k = jnp.stack(sk_list)
    sample_sb_v = jnp.stack(sv_list)
    sample_ret_state = jnp.stack(ss_list)
    return (y_prompt, y_sample, prompt_sb_k, prompt_sb_v, prompt_ret_state, sample_sb_k, sample_sb_v, sample_ret_state)


_drawn_inputs = setup_inputs


def setup_inputs(seed=0):
    import zlib

    import numpy as np

    out = dict(_drawn_inputs(seed))
    spreads = {}
    factors = {'norm1_w': 3.34,
     'ret_gn_w': 30.589,
     'norm2_w': 26.672,
     'norm_f_w': 185.004,
     'cache_sb_k': 17.718,
     'cache_sb_v': 13.694,
     'state_ret': 4.519}
    for name, (base, spread) in spreads.items():
        noise = np.random.default_rng([zlib.crc32(name.encode()), seed]).standard_normal(out[name].shape)
        drawn = base * np.exp(spread * noise) if base else spread * noise
        out[name] = __import__('jax').numpy.asarray(drawn.astype(out[name].dtype))
    for name, factor in factors.items():
        out[name] = (out[name] * factor).astype(out[name].dtype)
    return out
```

```python
from contextlib import ExitStack

import numpy as np

import concourse.bass as bass
from concourse import mybir

F32 = mybir.dt.float32
U32 = mybir.dt.uint32
ALU = mybir.AluOpType
ACT = mybir.ActivationFunctionType
AX_X = mybir.AxisListType.X

P = 128
D = 1024
KD = D // P
SEQ = 1024
TILES = SEQ // P
SAMPLE = 64
PAST = 128
TOKENS = SEQ + SAMPLE
CHUNK = 64
HEADS = 4
DK = 128
DV = 256
BANK = 512
RQ, RV, RG, SQ, SK, SV, GT = 0, 1024, 2048, 3072, 3584, 4096, 4608
IN_W = 6656
N_CHUNKS = IN_W // BANK
KEYS = 128
PHEADS = 8
TOPK = 16
SLOTS = PHEADS * TOPK
SIDES = 2 * PHEADS
PQ_W = SIDES * P
RING = 8
EPS = 1e-6
LOWEST = -3.0e38
SCORE_SCALE = float(DK) ** -0.5


def host_constants():
    log_g = np.log(1.0 - 2.0 ** (-5.0 - np.arange(HEADS)))
    i = np.arange(P)
    row, col = i[:, None], i[None, :]
    seen = (row // CHUNK) <= (col // CHUNK)
    decay = np.stack([np.where(seen, np.exp(g * (np.abs(row - col) - (col + 1.0))), 0.0) for g in log_g], 1)
    k_dec = np.exp((P - 1.0 - i)[:, None] * log_g[None, :])
    k_dec_sample = np.exp((SAMPLE - 1.0 - i)[:, None] * log_g[None, :])
    parts = {
        "ident": np.eye(P),
        "neg_tri": -(row >= col).astype(np.float64),
        "neg_ones": -np.ones((P, P)),
        "decay": (decay * SCORE_SCALE).reshape(P, HEADS * P),
        "k_dec": np.repeat(k_dec * SCORE_SCALE, DK, axis=1),
        "k_dec_sample": np.repeat(k_dec_sample * SCORE_SCALE, DK, axis=1),
        "inter": np.exp((i[:, None] + 1.0) * log_g[None, :]),
        "iota16": np.tile(np.arange(TOPK), (P, 1)),
        "eps": np.full((P, 1), EPS),
        "one": np.ones((P, 1)),
    }
    at, where = 0, {}
    for name, a in parts.items():
        where[name] = (at, at + a.shape[1])
        at += a.shape[1]
    table = np.concatenate(list(parts.values()), 1).astype(np.float32)
    inv = (np.float32(10000.0) ** (-np.arange(0, DK, 2, dtype=np.float32) / np.float32(DK))).astype(np.float32)
    ang = np.arange(SEQ, dtype=np.float32)[:, None] * inv[None, :]
    rope = np.concatenate([np.cos(ang), np.sin(ang)], 1).astype(np.float32)
    return table, where, rope


CONST_TABLE, CONST_AT, ROPE_TABLE = host_constants()


def gamma_to(steps):
    return [float((1.0 - 2.0 ** (-5.0 - h)) ** steps) for h in range(HEADS)]


class Chain:

    def __init__(self, eng, sem, start):
        self.eng, self.sem, self.start, self.n = eng, sem, start, 0

    def then(self, ins):
        self.n += 1
        return ins.then_inc(self.sem, 1)

    def wait(self):
        self.eng.wait_ge(self.sem, self.start + self.n)

    def hold(self, hold):
        hold(self.eng, self.sem, self.start + self.n)


class Hold:

    def __init__(self, passed):
        self.passed = passed

    def __call__(self, eng, sem, value):
        eng.wait_ge(sem, value)
        if not isinstance(value, int):
            eng.sem_inc(self.passed, 1)


def broadcast_rows(vec, rows):
    return vec.rearrange("(a n) -> a n", a=1).to_broadcast([rows, vec.shape[0]])


def rstd_newton(dve, chain, m, root, rstd, tmp, scale):
    chain.then(dve.tensor_scalar(m, m, scale, EPS, ALU.mult, ALU.add))
    chain.then(dve.reciprocal(rstd, root))
    chain.wait()
    chain.then(dve.tensor_tensor(tmp, rstd, rstd, ALU.mult))
    chain.wait()
    chain.then(dve.tensor_tensor(tmp, tmp, m, ALU.mult))
    chain.wait()
    chain.then(dve.tensor_scalar(tmp, tmp, -0.5, 1.5, ALU.mult, ALU.add))
    chain.wait()
    chain.then(dve.tensor_tensor(rstd, rstd, tmp, ALU.mult))
    chain.wait()


NEWTON_STEPS = 6


def first(n):
    return isinstance(n, int) and n == 0


def token_col(n):
    return SEQ if first(n) else (n - 1) * P


def thirds(ap):
    return ap.rearrange("p (k r) -> p k r", r=P)


def build(nc, x_prompt, x_sample, cache_k, cache_v, state_ret, norm1_w, w_in, ret_gn_w, w_ret_o, w_sb_o,
          w_out, norm2_w, w_pq, pk_keys, peer_u, peer_v, norm_f_w, consts, rope,
          y_prompt, y_sample, prompt_k, prompt_v, prompt_state, sample_k, sample_v, sample_state):
    scratch = lambda n, s: nc.dram_tensor(n, s, F32).ap()
    proj = scratch("proj", [TOKENS, IN_W])
    skT_d = scratch("skT_d", [TILES, P, HEADS * P])
    x2_d = scratch("x2_d", [TOKENS, D])
    h2_d = scratch("h2_d", [TOKENS, D])
    h2T_d = scratch("h2T_d", [(TILES + 1) * P, KD * P])
    with ExitStack() as ctx:
        sb = lambda n, s, d=F32: ctx.enter_context(nc.sbuf_tensor(n, s, d))
        sem = lambda n: ctx.enter_context(nc.semaphore(n))
        pair = [ctx.enter_context(nc.psum_tensor(f"pair{i}", [P, 2 * BANK], F32)) for i in range(4)]
        cst = sb("cst", [P, CONST_TABLE.shape[1]])
        C = {k: cst[:, a:b] for k, (a, b) in CONST_AT.items()}
        hold = Hold(sem("passed"))
        project(nc, sem, hold, pair, C, cst, consts, x_prompt, x_sample, norm1_w, w_in, proj)
        mix(nc, sem, hold, pair, C, cst, x_prompt, x_sample, cache_k, cache_v, state_ret, ret_gn_w, w_ret_o, w_sb_o, w_out,
            norm2_w, rope, proj, skT_d, x2_d, h2_d, h2T_d, prompt_k, prompt_v, prompt_state, sample_k, sample_v,
            sample_state)
        eidx = sb("eidx", [P, (TILES + 1) * SLOTS], U32)
        gate = sb("gate", [P, (TILES + 1) * SLOTS])
        route(nc, sem, hold, pair, C, w_pq, pk_keys, h2T_d, eidx, gate)
        experts(nc, sem, hold, pair, C, peer_u, peer_v, norm_f_w, x2_d, h2_d, eidx, gate, y_prompt, y_sample)



def project(nc, sem, hold, pair, C, cst, consts, x_prompt, x_sample, norm1_w, w_in, proj):
    NT = TILES + 1
    OUTS = 3
    order = [(t * P, P) for t in range(TILES)] + [(SEQ, SAMPLE)]
    ps_out = [pair[1][:, 0:BANK], pair[1][:, BANK:2 * BANK], pair[2][:, 0:BANK]]
    with ExitStack() as ctx:
        sb = lambda n, s, d=F32: ctx.enter_context(nc.sbuf_tensor(n, s, d))
        hT = sb("hT", [P, KD, TOKENS])
        w = sb("w", [P, 2, KD, BANK])
        out_sb = sb("out_sb", [P, OUTS, BANK])
        xt = sb("xt", [P, D])
        xsq = sb("xsq", [P, D])
        xn = sb("xn", [P, D])
        g1 = sb("g1", [P, D])
        st = sb("st", [P, 4])
        w_v = w_in[0].rearrange("(k p) n -> p k n", p=P)

        consts_in, g_in, x_in = sem("a_consts_in"), sem("a_g_in"), sem("a_x_in")
        squares, normed, turned = sem("a_squares"), sem("a_normed"), sem("a_turned")
        hT_act, hT_dve, dve_own = sem("a_hT_act"), sem("a_hT_dve"), sem("a_dve_own")
        w_loaded = [sem(f"a_w_loaded{i}") for i in range(2)]
        ps_ready = [sem(f"a_ps_ready{i}") for i in range(OUTS)]
        copied = [sem(f"a_copied{i}") for i in range(OUTS)]
        stored = [sem(f"a_stored{i}") for i in range(OUTS)]

        def chunks(eng, one):
            one(0, 0)
            with eng.Fori(0, N_CHUNKS // 2) as c2:
                one(c2 * 2 + 1, 1)
                one(c2 * 2 + 2, 0)

        def copy(eng, c, i, rows, buf):
            s, use = i % OUTS, c * (NT // OUTS) + i // OUTS
            eng.wait_ge(ps_ready[s], use + 1)
            if not (isinstance(c, int) and i < OUTS):
                eng.wait_ge(stored[s], 16 * use)
            if i % 2 == 0:
                ins = eng.activation(out_sb[0:rows, s, :], ps_out[s][0:rows], ACT.Copy)
            else:
                ins = eng.tensor_copy(out_sb[0:rows, s, :], ps_out[s][0:rows])
            ins.then_inc(copied[s], 1)

        with nc.Block() as block:
            @block.sync
            def _(sp):
                sp.dma_start(xt[0:SAMPLE, :], x_sample[0]).then_inc(x_in, 16)
                sp.dma_start(cst[:, :], consts).then_inc(consts_in, 16)
                sp.dma_start(g1[:, :], broadcast_rows(norm1_w[0], P)).then_inc(g_in, 16)
                with sp.Fori(0, TILES) as t:
                    hold(sp, normed, t + 1)
                    sp.dma_start(xt[:, :], x_prompt[0, bass.ds(t * P, P), :]).then_inc(x_in, 16)

                def store(c, buf):
                    for i, (row, rows) in enumerate(order):
                        hold(sp, copied[i % OUTS], c * (NT // OUTS) + i // OUTS + 1)
                        sp.dma_start(proj[row:row + rows, bass.ds(c * BANK, BANK)],
                                     out_sb[0:rows, i % OUTS, :]).then_inc(stored[i % OUTS], 16)
                chunks(sp, store)
                for s in stored:
                    hold(sp, s, 16 * N_CHUNKS * (NT // OUTS))

            @block.gpsimd
            def _(pool):
                def load(c, buf):
                    if not isinstance(c, int):
                        hold(pool, ps_ready[(NT - 1) % OUTS], (c - 1) * (NT // OUTS))
                    pool.dma_start(w[:, buf], w_v[:, :, bass.ds(c * BANK, BANK)]).then_inc(w_loaded[buf], 16)
                load(0, 0)
                load(1, 1)
                with pool.Fori(0, (N_CHUNKS - 3) // 2) as c2:
                    load(c2 * 2 + 2, 0)
                    load(c2 * 2 + 3, 1)
                hold(pool, ps_ready[(NT - 1) % OUTS], (N_CHUNKS - 2) * (NT // OUTS))
                load(N_CHUNKS - 1, 0)

            @block.scalar
            def _(act):
                act.wait_ge(consts_in, 16)

                def tile(n, rows):
                    r = slice(0, rows)
                    act.wait_ge(x_in, (n + 1) * 16)
                    if not first(n):
                        act.wait_ge(normed, n)
                    act.activation(xsq[r, :], xt[r, :], ACT.Square, accum_out=st[r, 0:1]).then_inc(squares, 1)
                    act.wait_ge(squares, 2 * n + 1)
                    act.activation(st[r, 1:2], st[r, 0:1], ACT.Sqrt, scale=1.0 / D,
                                   bias=C["eps"][r]).then_inc(squares, 1)
                    act.wait_ge(turned, n + 1)
                    act.activation(hT[:, 4:8, bass.ds(token_col(n), rows)],
                                   thirds(pair[0][:, BANK:])[:, :, r], ACT.Copy).then_inc(hT_act, 1)
                tile(0, SAMPLE)
                with act.Fori(0, TILES) as t:
                    tile(t + 1, P)

                def copy_out(c, buf):
                    for i, (row, rows) in enumerate(order):
                        if i % 2 == 0:
                            copy(act, c, i, rows, buf)
                chunks(act, copy_out)

            @block.vector
            def _(dve):
                dve.wait_ge(g_in, 16)

                def tile(n, rows):
                    r = slice(0, rows)
                    chain = Chain(dve, dve_own, n * NEWTON_STEPS)
                    dve.wait_ge(squares, 2 * n + 2)
                    rstd_newton(dve, chain, st[r, 0:1], st[r, 1:2], st[r, 2:3], st[r, 3:4], 1.0 / D)
                    if not first(n):
                        dve.wait_ge(turned, n)
                    dve.scalar_tensor_tensor(out=xn[r, :], in0=xt[r, :], scalar=st[r, 2:3], in1=g1[r, :],
                                             op0=ALU.mult, op1=ALU.mult).then_inc(normed, 1)
                    dve.wait_ge(turned, n + 1)
                    dve.tensor_copy(hT[:, 0:4, bass.ds(token_col(n), rows)],
                                    thirds(pair[0][:, 0:BANK])[:, :, r]).then_inc(hT_dve, 1)
                tile(0, SAMPLE)
                with dve.Fori(0, TILES) as t:
                    tile(t + 1, P)

                def copy_out(c, buf):
                    for i, (row, rows) in enumerate(order):
                        if i % 2 == 1:
                            copy(dve, c, i, rows, buf)
                chunks(dve, copy_out)

            @block.tensor
            def _(pe):
                pe.wait_ge(consts_in, 16)

                def tile(n, rows):
                    pe.wait_ge(normed, n + 1)
                    if not first(n):
                        pe.wait_ge(hT_act, n)
                        pe.wait_ge(hT_dve, n)
                    for k in range(KD):
                        last = pe.transpose(pair[0][:, k * P:k * P + rows], xn[0:rows, k * P:(k + 1) * P],
                                            C["ident"][0:rows, 0:rows])
                    last.then_inc(turned, 1)
                tile(0, SAMPLE)
                with pe.Fori(0, TILES) as t:
                    tile(t + 1, P)
                pe.wait_ge(hT_act, NT)
                pe.wait_ge(hT_dve, NT)

                def multiply(c, buf):
                    pe.wait_ge(w_loaded[buf], (c - buf) * 8 + 16)
                    for i, (row, rows) in enumerate(order):
                        s, use = i % OUTS, c * (NT // OUTS) + i // OUTS
                        if not (isinstance(c, int) and i < OUTS):
                            pe.wait_ge(copied[s], use)
                        for k in range(KD):
                            last = pe.matmul(ps_out[s][0:rows], hT[:, k, row:row + rows], w[:, buf, k, :],
                                             start=(k == 0), stop=(k == KD - 1))
                        last.then_inc(ps_ready[s], 1)

                chunks(pe, multiply)


def mix(nc, sem, hold, pair, C, cst, x_prompt, x_sample, cache_k, cache_v, state_ret, ret_gn_w, w_ret_o, w_sb_o, w_out,
        norm2_w, rope, proj, skT_d, x2_d, h2_d, h2T_d, prompt_k, prompt_v, prompt_state, sample_k, sample_v,
        sample_state):
    NT = TILES + 1
    qT_ps, kT_ps = pair[0][:, 0:BANK], pair[0][:, BANK:]
    sqT_ps, skT_ps = pair[1][:, 0:BANK], pair[1][:, BANK:]
    scores_ps = pair[2][:, 0:BANK]
    state_ps = pair[3]
    ret_ps = pair[0]
    z_ps, suffix_ps = pair[1][:, 0:BANK], pair[1][:, BANK:]
    sboT_ps = pair[2][:, 0:BANK]
    turn_ps = pair[3]
    retb_ps, sbb_ps, res_ps = pair[0], pair[2], pair[1]
    with ExitStack() as ctx:
        sb = lambda n, s, d=F32: ctx.enter_context(nc.sbuf_tensor(n, s, d))
        wret = sb("wret", [P, KD, D])
        wsb = sb("wsb", [P, HEADS, D])
        wout = sb("wout", [P, KD, D])
        gnw = sb("gnw", [P, D])
        g2 = sb("g2", [P, D])
        qk = sb("qk", [P, 1024])
        cs = sb("cs", [P, P])
        rv = sb("rv", [P, D])
        sqkv = sb("sqkv", [P, 3 * BANK])
        rg = sb("rg", [P, D])
        gates = sb("gates", [P, 2 * D])
        x = sb("x", [P, D])
        rot = sb("rot", [P, 1024])
        ra = sb("ra", [P, 1024])
        rb = sb("rb", [P, 1024])
        kd = sb("kd", [P, BANK])
        qT = sb("qT", [P, BANK])
        kT = sb("kT", [P, BANK])
        pT = sb("pT", [P, BANK])
        S = sb("S", [P, HEADS, DV])
        ret = sb("ret", [P, D])
        stats = sb("stats", [P, HEADS, 6])
        mv = sb("mv", [P, HEADS, 2])
        gst = sb("gst", [P, 3, HEADS])
        sqT = sb("sqT", [P, BANK])
        skT = sb("skT", [P, BANK])
        KT = sb("KT", [P, BANK])
        V = sb("V", [P, BANK])
        az = sb("az", [P, BANK])
        sp = sb("sp", [P, BANK])
        spsum = sb("spsum", [P, BANK])
        wT = sb("wT", [P, BANK])
        sboT = sb("sboT", [P, BANK])
        big = sb("big", [P, D])
        turnedT = sb("turnedT", [P, KD, P])
        n2 = sb("n2", [P, 4])

        names = ("weights_in qk_in rv_in sqkv_in rg_in gates_in x_in k_in v_in cache_in s_in s_zero dve act qk_rot "
                 "kd_rdy qk_turned qkT_rdy sq_turned skT_rdy scores_rdy pT_rdy state_mm o_rdy ret_rdy S_new sig_rdy "
                 "var_rdy root_rdy r_rdy z_rdy ln_rdy sp_rdy sp_masked suffix_rdy spsum_rdy w_rdy w_masked pv_done "
                 "sbo_rdy r_turned rT_rdy retb_rdy sbb_rdy mixed_rdy m_turned mT_rdy res_rdy x2_rdy sq2_rdy h2_rdy "
                 "h2_turned h2T_rdy kv_out skT_out x2_out h2_out h2T_out state_out cache_turned cacheT_rdy").split()
        s = {n: sem("b_" + n) for n in names}

        def block_no(n, j=0):
            return j if first(n) else 2 + (n * (n - 1)) // 2 + j

        def h4(ap, cols=P):
            return ap.rearrange("p (h r) -> p h r", h=HEADS)[:, :, 0:cols]

        def tiles(eng, tile):
            tile(0, SAMPLE)
            tile(1, P)
            with eng.Fori(2, NT) as n:
                tile(n, P)

        def past_blocks(eng, n, block):
            if first(n):
                block(block_no(0, 1), 1)
            elif not isinstance(n, int):
                with eng.Fori(1, n) as j:
                    block(block_no(n) + j, j)

        def past_no(n, j):
            return ((n - 1) * (n - 2)) // 2 + j

        with nc.Block() as block:
            @block.sync
            def _(sy):
                sy.dma_start(wret[:], w_ret_o[0].rearrange("(k p) n -> p k n", p=P)).then_inc(s["weights_in"], 16)
                sy.dma_start(wsb[:], w_sb_o[0].rearrange("(k p) n -> p k n", p=P)).then_inc(s["weights_in"], 16)
                sy.dma_start(wout[:], w_out[0].rearrange("(k p) n -> p k n", p=P)).then_inc(s["weights_in"], 16)
                sy.dma_start(gnw[:, :], broadcast_rows(ret_gn_w[0], P)).then_inc(s["weights_in"], 16)
                sy.dma_start(g2[:, :], broadcast_rows(norm2_w[0], P)).then_inc(s["weights_in"], 16)

                def tile(n, rows):
                    r = slice(0, rows)
                    at = bass.ds(token_col(n), rows)
                    pos = bass.ds(PAST if first(n) else token_col(n), rows)
                    if not first(n):
                        hold(sy, s["qk_rot"], n)
                    sy.dma_start(qk[r, :], proj[at, RQ:RV]).then_inc(s["qk_in"], 16)
                    sy.dma_start(cs[r, :], rope[pos, :]).then_inc(s["qk_in"], 16)
                    if not first(n):
                        hold(sy, s["o_rdy"], n)
                    sy.dma_start(rv[r, :], proj[at, RV:RG]).then_inc(s["rv_in"], 16)
                    if not first(n):
                        hold(sy, s["sq_turned"], n)
                        hold(sy, s["pv_done"], block_no(n - 1) + 1)
                        hold(sy, s["kv_out"], 32 * n)
                    sy.dma_start(sqkv[r, :], proj[at, SQ:GT]).then_inc(s["sqkv_in"], 16)
                    if not first(n):
                        hold(sy, s["r_rdy"], n)
                    sy.dma_start(rg[r, :], proj[at, RG:SQ]).then_inc(s["rg_in"], 16)
                    if not first(n):
                        hold(sy, s["mixed_rdy"], n)
                    sy.dma_start(gates[r, :], proj[at, GT:IN_W]).then_inc(s["gates_in"], 16)
                    if not first(n):
                        hold(sy, s["x2_out"], 16 * n)
                        hold(sy, s["h2_rdy"], n)
                    sy.dma_start(x[r, :], x_sample[0] if first(n) else x_prompt[0, at, :]).then_inc(s["x_in"], 16)
                tiles(sy, tile)

            @block.gpsimd
            def _(pool):
                pool.dma_start(az[:, :], cache_k[0, 0].rearrange("t h d -> t (h d)")).then_inc(s["cache_in"], 16)
                pool.dma_start(V[:, :], cache_v[0, 0].rearrange("t h d -> t (h d)")).then_inc(s["v_in"], 16)
                pool.dma_start(S[:], state_ret[0, 0].rearrange("h k v -> k h v")).then_inc(s["s_in"], 16)

                def tile(n, rows):
                    r = slice(0, rows)
                    at = bass.ds(token_col(n), rows)
                    k_out, v_out = (sample_k, sample_v) if first(n) else (prompt_k, prompt_v)
                    o_at = slice(0, SAMPLE) if first(n) else at
                    hold(pool, s["sqkv_in"], 16 * (n + 1))
                    for i, o in ((1, k_out), (2, v_out)):
                        pool.dma_start(o[0, 0, o_at].rearrange("t h d -> t (h d)"),
                                       sqkv[r, i * BANK:(i + 1) * BANK]).then_inc(s["kv_out"], 16)
                    if not first(n):
                        if not isinstance(n, int):
                            hold(pool, s["skT_out"], 16 * (n - 1))
                        hold(pool, s["skT_rdy"], 2 * n + 2)
                        pool.dma_start(skT_d[n - 1], skT[:, :]).then_inc(s["skT_out"], 16)
                    for what, rdy, masked in ((sp, "sp_rdy", "sp_masked"), (wT, "w_rdy", "w_masked")):
                        hold(pool, s[rdy], block_no(n) + 1)
                        v = h4(what[r, :], rows)
                        pool.affine_select(out=v, in_=v, compare_op=ALU.is_gt, fill=0.0, base=0,
                                           pattern=[[0, HEADS], [1, rows]], channel_multiplier=-1)\
                            .then_inc(s[masked], 1)
                    if first(n):
                        hold(pool, s["S_new"], 1)
                        pool.dma_start(sample_state[0, 0].rearrange("h k v -> k h v"), S[:])\
                            .then_inc(s["state_out"], 16)
                        hold(pool, s["state_out"], 16)
                        pool.memset(S[:], 0.0).then_inc(s["s_zero"], 1)

                    def past(m, j):
                        key_tile = nc.s_assert_within(n - 1 - j, 0, TILES - 2, 
                                                      skip_runtime_bounds_check_because="1 <= j < n")
                        hold(pool, s["suffix_rdy"], m)
                        pool.dma_start(KT[:, :], skT_d[bass.ds(key_tile, 1)].rearrange("a p c -> (a p) c"))\
                            .then_inc(s["k_in"], 16)
                        hold(pool, s["pv_done"], m)
                        pool.dma_start(V[:, :], proj[bass.ds(key_tile * P, P), SV:GT]).then_inc(s["v_in"], 16)
                    if not first(n):
                        past_blocks(pool, n, past)
                    hold(pool, s["x2_rdy"], n + 1)
                    pool.dma_start(x2_d[at, :], x[r, :]).then_inc(s["x2_out"], 16)
                    hold(pool, s["h2_rdy"], n + 1)
                    pool.dma_start(h2_d[at, :], big[r, :]).then_inc(s["h2_out"], 16)
                    hold(pool, s["h2T_rdy"], n + 1)
                    pool.dma_start(h2T_d[bass.ds(n * P, P)].rearrange("p (k c) -> p k c", c=P)[:, :, r],
                                   turnedT[:, :, r]).then_inc(s["h2T_out"], 16)
                tiles(pool, tile)
                pool.dma_start(prompt_state[0, 0].rearrange("h k v -> k h v"), S[:]).then_inc(s["state_out"], 16)
                hold(pool, s["state_out"], 32)
                hold(pool, s["kv_out"], 32 * NT)
                hold(pool, s["skT_out"], 16 * TILES)
                for o in ("x2_out", "h2_out", "h2T_out"):
                    hold(pool, s[o], 16 * NT)

            @block.scalar
            def _(act):
                def turned(n, rows, ready, done):
                    act.wait_ge(s[ready], n + 1)
                    if ready == "r_turned" and not first(n):
                        act.wait_ge(s["h2T_out"], 16 * n)
                    act.activation(turnedT[:, :, 0:rows], thirds(turn_ps[:, :])[:, :, 0:rows], ACT.Copy)\
                        .then_inc(s[done], 1)

                def attend(m, k_rows, q_rows):
                    kr = slice(0, k_rows)
                    a, z = h4(az[kr, :], q_rows), h4(z_ps[kr, :], q_rows)
                    act.wait_ge(s["z_rdy"], m + 1)
                    act.activation(a, z, ACT.Abs).then_inc(s["act"], 1)
                    act.wait_ge(s["act"], m * 2 + 1)
                    act.activation(a, a, ACT.Exp, scale=-1.0).then_inc(s["act"], 1)
                    act.wait_ge(s["act"], m * 2 + 2)
                    act.activation(a, a, ACT.Ln, bias=C["one"][kr]).then_inc(s["ln_rdy"], 1)
                    act.wait_ge(s["suffix_rdy"], m + 1)
                    act.activation(h4(wT[kr, :], q_rows), h4(suffix_ps[kr, :], q_rows), ACT.Exp)\
                        .then_inc(s["w_rdy"], 1)

                def tile(n, rows):
                    r = slice(0, rows)
                    if first(n):
                        act.wait_ge(s["cache_turned"], 1)
                        act.activation(KT[:, :], z_ps, ACT.Copy).then_inc(s["cacheT_rdy"], 1)
                    act.wait_ge(s["qk_turned"], n + 1)
                    act.activation(h4(qT[:, :], rows), h4(qT_ps, rows), ACT.Copy).then_inc(s["qkT_rdy"], 1)
                    act.activation(h4(kT[:, :], rows), h4(kT_ps, rows), ACT.Copy).then_inc(s["qkT_rdy"], 1)
                    act.wait_ge(s["o_rdy"], n + 1)
                    for h in range(HEADS):
                        act.activation(ret[r, h * DV:(h + 1) * DV], ret_ps[r, h * DV:(h + 1) * DV], ACT.Copy,
                                       scale=C["inter"][r, h:h + 1]).then_inc(s["ret_rdy"], 1)
                    act.wait_ge(s["rg_in"], 16 * (n + 1))
                    act.activation(rb[r, :], rg[r, :], ACT.Sigmoid).then_inc(s["sig_rdy"], 1)
                    act.wait_ge(s["gates_in"], 16 * (n + 1))
                    act.activation(gates[r, :], gates[r, :], ACT.Sigmoid).then_inc(s["sig_rdy"], 1)
                    act.wait_ge(s["var_rdy"], n + 1)
                    act.activation(gst[r, 0, :], mv[r, :, 1], ACT.Sqrt, bias=C["eps"][r]).then_inc(s["root_rdy"], 1)
                    attend(block_no(n), rows, rows)
                    past_blocks(act, n, lambda m, j: attend(m, P, rows))
                    turned(n, rows, "r_turned", "rT_rdy")
                    turned(n, rows, "m_turned", "mT_rdy")
                    act.wait_ge(s["x2_rdy"], n + 1)
                    act.activation(rb[r, :], x[r, :], ACT.Square, accum_out=n2[r, 0:1]).then_inc(s["sq2_rdy"], 1)
                    act.wait_ge(s["sq2_rdy"], 2 * n + 1)
                    act.activation(n2[r, 1:2], n2[r, 0:1], ACT.Sqrt, scale=1.0 / D, bias=C["eps"][r])\
                        .then_inc(s["sq2_rdy"], 1)
                    turned(n, rows, "h2_turned", "h2T_rdy")
                tiles(act, tile)

            @block.vector
            def _(dve):
                dve.wait_ge(s["weights_in"], 80)
                STEPS = 4 + 3 + 7 + NEWTON_STEPS + 4 + 1 + 1 + 2 + NEWTON_STEPS

                def attend(n, m, own, k_rows, q_rows, sum_rows):
                    kr = slice(0, k_rows)
                    dve.wait_ge(s["ln_rdy"], m + 1)
                    if not first(m):
                        dve.wait_ge(s["suffix_rdy"], m)
                        dve.wait_ge(s["spsum_rdy"], m)
                    dve.scalar_tensor_tensor(out=h4(sp[kr, :], q_rows), in0=h4(z_ps[kr, :], q_rows), scalar=0.0,
                                             in1=h4(az[kr, :], q_rows), op0=ALU.max, op1=ALU.add)\
                        .then_inc(s["sp_rdy"], 1)
                    add, to = h4(sp[0:sum_rows, :], q_rows), h4(spsum[0:sum_rows, :], q_rows)
                    if own:
                        dve.wait_ge(s["sp_masked"], n + 1)
                        dve.tensor_copy(to, add).then_inc(s["spsum_rdy"], 1)
                    else:
                        dve.wait_ge(s["suffix_rdy"], m + 1)
                        dve.wait_ge(s["spsum_rdy"], m)
                        dve.wait_ge(s["sp_rdy"], m + 1)
                        dve.tensor_tensor(to, to, add, ALU.add).then_inc(s["spsum_rdy"], 1)

                def tile(n, rows):
                    r = slice(0, rows)
                    k_dec = C["k_dec_sample"] if first(n) else C["k_dec"]
                    gamma = gamma_to(rows)
                    chain = Chain(dve, s["dve"], n * STEPS)
                    dve.wait_ge(s["qk_in"], 32 * (n + 1))
                    if not first(n):
                        dve.wait_ge(s["qk_turned"], n)
                        dve.wait_ge(s["kd_rdy"], n)
                    half = lambda ap, i: ap[r, :].rearrange("p (h two d) -> p two h d", two=2, d=DK // 2)[:, i]
                    cos = cs[r, 0:64].rearrange("p (a d) -> p a d", a=1)
                    sin = cs[r, 64:128].rearrange("p (a d) -> p a d", a=1)
                    chain.then(dve.tensor_tensor(ra[r, :].rearrange("p (h d) -> p h d", d=64),
                                                 qk[r, :].rearrange("p (h d) -> p h d", d=64),
                                                 cos.to_broadcast([rows, 16, 64]), ALU.mult))
                    chain.then(dve.tensor_tensor(half(rot, 0), half(qk, 1), sin.to_broadcast([rows, 8, 64]), ALU.mult))
                    chain.then(dve.tensor_tensor(half(rot, 1), half(qk, 0), sin.to_broadcast([rows, 8, 64]), ALU.mult))
                    chain.wait()
                    chain.then(dve.tensor_tensor(half(rot, 0), half(ra, 0), half(rot, 0), ALU.subtract))
                    dve.tensor_tensor(half(rot, 1), half(ra, 1), half(rot, 1), ALU.add).then_inc(s["qk_rot"], 1)
                    dve.wait_ge(s["qk_rot"], n + 1)
                    chain.wait()
                    if not first(n):
                        dve.wait_ge(s["state_mm"], n)
                    dve.tensor_tensor(kd[r, :], rot[r, BANK:], k_dec[r], ALU.mult).then_inc(s["kd_rdy"], 1)
                    dve.wait_ge(s["sq_turned"], n + 1)
                    dve.tensor_scalar(h4(sqT[:, :], rows), h4(sqT_ps, rows), SCORE_SCALE, None, ALU.mult)\
                        .then_inc(s["skT_rdy"], 1)
                    if not isinstance(n, int):
                        dve.wait_ge(s["skT_out"], 16 * (n - 1))
                    dve.tensor_copy(h4(skT[:, :], rows), h4(skT_ps, rows)).then_inc(s["skT_rdy"], 1)
                    dve.wait_ge(s["scores_rdy"], n + 1)
                    dve.tensor_tensor(h4(pT[r, :], rows), h4(scores_ps[r, :], rows), h4(C["decay"][r], rows),
                                      ALU.mult).then_inc(s["pT_rdy"], 1)
                    if first(n):
                        dve.wait_ge(s["s_in"], 16)
                    elif isinstance(n, int):
                        dve.wait_ge(s["s_zero"], 1)
                    dve.wait_ge(s["o_rdy"], n + 1)
                    for h in range(HEADS):
                        chain.then(dve.scalar_tensor_tensor(out=S[:, h, :], in0=S[:, h, :], scalar=gamma[h],
                                                            in1=state_ps[:, h * DV:(h + 1) * DV], op0=ALU.mult,
                                                            op1=ALU.add)) if h < HEADS - 1 else \
                            dve.scalar_tensor_tensor(out=S[:, h, :], in0=S[:, h, :], scalar=gamma[h],
                                                     in1=state_ps[:, h * DV:(h + 1) * DV], op0=ALU.mult,
                                                     op1=ALU.add).then_inc(s["S_new"], 1)
                    chain.wait()
                    dve.wait_ge(s["S_new"], n + 1)
                    dve.wait_ge(s["ret_rdy"], HEADS * (n + 1))
                    for h in range(HEADS):
                        chain.then(dve.bn_stats(stats[r, h, :], ret[r, h * DV:(h + 1) * DV]))
                    hold(dve, s["dve"], chain.start + chain.n)
                    for h in range(HEADS):
                        ins = dve.bn_aggr(mv[r, h, :], stats[r, h, :])
                        if h < HEADS - 1:
                            chain.then(ins)
                    ins.then_inc(s["var_rdy"], 1)
                    chain.wait()
                    dve.wait_ge(s["var_rdy"], n + 1)
                    dve.wait_ge(s["root_rdy"], n + 1)
                    rstd_newton(dve, chain, mv[r, :, 1], gst[r, 0, :], gst[r, 1, :], gst[r, 2, :], 1.0)
                    for h in range(HEADS):
                        chain.then(dve.tensor_scalar(ret[r, h * DV:(h + 1) * DV], ret[r, h * DV:(h + 1) * DV],
                                                     mv[r, h, 0:1], gst[r, 1, h:h + 1], ALU.subtract, ALU.mult))
                    dve.wait_ge(s["sig_rdy"], 2 * n + 2)
                    chain.then(dve.tensor_tensor(rb[r, :], rb[r, :], rg[r, :], ALU.mult))
                    chain.wait()
                    chain.then(dve.tensor_tensor(ret[r, :], ret[r, :], gnw[r, :], ALU.mult))
                    chain.wait()
                    dve.tensor_tensor(ret[r, :], ret[r, :], rb[r, :], ALU.mult).then_inc(s["r_rdy"], 1)
                    attend(n, block_no(n), True, rows, rows, rows)
                    past_blocks(dve, n, lambda m, j: attend(n, m, False, P, rows, rows))
                    dve.wait_ge(s["pv_done"], block_no(n + 1) if not first(n) else 2)
                    dve.tensor_copy(h4(sboT[:, :], rows), h4(sboT_ps, rows)).then_inc(s["sbo_rdy"], 1)
                    dve.wait_ge(s["retb_rdy"], n + 1)
                    if not first(n):
                        dve.wait_ge(s["h2_out"], 16 * n)
                        dve.wait_ge(s["h2_turned"], n)
                    chain.then(dve.tensor_tensor(big[r, :], retb_ps[r, :], gates[r, 0:D], ALU.mult))
                    dve.wait_ge(s["sbb_rdy"], n + 1)
                    chain.then(dve.tensor_tensor(ra[r, :], sbb_ps[r, :], gates[r, D:], ALU.mult))
                    chain.wait()
                    dve.tensor_tensor(big[r, :], big[r, :], ra[r, :], ALU.add).then_inc(s["mixed_rdy"], 1)
                    dve.wait_ge(s["x_in"], 16 * (n + 1))
                    dve.wait_ge(s["res_rdy"], n + 1)
                    dve.tensor_tensor(x[r, :], x[r, :], res_ps[r, :], ALU.add).then_inc(s["x2_rdy"], 1)
                    dve.wait_ge(s["sq2_rdy"], 2 * n + 2)
                    rstd_newton(dve, chain, n2[r, 0:1], n2[r, 1:2], n2[r, 2:3], n2[r, 3:4], 1.0 / D)
                    dve.scalar_tensor_tensor(out=big[r, :], in0=x[r, :], scalar=n2[r, 2:3], in1=g2[r, :],
                                             op0=ALU.mult, op1=ALU.mult).then_inc(s["h2_rdy"], 1)
                    assert chain.n == STEPS, chain.n
                tiles(dve, tile)

            @block.tensor
            def _(pe):
                pe.wait_ge(s["weights_in"], 80)

                def attend(n, m, j, KTt, Vt, k_rows, q_rows, sum_rows):
                    kr = slice(0, k_rows)
                    own = isinstance(j, int) and j == 0

                    def scores(ps):
                        for h in range(HEADS):
                            last = pe.matmul(h4(ps[kr, :], q_rows)[:, h], KTt[:, h * P:h * P + k_rows],
                                             h4(sqT[:, :], q_rows)[:, h], start=(h == 0), stop=True,
                                             skip_group_check=True)
                        return last
                    if own:
                        pe.wait_ge(s["skT_rdy"], 2 * n + 2)
                    elif first(n):
                        pe.wait_ge(s["cacheT_rdy"], 1)
                    else:
                        pe.wait_ge(s["k_in"], 16 * past_no(n, j))
                    scores(z_ps).then_inc(s["z_rdy"], 1)
                    scores(suffix_ps)
                    if own:
                        pe.wait_ge(s["sp_masked"], n + 1)
                    else:
                        pe.wait_ge(s["sp_rdy"], m + 1)
                    last = pe.matmul(h4(suffix_ps[kr, :], q_rows), C["neg_tri"][kr, kr], h4(sp[kr, :], q_rows),
                                     start=False, stop=True, skip_group_check=True)
                    if not own:
                        pe.wait_ge(s["spsum_rdy"], m)
                        last = pe.matmul(h4(suffix_ps[kr, :], q_rows), C["neg_ones"][0:sum_rows, kr],
                                         h4(spsum[0:sum_rows, :], q_rows), start=False, stop=True,
                                         skip_group_check=True)
                    last.then_inc(s["suffix_rdy"], 1)
                    if own:
                        pe.wait_ge(s["w_masked"], n + 1)
                        pe.wait_ge(s["sqkv_in"], 16 * (n + 1))
                    else:
                        pe.wait_ge(s["w_rdy"], m + 1)
                        pe.wait_ge(s["v_in"], 16 if first(n) else 16 * (past_no(n, j) + 1))
                    for h in range(HEADS):
                        last = pe.matmul(h4(sboT_ps, q_rows)[:, h], Vt[kr, h * P:(h + 1) * P],
                                         h4(wT[kr, :], q_rows)[:, h], start=(own and h == 0), stop=True,
                                         skip_group_check=True)
                    last.then_inc(s["pv_done"], 1)

                def turn(dst, src, rows, blocks):
                    for k in range(blocks):
                        last = pe.transpose(dst[:, k * P:k * P + rows], src[0:rows, k * P:(k + 1) * P],
                                            C["ident"][0:rows, 0:rows])
                    return last

                def wide(dst, lhsT, rhs, blocks, rows):
                    for half in range(2):
                        c = slice(half * BANK, (half + 1) * BANK)
                        for k in range(blocks):
                            last = pe.matmul(dst[0:rows, c], lhsT(k), rhs[:, k, c], start=(k == 0),
                                             stop=(k == blocks - 1))
                    return last

                def tile(n, rows):
                    r = slice(0, rows)
                    pe.wait_ge(s["qk_rot"], n + 1)
                    pe.wait_ge(s["kd_rdy"], n + 1)
                    if not first(n):
                        pe.wait_ge(s["mixed_rdy"], n)
                    turn(pair[0], rot, rows, 8).then_inc(s["qk_turned"], 1)
                    if first(n):
                        pe.wait_ge(s["cache_in"], 16)
                        turn(z_ps, az, P, 4).then_inc(s["cache_turned"], 1)
                        pe.wait_ge(s["cacheT_rdy"], 1)
                    else:
                        pe.wait_ge(s["x2_rdy"], n)
                    pe.wait_ge(s["sqkv_in"], 16 * (n + 1))
                    turn(pair[1], sqkv, rows, 8).then_inc(s["sq_turned"], 1)
                    pe.wait_ge(s["qkT_rdy"], 2 * n + 2)
                    for h in range(HEADS):
                        last = pe.matmul(h4(scores_ps[r, :], rows)[:, h], kT[:, h * P:h * P + rows],
                                         qT[:, h * P:h * P + rows], start=(h == 0), stop=True, skip_group_check=True)
                    last.then_inc(s["scores_rdy"], 1)
                    pe.wait_ge(s["rv_in"], 16 * (n + 1))
                    if not first(n):
                        pe.wait_ge(s["h2T_rdy"], n)
                    for h in range(HEADS):
                        v = slice(h * DV, (h + 1) * DV)
                        last = pe.matmul(state_ps[:, v], kd[r, h * P:(h + 1) * P], rv[r, v], start=(h % 2 == 0),
                                         stop=True, skip_group_check=True)
                    last.then_inc(s["state_mm"], 1)
                    pe.wait_ge(s["pT_rdy"], n + 1)
                    if first(n):
                        pe.wait_ge(s["s_in"], 16)
                    elif isinstance(n, int):
                        pe.wait_ge(s["s_zero"], 1)
                    else:
                        pe.wait_ge(s["S_new"], n)
                    for h in range(HEADS):
                        v = slice(h * DV, (h + 1) * DV)
                        pe.matmul(ret_ps[r, v], pT[r, h * P:h * P + rows], rv[r, v], start=(h % 2 == 0), stop=True,
                                  skip_group_check=True)
                        last = pe.matmul(ret_ps[r, v], qT[:, h * P:h * P + rows], S[:, h, :], start=False, stop=True,
                                         skip_group_check=True)
                    last.then_inc(s["o_rdy"], 1)
                    attend(n, block_no(n), 0, skT, sqkv[:, 2 * BANK:], rows, rows, rows)
                    past_blocks(pe, n, lambda m, j: attend(n, m, j, KT, V, P, rows, rows))
                    pe.wait_ge(s["r_rdy"], n + 1)
                    pe.wait_ge(s["S_new"], n + 1)
                    turn(turn_ps, ret, rows, 8).then_inc(s["r_turned"], 1)
                    pe.wait_ge(s["rT_rdy"], n + 1)
                    pe.wait_ge(s["ret_rdy"], HEADS * (n + 1))
                    wide(retb_ps, lambda k: turnedT[:, k, r], wret, KD, rows).then_inc(s["retb_rdy"], 1)
                    pe.wait_ge(s["sbo_rdy"], n + 1)
                    wide(sbb_ps, lambda k: sboT[:, k * P:k * P + rows], wsb, HEADS, rows).then_inc(s["sbb_rdy"], 1)
                    pe.wait_ge(s["mixed_rdy"], n + 1)
                    turn(turn_ps, big, rows, 8).then_inc(s["m_turned"], 1)
                    pe.wait_ge(s["mT_rdy"], n + 1)
                    wide(res_ps, lambda k: turnedT[:, k, r], wout, KD, rows).then_inc(s["res_rdy"], 1)
                    pe.wait_ge(s["h2_rdy"], n + 1)
                    turn(turn_ps, big, rows, 8).then_inc(s["h2_turned"], 1)
                tiles(pe, tile)


def tiles(eng, tile):
    tile(0, SAMPLE)
    tile(1, P)
    with eng.Fori(2, TILES + 1) as n:
        tile(n, P)


def route(nc, sem, hold, pair, C, w_pq, pk_keys, h2T_d, eidx, gate):
    NT = TILES + 1
    STEPS = 5 * SIDES + 3 + 5 * PHEADS + 11 + 1 + 2
    with ExitStack() as ctx:
        sb = lambda n, s, d=F32: ctx.enter_context(nc.sbuf_tensor(n, s, d))
        wpq = sb("wpq", [P, KD, PQ_W])
        keys = sb("keys", [P, SIDES, P])
        pkT = sb("pkT", [P, SIDES, P])
        hT = sb("r_hT", [P, KD, P])
        qT = sb("r_qT", [P, SIDES, P])
        sc = sb("sc", [P, SIDES, KEYS])
        sc2 = sb("sc2", [P, SIDES, KEYS])
        top = sb("top", [P, SIDES, TOPK])
        topi = sb("topi", [P, SIDES, TOPK], U32)
        topf = sb("topf", [P, SIDES, TOPK])
        best = sb("best", [P, PHEADS, TOPK])
        besti = sb("besti", [P, PHEADS, TOPK], U32)
        parti = sb("parti", [P, 2, PHEADS, TOPK], U32)
        part = sb("part", [P, 2, PHEADS, TOPK])
        found = sb("found", [P, 2, PHEADS, TOPK])
        sums = sb("sums", [P, PHEADS])
        cand = sb("cand", [P, PHEADS, TOPK * TOPK])
        cand2 = sb("cand2", [P, PHEADS, TOPK * TOPK])
        grid = lambda ap: ap.rearrange("p h (a b) -> p h a b", a=TOPK)

        names = ("w_in keys_in h_in keys_turned keysT_rdy q_rdy qT_rdy s_rdy sc_rdy dve best_rdy exp_rdy gates_rdy").split()
        s = {n: sem("c_" + n) for n in names}

        with nc.Block() as block:
            @block.sync
            def _(sy):
                sy.dma_start(keys[:].rearrange("k (h two) c -> k two h c", two=2)[:, 0],
                             pk_keys[0, 0].rearrange("h k c -> k h c")).then_inc(s["keys_in"], 16)
                sy.dma_start(keys[:].rearrange("k (h two) c -> k two h c", two=2)[:, 1],
                             pk_keys[0, 1].rearrange("h k c -> k h c")).then_inc(s["keys_in"], 16)
                sy.dma_start(wpq[:], w_pq[0].rearrange("(k p) n -> p k n", p=P)).then_inc(s["w_in"], 16)

                def tile(n, rows):
                    if not first(n):
                        hold(sy, s["q_rdy"], n)
                    sy.dma_start(hT[:, :, 0:rows],
                                 h2T_d[bass.ds(n * P, P)].rearrange("p (k c) -> p k c", c=P)[:, :, 0:rows])\
                        .then_inc(s["h_in"], 16)
                tiles(sy, tile)

            @block.scalar
            def _(act):
                for half in range(2):
                    act.wait_ge(s["keys_turned"], half + 1)
                    act.activation(pkT[:, half * 8:half * 8 + 8, :], thirds(pair[half][:, :]), ACT.Copy)\
                        .then_inc(s["keysT_rdy"], 1)

                def tile(n, rows):
                    r = slice(0, rows)
                    act.wait_ge(s["q_rdy"], n + 1)
                    for half in range(2):
                        act.activation(qT[:, half * 8:half * 8 + 8, r], thirds(pair[half][:, :])[:, :, r], ACT.Copy)\
                            .then_inc(s["qT_rdy"], 1)
                    act.wait_ge(s["s_rdy"], n + 1)
                    if not first(n):
                        act.wait_ge(s["best_rdy"], n)
                    for half in range(2):
                        act.activation(sc[r, half * 8:half * 8 + 8, :], thirds(pair[2 + half][r, :]), ACT.Copy)\
                            .then_inc(s["sc_rdy"], 1)
                    act.wait_ge(s["best_rdy"], n + 1)
                    act.activation(best[r], best[r], ACT.Exp).then_inc(s["exp_rdy"], 1)
                tiles(act, tile)

            @block.vector
            def _(dve):
                def top16(chain, values, spare, out, out_i, count, r):
                    for i in range(count):
                        chain.then(dve.max(out[r, i, 0:8], values[r, i]))
                    chain.hold(hold)
                    for i in range(count):
                        chain.then(dve.max_index(out_i[r, i, 0:8], out[r, i, 0:8], values[r, i]))
                    for i in range(count):
                        chain.then(dve.match_replace(spare[r, i], out[r, i, 0:8], values[r, i], LOWEST))
                    chain.hold(hold)
                    for i in range(count):
                        chain.then(dve.max(out[r, i, 8:16], spare[r, i]))
                    chain.hold(hold)
                    for i in range(count):
                        chain.then(dve.max_index(out_i[r, i, 8:16], out[r, i, 8:16], spare[r, i]))
                    chain.hold(hold)

                def tile(n, rows):
                    r = slice(0, rows)
                    chain = Chain(dve, s["dve"], n * STEPS)
                    hold(dve, s["sc_rdy"], 2 * n + 2)
                    if not first(n):
                        hold(dve, s["gates_rdy"], n)
                    top16(chain, sc, sc2, top, topi, SIDES, r)
                    side = lambda ap, i: ap[r].rearrange("p (h two) k -> p two h k", two=2)[:, i]
                    full = [rows, PHEADS, TOPK, TOPK]
                    over_b = lambda ap: ap.rearrange("p h (k a) -> p h k a", a=1).to_broadcast(full)
                    over_a = lambda ap: ap.rearrange("p h (a k) -> p h a k", a=1).to_broadcast(full)
                    chain.then(dve.tensor_tensor(grid(cand)[r], over_b(side(top, 0)), over_a(side(top, 1)), ALU.add))
                    chain.then(dve.tensor_copy(topf[r], topi[r]))
                    chain.hold(hold)
                    top16(chain, cand, cand2, best, besti, PHEADS, r)
                    peak = best[r, :, 0:1].to_broadcast([rows, PHEADS, TOPK])
                    chain.then(dve.tensor_copy(part[r, 0, :, :], peak))
                    chain.wait()
                    dve.tensor_tensor(best[r], best[r], part[r, 0], ALU.subtract).then_inc(s["best_rdy"], 1)
                    chain.then(dve.tensor_scalar(parti[r, 0], besti[r], 4, None, ALU.logical_shift_right))
                    chain.then(dve.tensor_scalar(parti[r, 1], besti[r], 15, None, ALU.bitwise_and))
                    chain.wait()
                    dve.wait_ge(s["best_rdy"], n + 1)
                    chain.then(dve.tensor_copy(part[r], parti[r]))
                    chain.wait()
                    iota = C["iota16"][r].rearrange("p (a b k) -> p a b k", a=1, b=1).to_broadcast(full)
                    for i in range(2):
                        hot = grid((cand, cand2)[i])[r]
                        chain.then(dve.tensor_tensor(hot, over_b(part[r, i]), iota, ALU.is_equal))
                    chain.wait()
                    for i in range(2):
                        hot = grid((cand, cand2)[i])[r]
                        chain.then(dve.tensor_tensor(hot, hot, over_a(side(topf, i)), ALU.mult))
                    chain.wait()
                    for i in range(2):
                        hot = grid((cand, cand2)[i])[r]
                        chain.then(dve.tensor_reduce(found[r, i], hot, AX_X, ALU.add))
                    chain.wait()
                    chain.then(dve.scalar_tensor_tensor(out=part[r, 0], in0=found[r, 0], scalar=float(KEYS),
                                                        in1=found[r, 1], op0=ALU.mult, op1=ALU.add))
                    chain.wait()
                    slot = bass.ds(n * SLOTS, SLOTS)
                    flat = lambda ap: ap.rearrange("p h k -> p (h k)")
                    chain.then(dve.tensor_copy(eidx[r, slot], flat(part[r, 0])))
                    dve.wait_ge(s["exp_rdy"], n + 1)
                    chain.then(dve.tensor_reduce(sums[r, :], best[r], AX_X, ALU.add))
                    chain.wait()
                    chain.then(dve.reciprocal(sums[r, :], sums[r, :]))
                    chain.wait()
                    chain.then(dve.tensor_copy(part[r, 1], sums[r, :].rearrange("p (h a) -> p h a", a=1)
                                               .to_broadcast([rows, PHEADS, TOPK])))
                    chain.wait()
                    dve.tensor_tensor(gate[r, slot], flat(best[r]), flat(part[r, 1]), ALU.mult)\
                        .then_inc(s["gates_rdy"], 1)
                    assert chain.n == STEPS, chain.n
                tiles(dve, tile)

            @block.tensor
            def _(pe):
                pe.wait_ge(s["keys_in"], 32)
                for half in range(2):
                    for i in range(8):
                        last = pe.transpose(pair[half][:, i * P:(i + 1) * P], keys[:, half * 8 + i, :], C["ident"])
                    last.then_inc(s["keys_turned"], 1)
                pe.wait_ge(s["w_in"], 16)
                pe.wait_ge(s["keysT_rdy"], 2)

                def tile(n, rows):
                    r = slice(0, rows)
                    pe.wait_ge(s["h_in"], 16 * (n + 1))
                    if not first(n):
                        pe.wait_ge(s["qT_rdy"], 2 * n)
                    for j in range(SIDES):
                        for k in range(KD):
                            last = pe.matmul(pair[j // 8][:, (j % 8) * P:(j % 8) * P + rows],
                                             wpq[:, k, j * P:(j + 1) * P], hT[:, k, r], start=(k == 0),
                                             stop=(k == KD - 1))
                    last.then_inc(s["q_rdy"], 1)
                    pe.wait_ge(s["qT_rdy"], 2 * n + 2)
                    if not first(n):
                        pe.wait_ge(s["sc_rdy"], 2 * n)
                    for j in range(SIDES):
                        last = pe.matmul(pair[2 + j // 8][r, (j % 8) * P:(j % 8 + 1) * P], qT[:, j, r], pkT[:, j, :],
                                         start=True, stop=True)
                    last.then_inc(s["s_rdy"], 1)
                tiles(pe, tile)


def experts(nc, sem, hold, pair, C, peer_u, peer_v, norm_f_w, x2_d, h2_d, eidx, gate, y_prompt, y_sample):
    NT = TILES + 1
    CHAIN = 6
    GELU_CUBE, GELU_ROOT = 0.044715, float(np.sqrt(2.0 / np.pi))
    acc = pair[0]
    with ExitStack() as ctx:
        sb = lambda n, s, d=F32: ctx.enter_context(nc.sbuf_tensor(n, s, d))
        ur = sb("ur", [P, RING, D])
        vr = sb("vr", [P, RING, D])
        idx_u = sb("idx_u", [P, 2, TOPK], U32)
        idx_v = sb("idx_v", [P, 2, TOPK], U32)
        h2 = sb("h2", [P, D])
        x2 = sb("x2t", [P, D])
        x3 = sb("x3", [P, D])
        y = sb("y", [P, D])
        gf = sb("gf", [P, D])
        dots = sb("dots", [P, 2, TOPK])
        ge = sb("ge", [P, 2, TOPK])
        coef = sb("coef", [P, 2, TOPK])
        diag = sb("diag", [P, TOPK, P])
        n3 = sb("n3", [P, 4])

        names = ("gf_in h2_in x2_in u_staged v_staged u_used v_used dve norm arg_rdy exp_rdy coef_rdy diag_rdy seeded "
                 "x3_rdy sq3_rdy y_rdy y_out").split()
        s = {n: sem("d_" + n) for n in names}
        u_in = [sem(f"d_u_in{i}") for i in range(RING)]
        v_in = [sem(f"d_v_in{i}") for i in range(RING)]

        def steps(eng, step):
            def tile(n, rows):
                before = SAMPLE if isinstance(n, int) else P
                step(n, 0, 0, rows, before)
                step(n, 1, 1, rows, rows)
                with eng.Fori(1, PHEADS // 2) as j:
                    step(n, j * 2, 0, rows, rows)
                    step(n, j * 2 + 1, 1, rows, rows)
            tiles(eng, tile)

        def at_start(h):
            return isinstance(h, int) and h == 0

        def filled(g, k):
            return 16 * (g * (TOPK // RING) + k // RING + 1)

        with nc.Block() as block:
            @block.sync
            def _(sy):
                sy.dma_start(gf[:, :], broadcast_rows(norm_f_w, P)).then_inc(s["gf_in"], 16)

                def store(n, rows, out):
                    hold(sy, s["y_rdy"], n + 1)
                    sy.dma_start(out, y[0:rows, :]).then_inc(s["y_out"], 16)

                def tile(n, rows):
                    r = slice(0, rows)
                    at = bass.ds(token_col(n), rows)
                    if not first(n):
                        hold(sy, s["u_used"], n * SLOTS)
                    sy.dma_start(h2[r, :], h2_d[at, :]).then_inc(s["h2_in"], 16)
                    if not first(n):
                        hold(sy, s["seeded"], n)
                    sy.dma_start(x2[r, :], x2_d[at, :]).then_inc(s["x2_in"], 16)
                    if not first(n):
                        if isinstance(n, int):
                            store(0, SAMPLE, y_sample[0])
                        else:
                            store(n - 1, P, y_prompt[0, bass.ds((n - 2) * P, P), :])
                tiles(sy, tile)
                store(TILES, P, y_prompt[0, SEQ - P:SEQ, :])
                sy.wait_ge(s["y_out"], 16 * NT)

            @block.gpsimd
            def _(pool):
                def gather(ring, table, idx, k, rows, arrived):
                    pool.indirect_dma_start(ring[0:rows, k % RING, :], None, table,
                                            bass.IndirectOffsetOnAxis(ap=idx[0:rows, k:k + 1], axis=0))\
                        .then_inc(arrived[k % RING], 16)

                def gather_v(g, parity, k, rows):
                    if not (first(g) and k < RING):
                        hold(pool, s["v_used"], g * TOPK + k + 1 - RING)
                    gather(vr, peer_v[0], idx_v[:, parity], k, rows, v_in)

                def stage_v(g, parity, rows):
                    if not isinstance(g, int):
                        hold(pool, s["v_used"], (g - 1) * TOPK)
                    pool.tensor_copy(idx_v[0:rows, parity], eidx[0:rows, bass.ds(g * TOPK, TOPK)])\
                        .then_inc(s["v_staged"], 1)
                    hold(pool, s["v_staged"], g + 1)

                def step(n, h, parity, rows, before):
                    g = n * PHEADS + h
                    if not isinstance(g, int) or g > 1:
                        hold(pool, s["u_used"], (g - 1) * TOPK)
                    pool.tensor_copy(idx_u[0:rows, parity], eidx[0:rows, bass.ds(g * TOPK, TOPK)])\
                        .then_inc(s["u_staged"], 1)
                    hold(pool, s["u_staged"], g + 1)
                    if not first(g):
                        stage_v(g - 1, 1 - parity, before)
                    for k in range(TOPK):
                        if not (first(g) and k < RING):
                            hold(pool, s["u_used"], g * TOPK + k + 1 - RING)
                        gather(ur, peer_u[0], idx_u[:, parity], k, rows, u_in)
                        if not first(g):
                            gather_v(g - 1, 1 - parity, k, before)
                steps(pool, step)
                last = NT * PHEADS - 1
                pool.wait_ge(s["v_used"], (last - 1) * TOPK)
                pool.tensor_copy(idx_v[:, 1], eidx[:, last * TOPK:]).then_inc(s["v_staged"], 1)
                pool.wait_ge(s["v_staged"], last + 1)
                for k in range(TOPK):
                    gather_v(last, 1, k, P)

            @block.scalar
            def _(act):
                def finish(n, rows):
                    r = slice(0, rows)
                    act.wait_ge(s["v_used"], (n + 1) * SLOTS)
                    if not first(n):
                        act.wait_ge(s["y_rdy"], n)
                    act.activation(x3[r, :], acc[r, :], ACT.Copy).then_inc(s["x3_rdy"], 1)
                    act.wait_ge(s["x3_rdy"], n + 1)
                    if not first(n):
                        act.wait_ge(s["y_out"], 16 * n)
                    act.activation(y[r, :], x3[r, :], ACT.Square, accum_out=n3[r, 0:1]).then_inc(s["sq3_rdy"], 1)
                    act.wait_ge(s["sq3_rdy"], 2 * n + 1)
                    act.activation(n3[r, 1:2], n3[r, 0:1], ACT.Sqrt, scale=1.0 / D, bias=C["eps"][r])\
                        .then_inc(s["sq3_rdy"], 1)

                def step(n, h, parity, rows, before):
                    r = slice(0, rows)
                    g = n * PHEADS + h
                    act.wait_ge(s["arg_rdy"], g + 1)
                    act.activation(ge[r, parity], ge[r, parity], ACT.Exp, scale=-2.0 * GELU_ROOT)\
                        .then_inc(s["exp_rdy"], 1)
                    if at_start(h) and not first(n):
                        finish(n - 1, before)
                    act.wait_ge(s["coef_rdy"], g + 1)
                    for k in range(TOPK):
                        if not first(g):
                            act.wait_ge(s["v_used"], (g - 1) * TOPK + k + 1)
                        act.activation(diag[r, k, :], C["ident"][r, :], ACT.Copy, scale=coef[r, parity, k:k + 1])\
                            .then_inc(s["diag_rdy"], 1)
                steps(act, step)
                finish(TILES, P)

            @block.vector
            def _(dve):
                dve.wait_ge(s["gf_in"], 16)

                def finish(n, rows):
                    r = slice(0, rows)
                    chain = Chain(dve, s["norm"], n * NEWTON_STEPS)
                    dve.wait_ge(s["sq3_rdy"], 2 * n + 2)
                    rstd_newton(dve, chain, n3[r, 0:1], n3[r, 1:2], n3[r, 2:3], n3[r, 3:4], 1.0 / D)
                    dve.scalar_tensor_tensor(out=y[r, :], in0=x3[r, :], scalar=n3[r, 2:3], in1=gf[r, :],
                                             op0=ALU.mult, op1=ALU.mult).then_inc(s["y_rdy"], 1)

                def step(n, h, parity, rows, before):
                    r = slice(0, rows)
                    g = n * PHEADS + h
                    if at_start(h):
                        hold(dve, s["h2_in"], 16 * (n + 1))
                    if not isinstance(g, int) or g > 1:
                        hold(dve, s["coef_rdy"], g - 1)
                    for k in range(TOPK):
                        dve.wait_ge(u_in[k % RING], filled(g, k))
                        dve.tensor_tensor_reduce(ur[r, k % RING, :], ur[r, k % RING, :], h2[r, :], 1.0, 0.0,
                                                 ALU.mult, ALU.add, dots[r, parity, k:k + 1])\
                            .then_inc(s["u_used"], 1)
                    chain = Chain(dve, s["dve"], g * CHAIN)
                    d, t = dots[r, parity], ge[r, parity]
                    dve.wait_ge(s["u_used"], (g + 1) * TOPK)
                    chain.then(dve.tensor_tensor(t, d, d, ALU.mult))
                    chain.wait()
                    chain.then(dve.tensor_scalar(t, t, GELU_CUBE, 1.0, ALU.mult, ALU.add))
                    chain.wait()
                    chain.then(dve.tensor_tensor(t, t, d, ALU.mult))
                    chain.wait()
                    dve.tensor_scalar(t, t, -50.0, None, ALU.max).then_inc(s["arg_rdy"], 1)
                    dve.wait_ge(s["exp_rdy"], g + 1)
                    chain.then(dve.tensor_scalar(t, t, 1.0, None, ALU.add))
                    chain.wait()
                    chain.then(dve.reciprocal(t, t))
                    chain.wait()
                    chain.then(dve.tensor_tensor(t, t, d, ALU.mult))
                    chain.wait()
                    if not isinstance(g, int) or g > 1:
                        dve.wait_ge(s["diag_rdy"], (g - 1) * TOPK)
                    dve.tensor_tensor(coef[r, parity], t, gate[r, bass.ds(g * TOPK, TOPK)], ALU.mult)\
                        .then_inc(s["coef_rdy"], 1)
                    if at_start(h) and not first(n):
                        finish(n - 1, before)
                steps(dve, step)
                finish(TILES, P)

            @block.tensor
            def _(pe):
                def weigh(g, rows):
                    r = slice(0, rows)
                    for k in range(TOPK):
                        pe.wait_ge(s["diag_rdy"], g * TOPK + k + 1)
                        pe.wait_ge(v_in[k % RING], filled(g, k))
                        for c in (slice(0, BANK), slice(BANK, 2 * BANK)):
                            last = pe.matmul(acc[:, c], diag[r, k, :], vr[r, k % RING, c], start=False, stop=True,
                                             skip_group_check=True)
                        last.then_inc(s["v_used"], 1)

                def step(n, h, parity, rows, before):
                    r = slice(0, rows)
                    g = n * PHEADS + h
                    if isinstance(h, int) and h == 1:
                        pe.wait_ge(s["x2_in"], 16 * (n + 1))
                        if not first(n):
                            pe.wait_ge(s["x3_rdy"], n)
                        for c in (slice(0, BANK), slice(BANK, 2 * BANK)):
                            last = pe.matmul(acc[:, c], C["ident"][r, :], x2[r, c], start=True, stop=True,
                                             skip_group_check=True)
                        last.then_inc(s["seeded"], 1)
                    if not first(g):
                        weigh(g - 1, before)
                steps(pe, step)
                weigh(NT * PHEADS - 1, P)


_INS = ["x_prompt", "x_sample", "cache_sb_k", "cache_sb_v", "state_ret", "norm1_w", "w_in", "ret_gn_w", "w_ret_o",
        "w_sb_o", "w_out", "norm2_w", "w_pq", "pk_keys", "peer_u", "peer_v", "norm_f_w"]
_OUTS = [(1, SEQ, D), (1, SAMPLE, D), (1, 1, SEQ, HEADS, DK), (1, 1, SEQ, HEADS, DK), (1, 1, HEADS, DK, DV),
         (1, 1, SAMPLE, HEADS, DK), (1, 1, SAMPLE, HEADS, DK), (1, 1, HEADS, DK, DV)]


def kernel(**inputs):
    import concourse.bacc as bacc
    from concourse.bass_utils import run_bass_kernel_spmd

    nc = bacc.Bacc("TRN2", target_bir_lowering=False, num_devices=1)
    arrays = {name: np.ascontiguousarray(inputs[name]) for name in _INS}
    arrays["consts"] = CONST_TABLE
    arrays["rope"] = ROPE_TABLE
    args = [nc.dram_tensor(f"in_{n}", a.shape, mybir.dt.from_np(a.dtype), kind="ExternalInput").ap()
            for n, a in arrays.items()]
    outs = [nc.dram_tensor(f"out_{i}", s, F32, kind="ExternalOutput").ap() for i, s in enumerate(_OUTS)]
    build(nc, *args, *outs)
    got = run_bass_kernel_spmd(nc, [{f"in_{n}": a for n, a in arrays.items()}], core_ids=[0])
    return tuple(got.results[0][f"out_{i}"] for i in range(len(_OUTS)))
```

```python
from contextlib import ExitStack

import numpy as np

import concourse.bass as bass
from concourse import mybir

F32 = mybir.dt.float32
F32R = mybir.dt.float32r
U32 = mybir.dt.uint32
ALU = mybir.AluOpType
ACT = mybir.ActivationFunctionType
AX_X = mybir.AxisListType.X

P = 128
D = 1024
KD = D // P
SEQ = 1024
TILES = SEQ // P
SAMPLE = 64
PAST = 128
TOKENS = SEQ + SAMPLE
CHUNK = 64
HEADS = 4
DK = 128
DV = 256
BANK = 512
RQ, RV, RG, SQ, SK, SV, GT = 0, 1024, 2048, 3072, 3584, 4096, 4608
IN_W = 6656
N_CHUNKS = IN_W // BANK
KEYS = 128
PHEADS = 8
TOPK = 16
SLOTS = PHEADS * TOPK
SIDES = 2 * PHEADS
PQ_W = SIDES * P
RING = 8
EPS = 1e-6
LOWEST = -3.0e38
SCORE_SCALE = float(DK) ** -0.5


def host_constants():
    log_g = np.log(1.0 - 2.0 ** (-5.0 - np.arange(HEADS)))
    i = np.arange(P)
    row, col = i[:, None], i[None, :]
    seen = (row // CHUNK) <= (col // CHUNK)
    decay = np.stack([np.where(seen, np.exp(g * (np.abs(row - col) - (col + 1.0))), 0.0) for g in log_g], 1)
    k_dec = np.exp((P - 1.0 - i)[:, None] * log_g[None, :])
    k_dec_sample = np.exp((SAMPLE - 1.0 - i)[:, None] * log_g[None, :])
    mix_parts = {
        "decay": (decay * SCORE_SCALE).reshape(P, HEADS * P),
        "k_dec": np.repeat(k_dec * SCORE_SCALE, DK, axis=1),
        "k_dec_sample": np.repeat(k_dec_sample * SCORE_SCALE, DK, axis=1),
    }
    parts = {
        "ident": np.eye(P),
        "neg_tri": -(row >= col).astype(np.float64),
        "neg_ones": -np.ones((P, P)),
        "inter": np.exp((i[:, None] + 1.0) * log_g[None, :]),
        "iota16": np.tile(np.arange(TOPK), (P, 1)),
        "eps": np.full((P, 1), EPS),
        "one": np.ones((P, 1)),
    }
    def packed(arrays):
        at, where = 0, {}
        for name, a in arrays.items():
            where[name] = (at, at + a.shape[1])
            at += a.shape[1]
        return np.concatenate(list(arrays.values()), 1).astype(np.float32), where

    inv = (np.float32(10000.0) ** (-np.arange(0, DK, 2, dtype=np.float32) / np.float32(DK))).astype(np.float32)
    ang = np.arange(SEQ, dtype=np.float32)[:, None] * inv[None, :]
    rope = np.concatenate([np.cos(ang), np.sin(ang)], 1).astype(np.float32)
    return *packed(parts), *packed(mix_parts), rope


CONST_TABLE, CONST_AT, DECAY_TABLE, DECAY_AT, ROPE_TABLE = host_constants()


def gamma_to(steps):
    return [float((1.0 - 2.0 ** (-5.0 - h)) ** steps) for h in range(HEADS)]


class Chain:

    def __init__(self, eng, sem, start):
        self.eng, self.sem, self.start, self.n = eng, sem, start, 0

    def then(self, ins):
        self.n += 1
        return ins.then_inc(self.sem, 1)

    def wait(self):
        self.eng.wait_ge(self.sem, self.start + self.n)

    def hold(self, hold):
        hold(self.eng, self.sem, self.start + self.n)


class Hold:

    def __init__(self, passed):
        self.passed = passed

    def __call__(self, eng, sem, value):
        eng.wait_ge(sem, value)
        if not isinstance(value, int):
            eng.sem_inc(self.passed, 1)


def broadcast_rows(vec, rows):
    return vec.rearrange("(a n) -> a n", a=1).to_broadcast([rows, vec.shape[0]])


def rstd_newton(dve, chain, m, root, rstd, tmp, scale):
    chain.then(dve.tensor_scalar(m, m, scale, EPS, ALU.mult, ALU.add))
    chain.then(dve.reciprocal(rstd, root))
    chain.wait()
    chain.then(dve.tensor_tensor(tmp, rstd, rstd, ALU.mult))
    chain.wait()
    chain.then(dve.tensor_tensor(tmp, tmp, m, ALU.mult))
    chain.wait()
    chain.then(dve.tensor_scalar(tmp, tmp, -0.5, 1.5, ALU.mult, ALU.add))
    chain.wait()
    chain.then(dve.tensor_tensor(rstd, rstd, tmp, ALU.mult))
    chain.wait()


NEWTON_STEPS = 6


def first(n):
    return isinstance(n, int) and n == 0


def token_col(n):
    return SEQ if first(n) else (n - 1) * P


def thirds(ap):
    return ap.rearrange("p (k r) -> p k r", r=P)


def build(nc, x_prompt, x_sample, cache_k, cache_v, state_ret, norm1_w, w_in, ret_gn_w, w_ret_o, w_sb_o,
          w_out, norm2_w, w_pq, pk_keys, peer_u, peer_v, norm_f_w, consts, decays, rope,
          y_prompt, y_sample, prompt_k, prompt_v, prompt_state, sample_k, sample_v, sample_state):
    scratch = lambda n, s: nc.dram_tensor(n, s, F32).ap()
    proj = scratch("proj", [TOKENS, IN_W])
    skT_d = scratch("skT_d", [TILES, P, HEADS * P])
    x2_d = scratch("x2_d", [TOKENS, D])
    h2_d = scratch("h2_d", [TOKENS, D])
    h2T_d = scratch("h2T_d", [(TILES + 1) * P, KD * P])
    with ExitStack() as ctx:
        sb = lambda n, s, d=F32: ctx.enter_context(nc.sbuf_tensor(n, s, d))
        sem = lambda n: ctx.enter_context(nc.semaphore(n))
        pair = [ctx.enter_context(nc.psum_tensor(f"pair{i}", [P, 2 * BANK], F32)) for i in range(4)]
        cst = sb("cst", [P, CONST_TABLE.shape[1]])
        C = {k: cst[:, a:b] for k, (a, b) in CONST_AT.items()}
        hold = Hold(sem("passed"))
        project(nc, sem, hold, pair, C, cst, consts, x_prompt, x_sample, norm1_w, w_in, proj)
        mix(nc, sem, hold, pair, C, cst, x_prompt, x_sample, cache_k, cache_v, state_ret, ret_gn_w, w_ret_o, w_sb_o, w_out,
            norm2_w, decays, rope, proj, skT_d, x2_d, h2_d, h2T_d, prompt_k, prompt_v, prompt_state, sample_k, sample_v,
            sample_state)
        experts(nc, sem, hold, pair, C, w_pq, pk_keys, peer_u, peer_v, norm_f_w, x2_d, h2_d, h2T_d, y_prompt,
                y_sample)



def project(nc, sem, hold, pair, C, cst, consts, x_prompt, x_sample, norm1_w, w_in, proj):
    NT = TILES + 1
    OUTS = 3
    order = [(SEQ, SAMPLE)] + [(t * P, P) for t in range(TILES)]
    turned_ps = [pair[0], pair[3]]
    ps_out = [pair[1][:, 0:BANK], pair[1][:, BANK:2 * BANK], pair[2][:, 0:BANK]]
    with ExitStack() as ctx:
        sb = lambda n, s, d=F32: ctx.enter_context(nc.sbuf_tensor(n, s, d))
        h_hi = sb("h_hi", [P, KD, TOKENS], F32R)
        h_lo = sb("h_lo", [P, KD, TOKENS], F32R)
        w = sb("w", [P, 2, KD, BANK])
        w_hi = sb("w_hi", [P, 2, KD, BANK], F32R)
        w_lo = sb("w_lo", [P, 2, KD, BANK], F32R)
        out_sb = sb("out_sb", [P, OUTS, BANK])
        xt = sb("xt", [P, 2, D])
        xn = sb("xn", [P, D])
        squares_sb = sb("squares_sb", [P, D])
        g1 = sb("g1", [P, D])
        st = sb("st", [P, 2, 4])
        w_v = w_in[0].rearrange("(k p) n -> p k n", p=P)

        consts_in, g_in = sem("a_consts_in"), sem("a_g_in")
        x_in = [sem(f"a_x_in{i}") for i in range(2)]
        squares, normed, turned = sem("a_squares"), sem("a_normed"), sem("a_turned")
        hi_rdy, lo_rdy, dve_own = sem("a_hi_rdy"), sem("a_lo_rdy"), sem("a_dve_own")
        whi_rdy, wlo_rdy = sem("a_whi_rdy"), sem("a_wlo_rdy")
        w_loaded = [sem(f"a_w_loaded{i}") for i in range(2)]
        ps_ready = [sem(f"a_ps_ready{i}") for i in range(OUTS)]
        copied = [sem(f"a_copied{i}") for i in range(OUTS)]
        stored = [sem(f"a_stored{i}") for i in range(OUTS)]

        def chunks(eng, one):
            with eng.Fori(0, N_CHUNKS // 2 - 1) as c2:
                one(c2 * 2 + 1, 1)
                one(c2 * 2 + 2, 0)
            one(N_CHUNKS - 2, 1)
            one(N_CHUNKS - 1, 0)

        def use_of(c, i):
            return c * (NT // OUTS) + i // OUTS

        def copy(eng, c, i):
            s, use, rows = i % OUTS, use_of(c, i), order[i][1]
            eng.wait_ge(ps_ready[s], use + 1)
            if not (isinstance(c, int) and c == 0 and i < OUTS):
                eng.wait_ge(stored[s], 16 * use)
            if i % 2 == 0:
                ins = eng.activation(out_sb[0:rows, s, :], ps_out[s][0:rows], ACT.Copy)
            else:
                ins = eng.tensor_copy(out_sb[0:rows, s, :], ps_out[s][0:rows])
            ins.then_inc(copied[s], 1)

        def last_product(eng, c, buf):
            if not (isinstance(c, int) and c < 2):
                eng.wait_ge(ps_ready[(NT - 1) % OUTS], (c - 1) * (NT // OUTS))

        with nc.Block() as block:
            @block.sync
            def _(sp):
                for n, (row, rows) in enumerate(order):
                    if n >= 2:
                        sp.wait_ge(normed, n - 1)
                    sp.dma_start(xt[0:rows, n % 2, :], x_sample[0] if n == 0 else x_prompt[0, row:row + rows, :])\
                        .then_inc(x_in[n % 2], 16)
                    if n == 0:
                        sp.dma_start(cst[:, :], consts).then_inc(consts_in, 16)
                        sp.dma_start(g1[:, :], broadcast_rows(norm1_w[0], P)).then_inc(g_in, 16)

                def store(c, buf):
                    for i, (row, rows) in enumerate(order):
                        hold(sp, copied[i % OUTS], use_of(c, i) + 1)
                        sp.dma_start(proj[row:row + rows, bass.ds(c * BANK, BANK)],
                                     out_sb[0:rows, i % OUTS, :]).then_inc(stored[i % OUTS], 16)
                store(0, 0)
                chunks(sp, store)
                for s in stored:
                    hold(sp, s, 16 * N_CHUNKS * (NT // OUTS))

            @block.gpsimd
            def _(pool):
                def load(c, buf):
                    if not (isinstance(c, int) and c < 2):
                        hold(pool, whi_rdy, c - 1)
                        hold(pool, wlo_rdy, c - 1)
                    pool.dma_start(w[:, buf], w_v[:, :, bass.ds(c * BANK, BANK)]).then_inc(w_loaded[buf], 16)
                load(0, 0)
                chunks(pool, load)

            @block.scalar
            def _(act):
                def split(c, buf):
                    act.wait_ge(w_loaded[buf], (c - buf) * 8 + 16)
                    last_product(act, c, buf)
                    act.activation(w_hi[:, buf], w[:, buf], ACT.Copy).then_inc(whi_rdy, 1)

                act.wait_ge(consts_in, 16)
                for n in range(NT + 3):
                    if n < NT:
                        rows, b = order[n][1], n % 2
                        r = slice(0, rows)
                        act.wait_ge(x_in[b], (n // 2 + 1) * 16)
                        if n >= 2:
                            act.wait_ge(normed, n - 1)
                        if n >= 1:
                            act.wait_ge(squares, 2 * n)
                        act.activation(squares_sb[r, :], xt[r, b, :], ACT.Square, accum_out=st[r, b, 0:1])\
                            .then_inc(squares, 1)
                        act.wait_ge(squares, 2 * n + 1)
                        act.activation(st[r, b, 1:2], st[r, b, 0:1], ACT.Sqrt, scale=1.0 / D,
                                       bias=C["eps"][r]).then_inc(squares, 1)
                    if n == 0:
                        split(0, 0)
                    if 1 <= n <= NT:
                        row, rows = order[n - 1]
                        act.wait_ge(turned, n)
                        act.activation(h_hi[:, :, row:row + rows],
                                       thirds(turned_ps[(n - 1) % 2][:, :])[:, :, 0:rows], ACT.Copy)\
                            .then_inc(hi_rdy, 1)
                    if n >= 3 and (n - 3) % 2 == 0:
                        copy(act, 0, n - 3)
                split(1, 1)

                def chunk(c, buf):
                    if not (isinstance(c, int) and c == N_CHUNKS - 1):
                        split(c + 1, 1 - buf)
                    for i in range(0, NT, 2):
                        copy(act, c, i)
                chunks(act, chunk)

            @block.vector
            def _(dve):
                def split(c, buf):
                    dve.wait_ge(whi_rdy, c + 1)
                    last_product(dve, c, buf)
                    dve.tensor_tensor(w_lo[:, buf], w[:, buf], w_hi[:, buf].bitcast(F32), ALU.subtract)\
                        .then_inc(wlo_rdy, 1)

                dve.wait_ge(g_in, 16)
                for n in range(NT + 3):
                    if n < NT:
                        rows, b = order[n][1], n % 2
                        r = slice(0, rows)
                        chain = Chain(dve, dve_own, n * NEWTON_STEPS)
                        dve.wait_ge(squares, 2 * n + 2)
                        rstd_newton(dve, chain, st[r, b, 0:1], st[r, b, 1:2], st[r, b, 2:3], st[r, b, 3:4], 1.0 / D)
                        if n >= 1:
                            dve.wait_ge(turned, n)
                        dve.scalar_tensor_tensor(out=xn[r, :], in0=xt[r, b, :], scalar=st[r, b, 2:3], in1=g1[r, :],
                                                 op0=ALU.mult, op1=ALU.mult).then_inc(normed, 1)
                    if n == 0:
                        split(0, 0)
                    if 1 <= n <= NT:
                        row, rows = order[n - 1]
                        dve.wait_ge(hi_rdy, n)
                        dve.tensor_tensor(h_lo[:, :, row:row + rows],
                                          thirds(turned_ps[(n - 1) % 2][:, :])[:, :, 0:rows],
                                          h_hi[:, :, row:row + rows].bitcast(F32), ALU.subtract).then_inc(lo_rdy, 1)
                    if n >= 3 and (n - 3) % 2 == 1:
                        copy(dve, 0, n - 3)
                split(1, 1)

                def chunk(c, buf):
                    if not (isinstance(c, int) and c == N_CHUNKS - 1):
                        split(c + 1, 1 - buf)
                    for i in range(1, NT, 2):
                        copy(dve, c, i)
                chunks(dve, chunk)

            @block.tensor
            def _(pe):
                def product(c, buf, i):
                    (row, rows), s = order[i], i % OUTS
                    if not (isinstance(c, int) and c == 0 and i < OUTS):
                        pe.wait_ge(copied[s], use_of(c, i))
                    at = slice(row, row + rows)
                    for k in range(KD):
                        for part, (a, b) in enumerate(((h_hi, w_hi), (h_hi, w_lo), (h_lo, w_hi))):
                            last = pe.matmul(ps_out[s][0:rows], a[:, k, at], b[:, buf, k, :],
                                             start=(k == 0 and part == 0), stop=(k == KD - 1 and part == 2))
                    last.then_inc(ps_ready[s], 1)

                pe.wait_ge(consts_in, 16)
                for n in range(NT + 1):
                    if n < NT:
                        rows = order[n][1]
                        pe.wait_ge(normed, n + 1)
                        if n >= 2:
                            pe.wait_ge(hi_rdy, n - 1)
                            pe.wait_ge(lo_rdy, n - 1)
                        for k in range(KD):
                            last = pe.transpose(turned_ps[n % 2][:, k * P:k * P + rows],
                                                xn[0:rows, k * P:(k + 1) * P], C["ident"][0:rows, 0:rows])
                        last.then_inc(turned, 1)
                    if n >= 1:
                        pe.wait_ge(hi_rdy, n)
                        pe.wait_ge(lo_rdy, n)
                        if n == 1:
                            pe.wait_ge(whi_rdy, 1)
                            pe.wait_ge(wlo_rdy, 1)
                        product(0, 0, n - 1)

                def multiply(c, buf):
                    pe.wait_ge(whi_rdy, c + 1)
                    pe.wait_ge(wlo_rdy, c + 1)
                    for i in range(NT):
                        product(c, buf, i)
                chunks(pe, multiply)


def mix(nc, sem, hold, pair, C, cst, x_prompt, x_sample, cache_k, cache_v, state_ret, ret_gn_w, w_ret_o, w_sb_o, w_out,
        norm2_w, decays, rope, proj, skT_d, x2_d, h2_d, h2T_d, prompt_k, prompt_v, prompt_state, sample_k, sample_v,
        sample_state):
    NT = TILES + 1
    qT_ps, kT_ps = pair[0][:, 0:BANK], pair[0][:, BANK:]
    ret_ps = pair[0]
    sqT_ps, skT_ps = pair[1][:, 0:BANK], pair[1][:, BANK:]
    state_ps = pair[1]
    z_ps = pair[1][:, 0:BANK]
    sboT_ps, scores_ps = pair[2][:, 0:BANK], pair[2][:, BANK:]
    merge_ps = pair[3]
    with ExitStack() as ctx:
        sb = lambda n, s, d=F32: ctx.enter_context(nc.sbuf_tensor(n, s, d))
        wret = sb("wret", [P, KD, D])
        wsb = sb("wsb", [P, HEADS, D])
        wout = sb("wout", [P, KD, D])
        gnw = sb("gnw", [P, D])
        dec = sb("dec", [P, DECAY_TABLE.shape[1]])
        C = {**C, **{k: dec[:, a:b] for k, (a, b) in DECAY_AT.items()}}
        g2 = sb("g2", [P, D])
        qk = sb("qk", [P, 1024])
        cs = sb("cs", [P, P])
        rv = sb("rv", [P, D])
        sqkv = sb("sqkv", [P, 3 * BANK])
        rg = sb("rg", [P, D])
        gates = sb("gates", [P, 2 * D])
        x = sb("x", [P, D])
        rot = sb("rot", [P, 1024])
        ra = sb("ra", [P, 1024])
        rb = sb("rb", [P, 1024])
        kd = sb("kd", [P, BANK])
        qT = sb("qT", [P, BANK])
        kT = sb("kT", [P, BANK])
        pT = sb("pT", [P, BANK])
        S = sb("S", [P, HEADS, DV])
        ret = sb("ret", [P, D])
        stats = sb("stats", [P, HEADS, 6])
        mv = sb("mv", [P, HEADS, 2])
        gst = sb("gst", [P, 3, HEADS])
        sqT = sb("sqT", [P, BANK])
        skT = sb("skT", [P, BANK])
        KT = sb("KT", [P, BANK])
        V = sb("V", [P, BANK])
        az = sb("az", [P, BANK])
        sp = sb("sp", [P, BANK])
        spsum = sb("spsum", [P, BANK])
        wT = sb("wT", [P, BANK])
        sboT = sb("sboT", [P, BANK])
        big = sb("big", [P, D])
        turnedT = sb("turnedT", [P, KD, P])
        junk = sb("junk", [P, D])
        n2 = sb("n2", [P, 4])

        names = ("gn_in dec_in weights_in dve_merge qk_in rv_in sqkv_in rg_in gates_in x_in k_in v_in cache_in s_in s_zero dve act qk_rot "
                 "kd_rdy qk_turned qkT_rdy sq_turned skT_rdy scores_rdy pT_rdy state_mm o_rdy ret_rdy S_new sig_rdy "
                 "var_rdy root_rdy r_rdy z_rdy ln_rdy sp_rdy sp_masked suffix_rdy spsum_rdy w_rdy w_masked pv_done "
                 "sbo_rdy r_turned rT_rdy retb_rdy sbb_rdy mixed_rdy m_turned mT_rdy res_rdy x2_rdy sq2_rdy h2_rdy "
                 "h2_turned h2T_rdy kv_out skT_out x2_out h2_out h2T_out state_out cache_turned cacheT_rdy").split()
        s = {n: sem("b_" + n) for n in names}

        def block_no(n, j=0):
            return j if first(n) else 2 + (n * (n - 1)) // 2 + j

        def h4(ap, cols=P):
            return ap.rearrange("p (h r) -> p h r", h=HEADS)[:, :, 0:cols]

        def tiles(eng, tile):
            tile(0, SAMPLE, None, None)
            tile(1, P, 0, SAMPLE)
            with eng.Fori(2, NT) as n:
                tile(n, P, n - 1, P)

        def past_blocks(eng, n, block):
            if first(n):
                block(block_no(0, 1), 1)
            elif not isinstance(n, int):
                with eng.Fori(1, n) as j:
                    block(block_no(n) + j, j)

        def past_no(n, j):
            return ((n - 1) * (n - 2)) // 2 + j

        with nc.Block() as block:
            @block.sync
            def _(sy):
                sy.dma_start(dec[:, :], decays).then_inc(s["dec_in"], 16)

                def tile(n, rows, m, m_rows):
                    r = slice(0, rows)
                    at = bass.ds(token_col(n), rows)
                    pos = bass.ds(PAST if first(n) else token_col(n), rows)
                    if not first(n):
                        hold(sy, s["qk_rot"], n)
                    sy.dma_start(qk[r, :], proj[at, RQ:RV]).then_inc(s["qk_in"], 16)
                    sy.dma_start(cs[r, :], rope[pos, :]).then_inc(s["qk_in"], 16)
                    if not first(n):
                        hold(sy, s["sq_turned"], n)
                        hold(sy, s["pv_done"], block_no(n - 1) + 1)
                        hold(sy, s["kv_out"], 32 * n)
                    sy.dma_start(sqkv[r, :], proj[at, SQ:GT]).then_inc(s["sqkv_in"], 16)
                    if not first(n):
                        hold(sy, s["o_rdy"], n)
                    sy.dma_start(rv[r, :], proj[at, RV:RG]).then_inc(s["rv_in"], 16)
                    if not first(n):
                        hold(sy, s["r_rdy"], n)
                    sy.dma_start(rg[r, :], proj[at, RG:SQ]).then_inc(s["rg_in"], 16)
                    if first(n):
                        for to, what in ((wret, w_ret_o), (wsb, w_sb_o), (wout, w_out)):
                            sy.dma_start(to[:], what[0].rearrange("(k p) n -> p k n", p=P))\
                                .then_inc(s["weights_in"], 16)
                        sy.dma_start(gnw[:, :], broadcast_rows(ret_gn_w[0], P)).then_inc(s["gn_in"], 16)
                        sy.dma_start(g2[:, :], broadcast_rows(norm2_w[0], P)).then_inc(s["gn_in"], 16)
                    else:
                        hold(sy, s["mixed_rdy"], n)
                    sy.dma_start(gates[r, :], proj[at, GT:IN_W]).then_inc(s["gates_in"], 16)
                    if not first(n):
                        store_rows(m, m_rows)
                        hold(sy, s["x2_out"], 16 * n)
                    sy.dma_start(x[r, :], x_sample[0] if first(n) else x_prompt[0, at, :]).then_inc(s["x_in"], 16)

                def store_rows(n, rows):
                    at = bass.ds(token_col(n), rows)
                    hold(sy, s["x2_rdy"], n + 1)
                    sy.dma_start(x2_d[at, :], x[0:rows, :]).then_inc(s["x2_out"], 16)
                    hold(sy, s["h2_rdy"], n + 1)
                    sy.dma_start(h2_d[at, :], big[0:rows, :]).then_inc(s["h2_out"], 16)
                tiles(sy, tile)
                store_rows(TILES, P)
                for o in ("x2_out", "h2_out"):
                    hold(sy, s[o], 16 * NT)

            @block.gpsimd
            def _(pool):
                pool.dma_start(az[:, :], cache_k[0, 0].rearrange("t h d -> t (h d)")).then_inc(s["cache_in"], 16)
                pool.dma_start(V[:, :], cache_v[0, 0].rearrange("t h d -> t (h d)")).then_inc(s["v_in"], 16)
                pool.dma_start(S[:], state_ret[0, 0].rearrange("h k v -> k h v")).then_inc(s["s_in"], 16)

                def tile(n, rows, m, m_rows):
                    r = slice(0, rows)
                    at = bass.ds(token_col(n), rows)
                    k_out, v_out = (sample_k, sample_v) if first(n) else (prompt_k, prompt_v)
                    o_at = slice(0, SAMPLE) if first(n) else at
                    hold(pool, s["sqkv_in"], 16 * (n + 1))
                    for i, o in ((1, k_out), (2, v_out)):
                        pool.dma_start(o[0, 0, o_at].rearrange("t h d -> t (h d)"),
                                       sqkv[r, i * BANK:(i + 1) * BANK]).then_inc(s["kv_out"], 16)
                    if not first(n):
                        if not isinstance(n, int):
                            hold(pool, s["skT_out"], 16 * (n - 1))
                        hold(pool, s["skT_rdy"], 2 * n + 2)
                        pool.dma_start(skT_d[n - 1], skT[:, :]).then_inc(s["skT_out"], 16)
                    for what, rdy, masked in ((sp, "sp_rdy", "sp_masked"), (wT, "w_rdy", "w_masked")):
                        hold(pool, s[rdy], block_no(n) + 1)
                        v = h4(what[r, :], rows)
                        pool.affine_select(out=v, in_=v, compare_op=ALU.is_gt, fill=0.0, base=0,
                                           pattern=[[0, HEADS], [1, rows]], channel_multiplier=-1)\
                            .then_inc(s[masked], 1)
                    if first(n):
                        hold(pool, s["S_new"], 1)
                        pool.dma_start(sample_state[0, 0].rearrange("h k v -> k h v"), S[:])\
                            .then_inc(s["state_out"], 16)
                        hold(pool, s["state_out"], 16)
                        pool.memset(S[:], 0.0).then_inc(s["s_zero"], 1)

                    def past(m, j):
                        key_tile = nc.s_assert_within(n - 1 - j, 0, TILES - 2, 
                                                      skip_runtime_bounds_check_because="1 <= j < n")
                        hold(pool, s["z_rdy"], m)
                        pool.dma_start(KT[:, :], skT_d[bass.ds(key_tile, 1)].rearrange("a p c -> (a p) c"))\
                            .then_inc(s["k_in"], 16)
                        hold(pool, s["pv_done"], m)
                        pool.dma_start(V[:, :], proj[bass.ds(key_tile * P, P), SV:GT]).then_inc(s["v_in"], 16)
                    if not first(n):
                        past_blocks(pool, n, past)
                    if not first(n):
                        store_h2T(m, m_rows)

                def store_h2T(n, rows):
                    hold(pool, s["h2T_rdy"], n + 1)
                    pool.dma_start(h2T_d[bass.ds(n * P, P)].rearrange("p (k c) -> p k c", c=P)[:, :, 0:rows],
                                   turnedT[:, :, 0:rows]).then_inc(s["h2T_out"], 16)
                tiles(pool, tile)
                store_h2T(TILES, P)
                pool.dma_start(prompt_state[0, 0].rearrange("h k v -> k h v"), S[:]).then_inc(s["state_out"], 16)
                hold(pool, s["state_out"], 32)
                hold(pool, s["kv_out"], 32 * NT)
                hold(pool, s["skT_out"], 16 * TILES)
                hold(pool, s["h2T_out"], 16 * NT)

            @block.scalar
            def _(act):
                def turned(n, rows, ready, done):
                    act.wait_ge(s[ready], n + 1)
                    if ready == "r_turned" and not first(n):
                        act.wait_ge(s["h2T_out"], 16 * n)
                    act.activation(turnedT[:, :, 0:rows], thirds(merge_ps[:, :])[:, :, 0:rows], ACT.Copy)\
                        .then_inc(s[done], 1)

                def attend(m, k_rows, q_rows, between=None):
                    kr = slice(0, k_rows)
                    a, z = h4(az[kr, :], q_rows), h4(z_ps[kr, :], q_rows)
                    act.wait_ge(s["z_rdy"], m + 1)
                    act.activation(a, z, ACT.Abs).then_inc(s["act"], 1)
                    act.wait_ge(s["act"], m * 2 + 1)
                    act.activation(a, a, ACT.Exp, scale=-1.0).then_inc(s["act"], 1)
                    act.wait_ge(s["act"], m * 2 + 2)
                    act.activation(a, a, ACT.Ln, bias=C["one"][kr]).then_inc(s["ln_rdy"], 1)
                    if between:
                        between()
                    act.wait_ge(s["suffix_rdy"], m + 1)
                    act.activation(h4(wT[kr, :], q_rows), z, ACT.Exp).then_inc(s["w_rdy"], 1)

                def square(n, rows):
                    r = slice(0, rows)
                    act.wait_ge(s["x2_rdy"], n + 1)
                    if not first(n):
                        act.wait_ge(s["sq2_rdy"], 2 * n)
                    act.activation(junk[r, :], x[r, :], ACT.Square, accum_out=n2[r, 0:1]).then_inc(s["sq2_rdy"], 1)
                    act.wait_ge(s["sq2_rdy"], 2 * n + 1)
                    act.activation(n2[r, 1:2], n2[r, 0:1], ACT.Sqrt, scale=1.0 / D, bias=C["eps"][r])\
                        .then_inc(s["sq2_rdy"], 1)

                def tile(n, rows, m, m_rows):
                    r = slice(0, rows)
                    if first(n):
                        act.wait_ge(s["cache_turned"], 1)
                        act.activation(KT[:, :], z_ps, ACT.Copy).then_inc(s["cacheT_rdy"], 1)
                    act.wait_ge(s["qk_turned"], n + 1)
                    act.activation(h4(qT[:, :], rows), h4(qT_ps, rows), ACT.Copy).then_inc(s["qkT_rdy"], 1)
                    act.activation(h4(kT[:, :], rows), h4(kT_ps, rows), ACT.Copy).then_inc(s["qkT_rdy"], 1)
                    act.wait_ge(s["rg_in"], 16 * (n + 1))
                    act.activation(rb[r, :], rg[r, :], ACT.Sigmoid).then_inc(s["sig_rdy"], 1)
                    act.wait_ge(s["o_rdy"], n + 1)
                    for h in range(HEADS):
                        act.activation(ret[r, h * DV:(h + 1) * DV], ret_ps[r, h * DV:(h + 1) * DV], ACT.Copy,
                                       scale=C["inter"][r, h:h + 1]).then_inc(s["ret_rdy"], 1)
                    attend(block_no(n), rows, rows,
                           None if first(n) else lambda: turned(m, m_rows, "m_turned", "mT_rdy"))
                    act.wait_ge(s["var_rdy"], n + 1)
                    act.activation(gst[r, 0, :], mv[r, :, 1], ACT.Sqrt, bias=C["eps"][r]).then_inc(s["root_rdy"], 1)
                    if not first(n):
                        square(m, m_rows)
                    past_blocks(act, n, lambda b, j: attend(b, P, rows))
                    act.wait_ge(s["gates_in"], 16 * (n + 1))
                    act.activation(gates[r, :], gates[r, :], ACT.Sigmoid).then_inc(s["sig_rdy"], 1)
                    if not first(n):
                        turned(m, m_rows, "h2_turned", "h2T_rdy")
                    turned(n, rows, "r_turned", "rT_rdy")
                tiles(act, tile)
                turned(TILES, P, "m_turned", "mT_rdy")
                square(TILES, P)
                turned(TILES, P, "h2_turned", "h2T_rdy")

            @block.vector
            def _(dve):
                dve.wait_ge(s["dec_in"], 16)
                STEPS = 4 + 3 + 7 + NEWTON_STEPS + 4 + 1 + 1
                MERGE_STEPS = 2 + NEWTON_STEPS

                def attend(n, m, own, k_rows, q_rows, sum_rows):
                    kr = slice(0, k_rows)
                    dve.wait_ge(s["ln_rdy"], m + 1)
                    if not first(m):
                        dve.wait_ge(s["suffix_rdy"], m)
                        dve.wait_ge(s["spsum_rdy"], m)
                    dve.scalar_tensor_tensor(out=h4(sp[kr, :], q_rows), in0=h4(z_ps[kr, :], q_rows), scalar=0.0,
                                             in1=h4(az[kr, :], q_rows), op0=ALU.max, op1=ALU.add)\
                        .then_inc(s["sp_rdy"], 1)
                    add, to = h4(sp[0:sum_rows, :], q_rows), h4(spsum[0:sum_rows, :], q_rows)
                    if own:
                        dve.wait_ge(s["sp_masked"], n + 1)
                        dve.tensor_copy(to, add).then_inc(s["spsum_rdy"], 1)
                    else:
                        dve.wait_ge(s["suffix_rdy"], m + 1)
                        dve.wait_ge(s["spsum_rdy"], m)
                        dve.wait_ge(s["sp_rdy"], m + 1)
                        dve.tensor_tensor(to, to, add, ALU.add).then_inc(s["spsum_rdy"], 1)

                def tile(n, rows, m, m_rows):
                    r = slice(0, rows)
                    k_dec = C["k_dec_sample"] if first(n) else C["k_dec"]
                    gamma = gamma_to(rows)
                    chain = Chain(dve, s["dve"], n * STEPS)
                    dve.wait_ge(s["qk_in"], 32 * (n + 1))
                    if not first(n):
                        dve.wait_ge(s["qk_turned"], n)
                        dve.wait_ge(s["kd_rdy"], n)
                        if not isinstance(n, int):
                            dve.wait_ge(s["mixed_rdy"], n - 1)
                    half = lambda ap, i: ap[r, :].rearrange("p (h two d) -> p two h d", two=2, d=DK // 2)[:, i]
                    cos = cs[r, 0:64].rearrange("p (a d) -> p a d", a=1)
                    sin = cs[r, 64:128].rearrange("p (a d) -> p a d", a=1)
                    chain.then(dve.tensor_tensor(ra[r, :].rearrange("p (h d) -> p h d", d=64),
                                                 qk[r, :].rearrange("p (h d) -> p h d", d=64),
                                                 cos.to_broadcast([rows, 16, 64]), ALU.mult))
                    chain.then(dve.tensor_tensor(half(rot, 0), half(qk, 1), sin.to_broadcast([rows, 8, 64]), ALU.mult))
                    chain.then(dve.tensor_tensor(half(rot, 1), half(qk, 0), sin.to_broadcast([rows, 8, 64]), ALU.mult))
                    chain.wait()
                    chain.then(dve.tensor_tensor(half(rot, 0), half(ra, 0), half(rot, 0), ALU.subtract))
                    dve.tensor_tensor(half(rot, 1), half(ra, 1), half(rot, 1), ALU.add).then_inc(s["qk_rot"], 1)
                    dve.wait_ge(s["qk_rot"], n + 1)
                    chain.wait()
                    if not first(n):
                        dve.wait_ge(s["state_mm"], n)
                    dve.tensor_tensor(kd[r, :], rot[r, BANK:], k_dec[r], ALU.mult).then_inc(s["kd_rdy"], 1)
                    dve.wait_ge(s["sq_turned"], n + 1)
                    dve.tensor_scalar(h4(sqT[:, :], rows), h4(sqT_ps, rows), SCORE_SCALE, None, ALU.mult)\
                        .then_inc(s["skT_rdy"], 1)
                    if not isinstance(n, int):
                        dve.wait_ge(s["skT_out"], 16 * (n - 1))
                    dve.tensor_copy(h4(skT[:, :], rows), h4(skT_ps, rows)).then_inc(s["skT_rdy"], 1)
                    dve.wait_ge(s["scores_rdy"], n + 1)
                    dve.tensor_tensor(h4(pT[r, :], rows), h4(scores_ps[r, :], rows), h4(C["decay"][r], rows),
                                      ALU.mult).then_inc(s["pT_rdy"], 1)
                    if not first(n):
                        merge_ret(m, m_rows)
                    if first(n):
                        dve.wait_ge(s["s_in"], 16)
                    elif isinstance(n, int):
                        dve.wait_ge(s["s_zero"], 1)
                    dve.wait_ge(s["o_rdy"], n + 1)
                    for h in range(HEADS):
                        chain.then(dve.scalar_tensor_tensor(out=S[:, h, :], in0=S[:, h, :], scalar=gamma[h],
                                                            in1=state_ps[:, h * DV:(h + 1) * DV], op0=ALU.mult,
                                                            op1=ALU.add)) if h < HEADS - 1 else \
                            dve.scalar_tensor_tensor(out=S[:, h, :], in0=S[:, h, :], scalar=gamma[h],
                                                     in1=state_ps[:, h * DV:(h + 1) * DV], op0=ALU.mult,
                                                     op1=ALU.add).then_inc(s["S_new"], 1)
                    chain.wait()
                    dve.wait_ge(s["S_new"], n + 1)
                    if not first(n):
                        merge_sb(m, m_rows)
                    attend(n, block_no(n), True, rows, rows, rows)
                    dve.wait_ge(s["ret_rdy"], HEADS * (n + 1))
                    for h in range(HEADS):
                        chain.then(dve.bn_stats(stats[r, h, :], ret[r, h * DV:(h + 1) * DV]))
                    hold(dve, s["dve"], chain.start + chain.n)
                    for h in range(HEADS):
                        ins = dve.bn_aggr(mv[r, h, :], stats[r, h, :])
                        if h < HEADS - 1:
                            chain.then(ins)
                    ins.then_inc(s["var_rdy"], 1)
                    chain.wait()
                    dve.wait_ge(s["var_rdy"], n + 1)
                    dve.wait_ge(s["root_rdy"], n + 1)
                    rstd_newton(dve, chain, mv[r, :, 1], gst[r, 0, :], gst[r, 1, :], gst[r, 2, :], 1.0)
                    for h in range(HEADS):
                        chain.then(dve.tensor_scalar(ret[r, h * DV:(h + 1) * DV], ret[r, h * DV:(h + 1) * DV],
                                                     mv[r, h, 0:1], gst[r, 1, h:h + 1], ALU.subtract, ALU.mult))
                    dve.wait_ge(s["sig_rdy"], 2 * n + 1)
                    chain.then(dve.tensor_tensor(rb[r, :], rb[r, :], rg[r, :], ALU.mult))
                    chain.wait()
                    if first(n):
                        dve.wait_ge(s["gn_in"], 32)
                    chain.then(dve.tensor_tensor(ret[r, :], ret[r, :], gnw[r, :], ALU.mult))
                    chain.wait()
                    dve.tensor_tensor(ret[r, :], ret[r, :], rb[r, :], ALU.mult).then_inc(s["r_rdy"], 1)
                    assert chain.n == STEPS, chain.n
                    if not first(n):
                        merge_end(m, m_rows)
                    past_blocks(dve, n, lambda b, j: attend(n, b, False, P, rows, rows))
                    dve.wait_ge(s["pv_done"], block_no(n + 1) if not first(n) else 2)
                    if not first(n):
                        dve.wait_ge(s["sbb_rdy"], n)
                    dve.tensor_copy(h4(sboT[:, :], rows), h4(sboT_ps, rows)).then_inc(s["sbo_rdy"], 1)

                def merge_ret(n, rows):
                    r = slice(0, rows)
                    chain = Chain(dve, s["dve_merge"], n * MERGE_STEPS)
                    dve.wait_ge(s["sig_rdy"], 2 * n + 2)
                    dve.wait_ge(s["retb_rdy"], n + 1)
                    if not first(n):
                        dve.wait_ge(s["h2_out"], 16 * n)
                        dve.wait_ge(s["h2_turned"], n)
                    chain.then(dve.tensor_tensor(big[r, :], merge_ps[r, :], gates[r, 0:D], ALU.mult))

                def merge_sb(n, rows):
                    r = slice(0, rows)
                    chain = Chain(dve, s["dve_merge"], n * MERGE_STEPS + 1)
                    dve.wait_ge(s["sbb_rdy"], n + 1)
                    chain.then(dve.tensor_tensor(ra[r, :], merge_ps[r, :], gates[r, D:], ALU.mult))
                    chain.wait()
                    dve.tensor_tensor(big[r, :], big[r, :], ra[r, :], ALU.add).then_inc(s["mixed_rdy"], 1)

                def merge_end(n, rows):
                    r = slice(0, rows)
                    chain = Chain(dve, s["dve_merge"], n * MERGE_STEPS + 2)
                    dve.wait_ge(s["x_in"], 16 * (n + 1))
                    dve.wait_ge(s["res_rdy"], n + 1)
                    dve.tensor_tensor(x[r, :], x[r, :], merge_ps[r, :], ALU.add).then_inc(s["x2_rdy"], 1)
                    dve.wait_ge(s["sq2_rdy"], 2 * n + 2)
                    rstd_newton(dve, chain, n2[r, 0:1], n2[r, 1:2], n2[r, 2:3], n2[r, 3:4], 1.0 / D)
                    dve.scalar_tensor_tensor(out=big[r, :], in0=x[r, :], scalar=n2[r, 2:3], in1=g2[r, :],
                                             op0=ALU.mult, op1=ALU.mult).then_inc(s["h2_rdy"], 1)
                tiles(dve, tile)
                merge_ret(TILES, P)
                merge_sb(TILES, P)
                merge_end(TILES, P)

            @block.tensor
            def _(pe):
                def attend(n, m, j, KTt, Vt, k_rows, q_rows, sum_rows, first_gap=None, second_gap=None):
                    kr = slice(0, k_rows)
                    own = isinstance(j, int) and j == 0

                    if own:
                        pe.wait_ge(s["skT_rdy"], 2 * n + 2)
                        pe.wait_ge(s["S_new"], n + 1)
                    elif first(n):
                        pe.wait_ge(s["w_rdy"], m)
                        pe.wait_ge(s["cacheT_rdy"], 1)
                    else:
                        pe.wait_ge(s["w_rdy"], m)
                        pe.wait_ge(s["k_in"], 16 * past_no(n, j))
                    for h in range(HEADS):
                        last = pe.matmul(h4(z_ps[kr, :], q_rows)[:, h], KTt[:, h * P:h * P + k_rows],
                                         h4(sqT[:, :], q_rows)[:, h], start=(h == 0), stop=True,
                                         skip_group_check=True)
                    last.then_inc(s["z_rdy"], 1)
                    if first_gap:
                        first_gap()
                    if own:
                        pe.wait_ge(s["sp_masked"], n + 1)
                    else:
                        pe.wait_ge(s["spsum_rdy"], m)
                        pe.wait_ge(s["sp_rdy"], m + 1)
                        pe.matmul(h4(z_ps[kr, :], q_rows), C["neg_ones"][0:sum_rows, kr],
                                  h4(spsum[0:sum_rows, :], q_rows), start=False, stop=True, skip_group_check=True)
                    pe.matmul(h4(z_ps[kr, :], q_rows), C["neg_tri"][kr, kr], h4(sp[kr, :], q_rows), start=False,
                              stop=True, skip_group_check=True).then_inc(s["suffix_rdy"], 1)
                    if second_gap:
                        second_gap()
                    if own:
                        pe.wait_ge(s["w_masked"], n + 1)
                        if not first(n):
                            pe.wait_ge(s["sbo_rdy"], n)
                        pe.wait_ge(s["sqkv_in"], 16 * (n + 1))
                    else:
                        pe.wait_ge(s["w_rdy"], m + 1)
                        pe.wait_ge(s["v_in"], 16 if first(n) else 16 * (past_no(n, j) + 1))
                    for h in range(HEADS):
                        last = pe.matmul(h4(sboT_ps, q_rows)[:, h], Vt[kr, h * P:(h + 1) * P],
                                         h4(wT[kr, :], q_rows)[:, h], start=(own and h == 0), stop=True,
                                         skip_group_check=True)
                    last.then_inc(s["pv_done"], 1)

                def turn(dst, src, rows, blocks):
                    for k in range(blocks):
                        last = pe.transpose(dst[:, k * P:k * P + rows], src[0:rows, k * P:(k + 1) * P],
                                            C["ident"][0:rows, 0:rows])
                    return last

                def wide(dst, lhsT, rhs, blocks, rows):
                    for half in range(2):
                        c = slice(half * BANK, (half + 1) * BANK)
                        for k in range(blocks):
                            last = pe.matmul(dst[0:rows, c], lhsT(k), rhs[:, k, c], start=(k == 0),
                                             stop=(k == blocks - 1))
                    return last

                def tile(n, rows, m, m_rows):
                    r = slice(0, rows)
                    pe.wait_ge(s["qk_rot"], n + 1)
                    if not first(n):
                        pe.wait_ge(s["ret_rdy"], HEADS * n)
                    turn(pair[0], rot, rows, 8).then_inc(s["qk_turned"], 1)
                    if first(n):
                        pe.wait_ge(s["cache_in"], 16)
                        turn(z_ps, az, P, 4).then_inc(s["cache_turned"], 1)
                        pe.wait_ge(s["cacheT_rdy"], 1)
                    else:
                        pe.wait_ge(s["w_rdy"], block_no(n))
                    pe.wait_ge(s["sqkv_in"], 16 * (n + 1))
                    turn(pair[1], sqkv, rows, 8).then_inc(s["sq_turned"], 1)
                    if not first(n):
                        merge_ret(m, m_rows)
                    pe.wait_ge(s["qkT_rdy"], 2 * n + 2)
                    if not first(n):
                        pe.wait_ge(s["pT_rdy"], n)
                    for h in range(HEADS):
                        last = pe.matmul(h4(scores_ps[r, :], rows)[:, h], kT[:, h * P:h * P + rows],
                                         qT[:, h * P:h * P + rows], start=(h == 0), stop=True, skip_group_check=True)
                    last.then_inc(s["scores_rdy"], 1)
                    pe.wait_ge(s["rv_in"], 16 * (n + 1))
                    pe.wait_ge(s["kd_rdy"], n + 1)
                    pe.wait_ge(s["skT_rdy"], 2 * n + 2)
                    for h in range(HEADS):
                        v = slice(h * DV, (h + 1) * DV)
                        last = pe.matmul(state_ps[:, v], kd[r, h * P:(h + 1) * P], rv[r, v], start=(h % 2 == 0),
                                         stop=True, skip_group_check=True)
                    last.then_inc(s["state_mm"], 1)
                    pe.wait_ge(s["pT_rdy"], n + 1)
                    if first(n):
                        pe.wait_ge(s["s_in"], 16)
                    elif isinstance(n, int):
                        pe.wait_ge(s["s_zero"], 1)
                    else:
                        pe.wait_ge(s["S_new"], n)
                    for h in range(HEADS):
                        v = slice(h * DV, (h + 1) * DV)
                        pe.matmul(ret_ps[r, v], pT[r, h * P:h * P + rows], rv[r, v], start=(h % 2 == 0), stop=True,
                                  skip_group_check=True)
                        last = pe.matmul(ret_ps[r, v], qT[:, h * P:h * P + rows], S[:, h, :], start=False, stop=True,
                                         skip_group_check=True)
                    last.then_inc(s["o_rdy"], 1)
                    if first(n):
                        attend(n, block_no(n), 0, skT, sqkv[:, 2 * BANK:], rows, rows, rows)
                    else:
                        merge_sb(m, m_rows)
                        attend(n, block_no(n), 0, skT, sqkv[:, 2 * BANK:], rows, rows, rows,
                               lambda: turn_mixed(m, m_rows), lambda: residual(m, m_rows))
                    past_blocks(pe, n, lambda b, j: attend(n, b, j, KT, V, P, rows, rows))
                    if not first(n):
                        turn_h2(m, m_rows)
                        pe.wait_ge(s["h2T_rdy"], n)
                    pe.wait_ge(s["r_rdy"], n + 1)
                    turn(merge_ps, ret, rows, 8).then_inc(s["r_turned"], 1)

                def merge_ret(n, rows):
                    if first(n):
                        pe.wait_ge(s["weights_in"], 48)
                    pe.wait_ge(s["rT_rdy"], n + 1)
                    wide(merge_ps, lambda k: turnedT[:, k, 0:rows], wret, KD, rows).then_inc(s["retb_rdy"], 1)

                def merge_sb(n, rows):
                    pe.wait_ge(s["sbo_rdy"], n + 1)
                    pe.wait_ge(s["dve_merge"], n * (2 + NEWTON_STEPS) + 1)
                    wide(merge_ps, lambda k: sboT[:, k * P:k * P + rows], wsb, HEADS, rows).then_inc(s["sbb_rdy"], 1)

                def turn_mixed(n, rows):
                    pe.wait_ge(s["mixed_rdy"], n + 1)
                    turn(merge_ps, big, rows, 8).then_inc(s["m_turned"], 1)

                def residual(n, rows):
                    pe.wait_ge(s["mT_rdy"], n + 1)
                    wide(merge_ps, lambda k: turnedT[:, k, 0:rows], wout, KD, rows).then_inc(s["res_rdy"], 1)

                def turn_h2(n, rows):
                    pe.wait_ge(s["h2_rdy"], n + 1)
                    turn(merge_ps, big, rows, 8).then_inc(s["h2_turned"], 1)
                tiles(pe, tile)
                for part in (merge_ret, merge_sb, turn_mixed, residual, turn_h2):
                    part(TILES, P)
def experts(nc, sem, hold, pair, C, w_pq, pk_keys, peer_u, peer_v, norm_f_w, x2_d, h2_d, h2T_d, y_prompt, y_sample):
    NT = TILES + 1
    CHAIN = 6
    ROUTE_STEPS = 5 * SIDES + 3 + 5 * PHEADS + 14
    HALF = SIDES // 2
    GELU_CUBE, GELU_ROOT = 0.044715, float(np.sqrt(2.0 / np.pi))
    acc, q_ps, s_ps = pair[0], pair[1], pair[2]
    with ExitStack() as ctx:
        sb = lambda n, s, d=F32: ctx.enter_context(nc.sbuf_tensor(n, s, d))
        wpq = sb("wpq", [P, KD, PQ_W])
        pkT = sb("pkT", [P, SIDES, P])
        hT = sb("r_hT", [P, KD, P])
        qT = sb("r_qT", [P, HALF, P])
        sc = sb("sc", [P, SIDES, KEYS])
        sc2 = sb("sc2", [P, SIDES, KEYS])
        top = sb("top", [P, SIDES, TOPK])
        topi = sb("topi", [P, SIDES, TOPK], U32)
        topf = sb("topf", [P, SIDES, TOPK])
        best = sb("best", [P, PHEADS, TOPK])
        besti = sb("besti", [P, PHEADS, TOPK], U32)
        parti = sb("parti", [P, 2, PHEADS, TOPK], U32)
        part = sb("part", [P, 2, PHEADS, TOPK])
        found = sb("found", [P, 2, PHEADS, TOPK])
        sums = sb("sums", [P, PHEADS])
        cand = sc[:].rearrange("p (h two) k -> p h (two k)", two=2)
        cand2 = sc2[:].rearrange("p (h two) k -> p h (two k)", two=2)
        grid = lambda ap: ap.rearrange("p h (a b) -> p h a b", a=TOPK)
        keys = sc
        eidx = sb("eidx", [P, NT * SLOTS], U32)
        gate = sb("gate", [P, NT * SLOTS])
        ur = sb("ur", [P, RING, D])
        vr = sb("vr", [P, RING, D])
        idx_u = sb("idx_u", [P, 2, TOPK], U32)
        idx_v = sb("idx_v", [P, 2, TOPK], U32)
        h2 = sb("h2", [P, D])
        x2 = sb("x2t", [P, D])
        x3 = sb("x3", [P, D])
        gf = sb("gf", [P, D])
        dots = sb("dots", [P, 2, TOPK])
        ge = sb("ge", [P, 2, TOPK])
        coef = sb("coef", [P, 2, TOPK])
        diag = sb("diag", [P, TOPK, P])
        n3 = sb("n3", [P, 4])

        names = ("gf_in h2_in x2_in u_staged v_staged u_used v_used gelu norm arg_rdy gelu_exp coef_rdy diag_rdy seeded "
                 "x3_rdy sq3_rdy y_rdy y_out").split()
        s = {n: sem("d_" + n) for n in names}
        s.update({n: sem("c_" + n) for n in ("w_in keys_in h_in keys_turned keysT_rdy q_rdy qT_rdy s_rdy sc_rdy dve "
                                             "best_rdy exp_rdy gates_rdy").split()})
        u_in = [sem(f"d_u_in{i}") for i in range(RING)]
        v_in = [sem(f"d_v_in{i}") for i in range(RING)]

        def steps(eng, step, between=None):
            def tile(n, rows):
                before = SAMPLE if isinstance(n, int) and n < 2 else P
                for h in range(PHEADS):
                    step(n, h, rows, before if h == 0 else rows)
                    if between and not (isinstance(n, int) and n == TILES):
                        between(n + 1, P, h)
            tile(0, SAMPLE)
            tile(1, P)
            with eng.Fori(2, TILES) as n:
                tile(n, P)
            tile(TILES, P)

        def route_all(part, n, rows):
            for h in range(PHEADS):
                part(n, rows, h)

        def filled(g, k):
            return 16 * (g * (TOPK // RING) + k // RING + 1)

        with nc.Block() as block:
            @block.sync
            def _(sy):
                sy.dma_start(keys[:].rearrange("k (h two) c -> k two h c", two=2)[:, 0],
                             pk_keys[0, 0].rearrange("h k c -> k h c")).then_inc(s["keys_in"], 16)
                sy.dma_start(keys[:].rearrange("k (h two) c -> k two h c", two=2)[:, 1],
                             pk_keys[0, 1].rearrange("h k c -> k h c")).then_inc(s["keys_in"], 16)
                sy.dma_start(wpq[:], w_pq[0].rearrange("(k p) n -> p k n", p=P)).then_inc(s["w_in"], 16)
                sy.dma_start(gf[:, :], broadcast_rows(norm_f_w, P)).then_inc(s["gf_in"], 16)

                def load_hT(n, rows):
                    if not first(n):
                        hold(sy, s["q_rdy"], 2 * n)
                    sy.dma_start(hT[:, :, 0:rows],
                                 h2T_d[bass.ds(n * P, P)].rearrange("p (k c) -> p k c", c=P)[:, :, 0:rows])\
                        .then_inc(s["h_in"], 16)

                def store(n, rows, out):
                    hold(sy, s["y_rdy"], n + 1)
                    sy.dma_start(out, x3[0:rows, :]).then_inc(s["y_out"], 16)

                def tile(n, rows):
                    r = slice(0, rows)
                    at = bass.ds(token_col(n), rows)
                    if not first(n):
                        hold(sy, s["u_used"], n * SLOTS)
                    sy.dma_start(h2[r, :], h2_d[at, :]).then_inc(s["h2_in"], 16)
                    if not (isinstance(n, int) and n == TILES):
                        load_hT(n + 1, P)
                    if not first(n):
                        hold(sy, s["seeded"], n)
                    sy.dma_start(x2[r, :], x2_d[at, :]).then_inc(s["x2_in"], 16)
                    if not first(n):
                        if isinstance(n, int) and n == 1:
                            store(0, SAMPLE, y_sample[0])
                        else:
                            store(n - 1, P, y_prompt[0, bass.ds((n - 2) * P, P), :])
                load_hT(0, SAMPLE)
                tile(0, SAMPLE)
                tile(1, P)
                with sy.Fori(2, TILES) as n:
                    tile(n, P)
                tile(TILES, P)
                store(TILES, P, y_prompt[0, SEQ - P:SEQ, :])
                sy.wait_ge(s["y_out"], 16 * NT)

            @block.gpsimd
            def _(pool):
                def gather(ring, table, idx, k, rows, arrived):
                    pool.indirect_dma_start(ring[0:rows, k % RING, :], None, table,
                                            bass.IndirectOffsetOnAxis(ap=idx[0:rows, k:k + 1], axis=0))\
                        .then_inc(arrived[k % RING], 16)

                def gather_v(g, parity, k, rows):
                    if not (first(g) and k < RING):
                        hold(pool, s["v_used"], g * TOPK + k + 1 - RING)
                    gather(vr, peer_v[0], idx_v[:, parity], k, rows, v_in)

                def stage_v(g, parity, rows):
                    if not isinstance(g, int):
                        hold(pool, s["v_used"], (g - 1) * TOPK)
                    pool.tensor_copy(idx_v[0:rows, parity], eidx[0:rows, bass.ds(g * TOPK, TOPK)])\
                        .then_inc(s["v_staged"], 1)
                    hold(pool, s["v_staged"], g + 1)

                def step(n, h, rows, before):
                    g, parity = n * PHEADS + h, h % 2
                    if h == 0:
                        hold(pool, s["gates_rdy"], n + 1)
                    if not isinstance(g, int) or g > 1:
                        hold(pool, s["u_used"], (g - 1) * TOPK)
                    pool.tensor_copy(idx_u[0:rows, parity], eidx[0:rows, bass.ds(g * TOPK, TOPK)])\
                        .then_inc(s["u_staged"], 1)
                    hold(pool, s["u_staged"], g + 1)
                    if not first(g):
                        stage_v(g - 1, 1 - parity, before)
                    for k in range(TOPK):
                        if not (first(g) and k < RING):
                            hold(pool, s["u_used"], g * TOPK + k + 1 - RING)
                        gather(ur, peer_u[0], idx_u[:, parity], k, rows, u_in)
                        if not first(g):
                            gather_v(g - 1, 1 - parity, k, before)
                steps(pool, step)
                last = NT * PHEADS - 1
                pool.wait_ge(s["v_used"], (last - 1) * TOPK)
                pool.tensor_copy(idx_v[:, 1], eidx[:, last * TOPK:]).then_inc(s["v_staged"], 1)
                pool.wait_ge(s["v_staged"], last + 1)
                for k in range(TOPK):
                    gather_v(last, 1, k, P)

            @block.scalar
            def _(act):
                for half in range(2):
                    act.wait_ge(s["keys_turned"], half + 1)
                    act.activation(pkT[:, half * 8:half * 8 + 8, :], thirds(pair[half + 1][:, :]), ACT.Copy)\
                        .then_inc(s["keysT_rdy"], 1)

                def q_copy(n, rows, i):
                    r = slice(0, rows)
                    act.wait_ge(s["q_rdy"], 2 * n + i + 1)
                    if not (first(n) and i == 0):
                        act.wait_ge(s["s_rdy"], 2 * n + i)
                    act.activation(qT[:, :, r], thirds(q_ps[:, :])[:, :, r], ACT.Copy).then_inc(s["qT_rdy"], 1)

                def s_copy(n, rows, i):
                    r = slice(0, rows)
                    act.wait_ge(s["s_rdy"], 2 * n + i + 1)
                    if not first(n):
                        act.wait_ge(s["gates_rdy"], n)
                    act.activation(sc[r, i * HALF:(i + 1) * HALF, :], thirds(s_ps[r, :]), ACT.Copy)\
                        .then_inc(s["sc_rdy"], 1)

                def routing(n, rows, h):
                    if h == 0:
                        q_copy(n, rows, 0)
                    elif h == 1:
                        s_copy(n, rows, 0)
                        q_copy(n, rows, 1)
                    elif h == 2:
                        s_copy(n, rows, 1)
                    elif h == 4:
                        act.wait_ge(s["best_rdy"], n + 1)
                        act.activation(best[0:rows], best[0:rows], ACT.Exp).then_inc(s["exp_rdy"], 1)

                def finish(n, rows):
                    r = slice(0, rows)
                    act.wait_ge(s["v_used"], (n + 1) * SLOTS)
                    if not first(n):
                        act.wait_ge(s["y_out"], 16 * n)
                    act.activation(x3[r, :], acc[r, :], ACT.Copy).then_inc(s["x3_rdy"], 1)
                    act.wait_ge(s["x3_rdy"], n + 1)
                    act.activation(acc[r, :], x3[r, :], ACT.Square, accum_out=n3[r, 0:1]).then_inc(s["sq3_rdy"], 1)
                    act.wait_ge(s["sq3_rdy"], 2 * n + 1)
                    act.activation(n3[r, 1:2], n3[r, 0:1], ACT.Sqrt, scale=1.0 / D, bias=C["eps"][r])\
                        .then_inc(s["sq3_rdy"], 1)

                def step(n, h, rows, before):
                    r = slice(0, rows)
                    g, parity = n * PHEADS + h, h % 2
                    act.wait_ge(s["arg_rdy"], g + 1)
                    act.activation(ge[r, parity], ge[r, parity], ACT.Exp, scale=-2.0 * GELU_ROOT)\
                        .then_inc(s["gelu_exp"], 1)
                    if h == 0 and not first(n):
                        finish(n - 1, before)
                    act.wait_ge(s["coef_rdy"], g + 1)
                    for k in range(TOPK):
                        if not first(g):
                            act.wait_ge(s["v_used"], (g - 1) * TOPK + k + 1)
                        act.activation(diag[r, k, :], C["ident"][r, :], ACT.Copy, scale=coef[r, parity, k:k + 1])\
                            .then_inc(s["diag_rdy"], 1)
                route_all(routing, 0, SAMPLE)
                steps(act, step, routing)
                finish(TILES, P)

            @block.vector
            def _(dve):
                dve.wait_ge(s["gf_in"], 16)

                def top16(chain, values, spare, out, out_i, count, r):
                    for i in range(count):
                        chain.then(dve.max(out[r, i, 0:8], values[r, i]))
                    chain.hold(hold)
                    for i in range(count):
                        chain.then(dve.max_index(out_i[r, i, 0:8], out[r, i, 0:8], values[r, i]))
                    for i in range(count):
                        chain.then(dve.match_replace(spare[r, i], out[r, i, 0:8], values[r, i], LOWEST))
                    chain.hold(hold)
                    for i in range(count):
                        chain.then(dve.max(out[r, i, 8:16], spare[r, i]))
                    chain.hold(hold)
                    for i in range(count):
                        chain.then(dve.max_index(out_i[r, i, 8:16], out[r, i, 8:16], spare[r, i]))
                    chain.hold(hold)

                def routing(n, rows, h):
                    r = slice(0, rows)
                    side = lambda ap, i: ap[r].rearrange("p (h two) k -> p two h k", two=2)[:, i]
                    full = [rows, PHEADS, TOPK, TOPK]
                    over_b = lambda ap: ap.rearrange("p h (k a) -> p h k a", a=1).to_broadcast(full)
                    over_a = lambda ap: ap.rearrange("p h (a k) -> p h a k", a=1).to_broadcast(full)
                    if h in (2, 3):
                        i = h - 2
                        chain = Chain(dve, s["dve"], n * ROUTE_STEPS + i * 5 * HALF)
                        v = slice(i * HALF, (i + 1) * HALF)
                        hold(dve, s["sc_rdy"], 2 * n + i + 1)
                        top16(chain, sc[:, v], sc2[:, v], top[:, v], topi[:, v], HALF, r)
                    elif h == 4:
                        chain = Chain(dve, s["dve"], n * ROUTE_STEPS + 5 * SIDES)
                        chain.then(dve.tensor_tensor(grid(cand)[r], over_b(side(top, 0)), over_a(side(top, 1)), ALU.add))
                        chain.then(dve.tensor_copy(topf[r], topi[r]))
                        chain.hold(hold)
                        top16(chain, cand, cand2, best, besti, PHEADS, r)
                        peak = best[r, :, 0:1].to_broadcast([rows, PHEADS, TOPK])
                        chain.then(dve.tensor_copy(part[r, 0, :, :], peak))
                        chain.wait()
                        dve.tensor_tensor(best[r], best[r], part[r, 0], ALU.subtract).then_inc(s["best_rdy"], 1)
                    elif h == 5:
                        chain = Chain(dve, s["dve"], n * ROUTE_STEPS + 5 * SIDES + 5 * PHEADS + 3)
                        chain.then(dve.tensor_scalar(parti[r, 0], besti[r], 4, None, ALU.logical_shift_right))
                        chain.then(dve.tensor_scalar(parti[r, 1], besti[r], 15, None, ALU.bitwise_and))
                        chain.wait()
                        dve.wait_ge(s["best_rdy"], n + 1)
                        chain.then(dve.tensor_copy(part[r], parti[r]))
                        chain.wait()
                        iota = C["iota16"][r].rearrange("p (a b k) -> p a b k", a=1, b=1).to_broadcast(full)
                        for i in range(2):
                            hot = grid((cand, cand2)[i])[r]
                            chain.then(dve.tensor_tensor(hot, over_b(part[r, i]), iota, ALU.is_equal))
                        chain.wait()
                        for i in range(2):
                            hot = grid((cand, cand2)[i])[r]
                            chain.then(dve.tensor_tensor(hot, hot, over_a(side(topf, i)), ALU.mult))
                        chain.wait()
                        for i in range(2):
                            hot = grid((cand, cand2)[i])[r]
                            chain.then(dve.tensor_reduce(found[r, i], hot, AX_X, ALU.add))
                        chain.wait()
                        chain.then(dve.scalar_tensor_tensor(out=part[r, 0], in0=found[r, 0], scalar=float(KEYS),
                                                            in1=found[r, 1], op0=ALU.mult, op1=ALU.add))
                        chain.wait()
                        slot = bass.ds(n * SLOTS, SLOTS)
                        flat = lambda ap: ap.rearrange("p h k -> p (h k)")
                        chain.then(dve.tensor_copy(eidx[r, slot], flat(part[r, 0])))
                        dve.wait_ge(s["exp_rdy"], n + 1)
                        chain.then(dve.tensor_reduce(sums[r, :], best[r], AX_X, ALU.add))
                        chain.wait()
                        chain.then(dve.reciprocal(sums[r, :], sums[r, :]))
                        chain.wait()
                        chain.then(dve.tensor_copy(part[r, 1], sums[r, :].rearrange("p (h a) -> p h a", a=1)
                                                   .to_broadcast([rows, PHEADS, TOPK])))
                        chain.wait()
                        dve.tensor_tensor(gate[r, slot], flat(best[r]), flat(part[r, 1]), ALU.mult)\
                            .then_inc(s["gates_rdy"], 1)
                        assert 5 * SIDES + 5 * PHEADS + 3 + chain.n == ROUTE_STEPS, chain.n

                def finish(n, rows):
                    r = slice(0, rows)
                    chain = Chain(dve, s["norm"], n * NEWTON_STEPS)
                    dve.wait_ge(s["sq3_rdy"], 2 * n + 2)
                    rstd_newton(dve, chain, n3[r, 0:1], n3[r, 1:2], n3[r, 2:3], n3[r, 3:4], 1.0 / D)
                    dve.scalar_tensor_tensor(out=x3[r, :], in0=x3[r, :], scalar=n3[r, 2:3], in1=gf[r, :],
                                             op0=ALU.mult, op1=ALU.mult).then_inc(s["y_rdy"], 1)

                def step(n, h, rows, before):
                    r = slice(0, rows)
                    g, parity = n * PHEADS + h, h % 2
                    if h == 0:
                        hold(dve, s["h2_in"], 16 * (n + 1))
                    if not isinstance(g, int) or g > 1:
                        hold(dve, s["coef_rdy"], g - 1)
                    for k in range(TOPK):
                        dve.wait_ge(u_in[k % RING], filled(g, k))
                        dve.tensor_tensor_reduce(ur[r, k % RING, :], ur[r, k % RING, :], h2[r, :], 1.0, 0.0,
                                                 ALU.mult, ALU.add, dots[r, parity, k:k + 1])\
                            .then_inc(s["u_used"], 1)
                    chain = Chain(dve, s["gelu"], g * CHAIN)
                    d, t = dots[r, parity], ge[r, parity]
                    dve.wait_ge(s["u_used"], (g + 1) * TOPK)
                    chain.then(dve.tensor_tensor(t, d, d, ALU.mult))
                    chain.wait()
                    chain.then(dve.tensor_scalar(t, t, GELU_CUBE, 1.0, ALU.mult, ALU.add))
                    chain.wait()
                    chain.then(dve.tensor_tensor(t, t, d, ALU.mult))
                    chain.wait()
                    dve.tensor_scalar(t, t, -50.0, None, ALU.max).then_inc(s["arg_rdy"], 1)
                    dve.wait_ge(s["gelu_exp"], g + 1)
                    chain.then(dve.tensor_scalar(t, t, 1.0, None, ALU.add))
                    chain.wait()
                    chain.then(dve.reciprocal(t, t))
                    chain.wait()
                    chain.then(dve.tensor_tensor(t, t, d, ALU.mult))
                    chain.wait()
                    if not isinstance(g, int) or g > 1:
                        dve.wait_ge(s["diag_rdy"], (g - 1) * TOPK)
                    dve.tensor_tensor(coef[r, parity], t, gate[r, bass.ds(g * TOPK, TOPK)], ALU.mult)\
                        .then_inc(s["coef_rdy"], 1)
                    if h == 0 and not first(n):
                        finish(n - 1, before)
                route_all(routing, 0, SAMPLE)
                steps(dve, step, routing)
                finish(TILES, P)

            @block.tensor
            def _(pe):
                pe.wait_ge(s["keys_in"], 32)
                for half in range(2):
                    for i in range(8):
                        last = pe.transpose(pair[half + 1][:, i * P:(i + 1) * P], keys[:, half * 8 + i, :], C["ident"])
                    last.then_inc(s["keys_turned"], 1)
                pe.wait_ge(s["w_in"], 16)
                pe.wait_ge(s["keysT_rdy"], 2)

                def queries(n, rows, i):
                    r = slice(0, rows)
                    pe.wait_ge(s["h_in"], 16 * (n + 1))
                    if not (first(n) and i == 0):
                        pe.wait_ge(s["qT_rdy"], 2 * n + i)
                    for j in range(HALF):
                        for k in range(KD):
                            last = pe.matmul(q_ps[:, j * P:j * P + rows],
                                             wpq[:, k, (i * HALF + j) * P:(i * HALF + j + 1) * P], hT[:, k, r],
                                             start=(k == 0), stop=(k == KD - 1))
                    last.then_inc(s["q_rdy"], 1)

                def key_scores(n, rows, i):
                    r = slice(0, rows)
                    pe.wait_ge(s["qT_rdy"], 2 * n + i + 1)
                    if not (first(n) and i == 0):
                        pe.wait_ge(s["sc_rdy"], 2 * n + i)
                    for j in range(HALF):
                        last = pe.matmul(s_ps[r, j * P:(j + 1) * P], qT[:, j, r], pkT[:, i * HALF + j, :],
                                         start=True, stop=True)
                    last.then_inc(s["s_rdy"], 1)

                def routing(n, rows, h):
                    if h == 0:
                        queries(n, rows, 0)
                    elif h == 1:
                        key_scores(n, rows, 0)
                        queries(n, rows, 1)
                    elif h == 2:
                        key_scores(n, rows, 1)

                def weigh(g, rows):
                    r = slice(0, rows)
                    for k in range(TOPK):
                        pe.wait_ge(s["diag_rdy"], g * TOPK + k + 1)
                        pe.wait_ge(v_in[k % RING], filled(g, k))
                        for c in (slice(0, BANK), slice(BANK, 2 * BANK)):
                            last = pe.matmul(acc[:, c], diag[r, k, :], vr[r, k % RING, c], start=False, stop=True,
                                             skip_group_check=True)
                        last.then_inc(s["v_used"], 1)

                def step(n, h, rows, before):
                    r = slice(0, rows)
                    g, parity = n * PHEADS + h, h % 2
                    if h == 1:
                        pe.wait_ge(s["x2_in"], 16 * (n + 1))
                        if not first(n):
                            pe.wait_ge(s["sq3_rdy"], 2 * n - 1)
                        for c in (slice(0, BANK), slice(BANK, 2 * BANK)):
                            last = pe.matmul(acc[:, c], C["ident"][r, :], x2[r, c], start=True, stop=True,
                                             skip_group_check=True)
                        last.then_inc(s["seeded"], 1)
                    if not first(g):
                        weigh(g - 1, before)
                route_all(routing, 0, SAMPLE)
                steps(pe, step, routing)
                weigh(NT * PHEADS - 1, P)


_INS = ["x_prompt", "x_sample", "cache_sb_k", "cache_sb_v", "state_ret", "norm1_w", "w_in", "ret_gn_w", "w_ret_o",
        "w_sb_o", "w_out", "norm2_w", "w_pq", "pk_keys", "peer_u", "peer_v", "norm_f_w"]
_OUTS = [(1, SEQ, D), (1, SAMPLE, D), (1, 1, SEQ, HEADS, DK), (1, 1, SEQ, HEADS, DK), (1, 1, HEADS, DK, DV),
         (1, 1, SAMPLE, HEADS, DK), (1, 1, SAMPLE, HEADS, DK), (1, 1, HEADS, DK, DV)]


def kernel(**inputs):
    import concourse.bacc as bacc
    from concourse.bass_utils import run_bass_kernel_spmd

    nc = bacc.Bacc("TRN2", target_bir_lowering=False, num_devices=1)
    arrays = {name: np.ascontiguousarray(inputs[name]) for name in _INS}
    arrays["consts"] = CONST_TABLE
    arrays["decays"] = DECAY_TABLE
    arrays["rope"] = ROPE_TABLE
    args = [nc.dram_tensor(f"in_{n}", a.shape, mybir.dt.from_np(a.dtype), kind="ExternalInput").ap()
            for n, a in arrays.items()]
    outs = [nc.dram_tensor(f"out_{i}", s, F32, kind="ExternalOutput").ap() for i, s in enumerate(_OUTS)]
    build(nc, *args, *outs)
    got = run_bass_kernel_spmd(nc, [{f"in_{n}": a for n, a in arrays.items()}], core_ids=[0])
    return tuple(got.results[0][f"out_{i}"] for i in range(len(_OUTS)))
```

```python
from contextlib import ExitStack

import numpy as np

import concourse.bass as bass
from concourse import mybir

F32 = mybir.dt.float32
F32R = mybir.dt.float32r
U32 = mybir.dt.uint32
ALU = mybir.AluOpType
ACT = mybir.ActivationFunctionType
AX_X = mybir.AxisListType.X

P = 128
D = 1024
KD = D // P
SEQ = 1024
TILES = SEQ // P
SAMPLE = 64
PAST = 128
TOKENS = SEQ + SAMPLE
CHUNK = 64
HEADS = 4
DK = 128
DV = 256
BANK = 512
RQ, RV, RG, SQ, SK, SV, GT = 0, 1024, 2048, 3072, 3584, 4096, 4608
IN_W = 6656
N_CHUNKS = IN_W // BANK
KEYS = 128
PHEADS = 8
TOPK = 16
SLOTS = PHEADS * TOPK
SIDES = 2 * PHEADS
PQ_W = SIDES * P
RING = 8
EPS = 1e-6
LOWEST = -3.0e38
SCORE_SCALE = float(DK) ** -0.5


def host_constants():
    log_g = np.log(1.0 - 2.0 ** (-5.0 - np.arange(HEADS)))
    i = np.arange(P)
    row, col = i[:, None], i[None, :]
    seen = (row // CHUNK) <= (col // CHUNK)
    decay = np.stack([np.where(seen, np.exp(g * (np.abs(row - col) - (col + 1.0))), 0.0) for g in log_g], 1)
    k_dec = np.exp((P - 1.0 - i)[:, None] * log_g[None, :])
    k_dec_sample = np.exp((SAMPLE - 1.0 - i)[:, None] * log_g[None, :])
    mix_parts = {
        "zeros": np.zeros((P, P)),
        "before": (col > row).astype(np.float64),
        "decay": (decay * SCORE_SCALE).reshape(P, HEADS * P),
        "k_dec": np.repeat(k_dec * SCORE_SCALE, DK, axis=1),
        "k_dec_sample": np.repeat(k_dec_sample * SCORE_SCALE, DK, axis=1),
    }
    parts = {
        "ident": np.eye(P),
        "fold": np.concatenate([np.eye(P)[0:SAMPLE], np.eye(P)[0:SAMPLE]], 0),
        "neg_tri": -(row >= col).astype(np.float64),
        "neg_ones": -np.ones((P, P)),
        "inter": np.exp((i[:, None] + 1.0) * log_g[None, :]),
        "iota16": np.tile(np.arange(TOPK), (P, 1)),
        "eps": np.full((P, 1), EPS),
        "one": np.ones((P, 1)),
    }
    def packed(arrays):
        at, where = 0, {}
        for name, a in arrays.items():
            where[name] = (at, at + a.shape[1])
            at += a.shape[1]
        return np.concatenate(list(arrays.values()), 1).astype(np.float32), where

    inv = (np.float32(10000.0) ** (-np.arange(0, DK, 2, dtype=np.float32) / np.float32(DK))).astype(np.float32)
    ang = np.arange(SEQ, dtype=np.float32)[:, None] * inv[None, :]
    rope = np.concatenate([np.cos(ang), np.sin(ang)], 1).astype(np.float32)
    return *packed(parts), *packed(mix_parts), rope


CONST_TABLE, CONST_AT, DECAY_TABLE, DECAY_AT, ROPE_TABLE = host_constants()


def gamma_to(steps):
    return [float((1.0 - 2.0 ** (-5.0 - h)) ** steps) for h in range(HEADS)]


class Chain:

    def __init__(self, eng, sem, start):
        self.eng, self.sem, self.start, self.n = eng, sem, start, 0

    def then(self, ins):
        self.n += 1
        return ins.then_inc(self.sem, 1)

    def wait(self):
        self.eng.wait_ge(self.sem, self.start + self.n)

    def hold(self, hold):
        hold(self.eng, self.sem, self.start + self.n)


class Hold:

    def __init__(self, passed):
        self.passed = passed

    def __call__(self, eng, sem, value):
        eng.wait_ge(sem, value)
        if not isinstance(value, int):
            eng.sem_inc(self.passed, 1)


def broadcast_rows(vec, rows):
    return vec.rearrange("(a n) -> a n", a=1).to_broadcast([rows, vec.shape[0]])


def rstd_guess(act, sem, count, out, mean_square, scale, eps):
    act.activation(out, mean_square, ACT.Ln, scale=scale, bias=eps).then_inc(sem, 1)
    act.wait_ge(sem, count + 1)
    act.activation(out, out, ACT.Exp, scale=-0.5).then_inc(sem, 1)


def rstd_newton(dve, chain, m, rstd, tmp, scale):
    chain.then(dve.tensor_scalar(m, m, scale, EPS, ALU.mult, ALU.add))
    chain.then(dve.tensor_tensor(tmp, rstd, rstd, ALU.mult))
    chain.wait()
    chain.then(dve.tensor_tensor(tmp, tmp, m, ALU.mult))
    chain.wait()
    chain.then(dve.tensor_scalar(tmp, tmp, -0.5, 1.5, ALU.mult, ALU.add))
    chain.wait()
    chain.then(dve.tensor_tensor(rstd, rstd, tmp, ALU.mult))
    chain.wait()


NEWTON_STEPS = 5
ACT_TABLE = "natural_log_exp_and_others"


def first(n):
    return isinstance(n, int) and n == 0


def later(n):
    return not isinstance(n, int) or n > 1


def final(n):
    return isinstance(n, int) and n == TILES


def token_col(n):
    return SEQ if first(n) else (n - 1) * P


def in_blocks(ap):
    return ap.rearrange("p (k r) -> p k r", r=P)


def build(nc, x_prompt, x_sample, cache_k, cache_v, state_ret, norm1_w, w_in, ret_gn_w, w_ret_o, w_sb_o,
          w_out, norm2_w, w_pq, pk_keys, peer_u, peer_v, norm_f_w, consts, decays, rope,
          y_prompt, y_sample, prompt_k, prompt_v, prompt_state, sample_k, sample_v, sample_state):
    scratch = lambda n, s: nc.dram_tensor(n, s, F32).ap()
    proj = scratch("proj", [TOKENS, IN_W])
    skT_d = scratch("skT_d", [TILES, P, HEADS * P])
    x2_d = scratch("x2_d", [TOKENS, D])
    h2_d = scratch("h2_d", [TOKENS, D])
    h2T_d = scratch("h2T_d", [(TILES + 1) * P, KD * P])
    with ExitStack() as ctx:
        sb = lambda n, s, d=F32: ctx.enter_context(nc.sbuf_tensor(n, s, d))
        sem = lambda n: ctx.enter_context(nc.semaphore(n))
        pair = [ctx.enter_context(nc.psum_tensor(f"pair{i}", [P, 2 * BANK], F32)) for i in range(4)]
        cst = sb("cst", [P, CONST_TABLE.shape[1]])
        C = {k: cst[:, a:b] for k, (a, b) in CONST_AT.items()}
        hold = Hold(sem("passed"))
        project(nc, sem, hold, pair, C, cst, consts, x_prompt, x_sample, norm1_w, w_in, proj)
        mix(nc, sem, hold, pair, C, cst, x_prompt, x_sample, cache_k, cache_v, state_ret, ret_gn_w, w_ret_o, w_sb_o, w_out,
            norm2_w, decays, rope, proj, skT_d, x2_d, h2_d, h2T_d, prompt_k, prompt_v, prompt_state, sample_k, sample_v,
            sample_state)
        experts(nc, sem, hold, pair, C, w_pq, pk_keys, peer_u, peer_v, norm_f_w, x2_d, h2_d, h2T_d, y_prompt,
                y_sample)



def project(nc, sem, hold, pair, C, cst, consts, x_prompt, x_sample, norm1_w, w_in, proj):
    NT = TILES + 1
    OUTS = 3
    order = [(SEQ, SAMPLE)] + [(t * P, P) for t in range(TILES)]
    turned_ps = [pair[0], pair[3]]
    ps_out = [pair[1][:, 0:BANK], pair[1][:, BANK:2 * BANK], pair[2][:, 0:BANK]]
    with ExitStack() as ctx:
        sb = lambda n, s, d=F32: ctx.enter_context(nc.sbuf_tensor(n, s, d))
        h_hi = sb("h_hi", [P, KD, TOKENS], F32R)
        h_lo = sb("h_lo", [P, KD, TOKENS], F32R)
        w = sb("w", [P, 2, KD, BANK])
        w_hi = sb("w_hi", [P, 2, KD, BANK], F32R)
        w_lo = sb("w_lo", [P, 2, KD, BANK], F32R)
        out_sb = sb("out_sb", [P, OUTS, BANK])
        xt = sb("xt", [P, 2, D])
        xn = sb("xn", [P, D])
        squares_sb = sb("squares_sb", [P, D])
        g1 = sb("g1", [P, D])
        st = sb("st", [P, 2, 4])
        w_v = w_in[0].rearrange("(k p) n -> p k n", p=P)

        consts_in, g_in = sem("a_consts_in"), sem("a_g_in")
        x_in = [sem(f"a_x_in{i}") for i in range(2)]
        squares, normed, turned = sem("a_squares"), sem("a_normed"), sem("a_turned")
        hi_rdy, lo_rdy, dve_own = sem("a_hi_rdy"), sem("a_lo_rdy"), sem("a_dve_own")
        whi_rdy, wlo_rdy = sem("a_whi_rdy"), sem("a_wlo_rdy")
        w_loaded = [sem(f"a_w_loaded{i}") for i in range(2)]
        ps_ready = [sem(f"a_ps_ready{i}") for i in range(OUTS)]
        copied = [sem(f"a_copied{i}") for i in range(OUTS)]
        stored = [sem(f"a_stored{i}") for i in range(OUTS)]

        def chunks(eng, one):
            with eng.Fori(0, N_CHUNKS // 2 - 1) as c2:
                one(c2 * 2 + 1, 1)
                one(c2 * 2 + 2, 0)
            one(N_CHUNKS - 2, 1)
            one(N_CHUNKS - 1, 0)

        def use_of(c, i):
            return c * (NT // OUTS) + i // OUTS

        def copy(eng, c, i):
            s, use, rows = i % OUTS, use_of(c, i), order[i][1]
            eng.wait_ge(ps_ready[s], use + 1)
            if not (isinstance(c, int) and c == 0 and i < OUTS):
                eng.wait_ge(stored[s], 16 * use)
            if i % 2 == 0:
                ins = eng.activation(out_sb[0:rows, s, :], ps_out[s][0:rows], ACT.Copy)
            else:
                ins = eng.tensor_copy(out_sb[0:rows, s, :], ps_out[s][0:rows])
            ins.then_inc(copied[s], 1)

        def last_product(eng, c, buf):
            if not (isinstance(c, int) and c < 2):
                eng.wait_ge(ps_ready[(NT - 1) % OUTS], (c - 1) * (NT // OUTS))

        with nc.Block() as block:
            @block.sync
            def _(sp):
                for n, (row, rows) in enumerate(order):
                    if n >= 2:
                        sp.wait_ge(normed, n - 1)
                    sp.dma_start(xt[0:rows, n % 2, :], x_sample[0] if n == 0 else x_prompt[0, row:row + rows, :])\
                        .then_inc(x_in[n % 2], 16)
                    if n == 0:
                        sp.dma_start(cst[:, :], consts).then_inc(consts_in, 16)
                        sp.dma_start(g1[:, :], broadcast_rows(norm1_w[0], P)).then_inc(g_in, 16)

                def store(c, buf):
                    for i, (row, rows) in enumerate(order):
                        hold(sp, copied[i % OUTS], use_of(c, i) + 1)
                        sp.dma_start(proj[row:row + rows, bass.ds(c * BANK, BANK)],
                                     out_sb[0:rows, i % OUTS, :]).then_inc(stored[i % OUTS], 16)
                store(0, 0)
                chunks(sp, store)
                for s in stored:
                    hold(sp, s, 16 * N_CHUNKS * (NT // OUTS))

            @block.gpsimd
            def _(pool):
                def load(c, buf):
                    if not (isinstance(c, int) and c < 2):
                        hold(pool, whi_rdy, c - 1)
                        hold(pool, wlo_rdy, c - 1)
                    pool.dma_start(w[:, buf], w_v[:, :, bass.ds(c * BANK, BANK)]).then_inc(w_loaded[buf], 16)
                load(0, 0)
                chunks(pool, load)

            @block.scalar
            def _(act):
                def split(c, buf):
                    act.wait_ge(w_loaded[buf], (c - buf) * 8 + 16)
                    last_product(act, c, buf)
                    act.activation(w_hi[:, buf], w[:, buf], ACT.Copy).then_inc(whi_rdy, 1)

                act.preload_act_table_set(ACT_TABLE)
                act.wait_ge(consts_in, 16)
                for n in range(NT + 3):
                    if n < NT:
                        rows, b = order[n][1], n % 2
                        r = slice(0, rows)
                        act.wait_ge(x_in[b], (n // 2 + 1) * 16)
                        if n >= 2:
                            act.wait_ge(normed, n - 1)
                        if n >= 1:
                            act.wait_ge(squares, 3 * n)
                        act.activation(squares_sb[r, :], xt[r, b, :], ACT.Square, accum_out=st[r, b, 0:1])\
                            .then_inc(squares, 1)
                        act.wait_ge(squares, 3 * n + 1)
                        rstd_guess(act, squares, 3 * n + 1, st[r, b, 1:2], st[r, b, 0:1], 1.0 / D, C["eps"][r])
                    if n in (0, 5):
                        split(n // 5, n // 5)
                    if 1 <= n <= NT:
                        row, rows = order[n - 1]
                        act.wait_ge(turned, n)
                        act.activation(h_hi[:, :, row:row + rows],
                                       in_blocks(turned_ps[(n - 1) % 2][:, :])[:, :, 0:rows], ACT.Copy)\
                            .then_inc(hi_rdy, 1)
                    if n >= 3 and (n - 3) % 2 == 0:
                        copy(act, 0, n - 3)

                def chunk(c, buf):
                    if not (isinstance(c, int) and c == N_CHUNKS - 1):
                        split(c + 1, 1 - buf)
                    for i in range(0, NT, 2):
                        copy(act, c, i)
                chunks(act, chunk)

            @block.vector
            def _(dve):
                def split(c, buf):
                    dve.wait_ge(whi_rdy, c + 1)
                    last_product(dve, c, buf)
                    dve.tensor_tensor(w_lo[:, buf], w[:, buf], w_hi[:, buf].bitcast(F32), ALU.subtract)\
                        .then_inc(wlo_rdy, 1)

                dve.wait_ge(g_in, 16)
                for n in range(NT + 3):
                    if n < NT:
                        rows, b = order[n][1], n % 2
                        r = slice(0, rows)
                        chain = Chain(dve, dve_own, n * NEWTON_STEPS)
                        dve.wait_ge(squares, 3 * n + 3)
                        rstd_newton(dve, chain, st[r, b, 0:1], st[r, b, 1:2], st[r, b, 2:3], 1.0 / D)
                        if n >= 1:
                            dve.wait_ge(turned, n)
                        dve.scalar_tensor_tensor(out=xn[r, :], in0=xt[r, b, :], scalar=st[r, b, 1:2], in1=g1[r, :],
                                                 op0=ALU.mult, op1=ALU.mult).then_inc(normed, 1)
                    if n in (0, 5):
                        split(n // 5, n // 5)
                    if 1 <= n <= NT:
                        row, rows = order[n - 1]
                        dve.wait_ge(hi_rdy, n)
                        dve.tensor_tensor(h_lo[:, :, row:row + rows],
                                          in_blocks(turned_ps[(n - 1) % 2][:, :])[:, :, 0:rows],
                                          h_hi[:, :, row:row + rows].bitcast(F32), ALU.subtract).then_inc(lo_rdy, 1)
                    if n >= 3 and (n - 3) % 2 == 1:
                        copy(dve, 0, n - 3)

                def chunk(c, buf):
                    if not (isinstance(c, int) and c == N_CHUNKS - 1):
                        split(c + 1, 1 - buf)
                    for i in range(1, NT, 2):
                        copy(dve, c, i)
                chunks(dve, chunk)

            @block.tensor
            def _(pe):
                def product(c, buf, i):
                    (row, rows), s = order[i], i % OUTS
                    if not (isinstance(c, int) and c == 0 and i < OUTS):
                        pe.wait_ge(copied[s], use_of(c, i))
                    at = slice(row, row + rows)
                    for k in range(KD):
                        for part, (a, b) in enumerate(((h_hi, w_hi), (h_hi, w_lo), (h_lo, w_hi))):
                            last = pe.matmul(ps_out[s][0:rows], a[:, k, at], b[:, buf, k, :],
                                             start=(k == 0 and part == 0), stop=(k == KD - 1 and part == 2))
                    last.then_inc(ps_ready[s], 1)

                pe.wait_ge(consts_in, 16)
                for n in range(NT + 1):
                    if n < NT:
                        rows = order[n][1]
                        pe.wait_ge(normed, n + 1)
                        if n >= 2:
                            pe.wait_ge(hi_rdy, n - 1)
                            pe.wait_ge(lo_rdy, n - 1)
                        for k in range(KD):
                            last = pe.transpose(turned_ps[n % 2][:, k * P:k * P + rows],
                                                xn[0:rows, k * P:(k + 1) * P], C["ident"][0:rows, 0:rows])
                        last.then_inc(turned, 1)
                    if n >= 1:
                        pe.wait_ge(hi_rdy, n)
                        pe.wait_ge(lo_rdy, n)
                        if n == 1:
                            pe.wait_ge(whi_rdy, 1)
                            pe.wait_ge(wlo_rdy, 1)
                        product(0, 0, n - 1)

                def multiply(c, buf):
                    pe.wait_ge(whi_rdy, c + 1)
                    pe.wait_ge(wlo_rdy, c + 1)
                    for i in range(NT):
                        product(c, buf, i)
                chunks(pe, multiply)


def mix(nc, sem, hold, pair, C, cst, x_prompt, x_sample, cache_k, cache_v, state_ret, ret_gn_w, w_ret_o, w_sb_o, w_out,
        norm2_w, decays, rope, proj, skT_d, x2_d, h2_d, h2T_d, prompt_k, prompt_v, prompt_state, sample_k, sample_v,
        sample_state):
    NT = TILES + 1
    qT_ps, kT_ps = pair[0][:, 0:BANK], pair[0][:, BANK:]
    ret_ps = pair[0]
    sqT_ps, skT_ps = pair[1][:, 0:BANK], pair[1][:, BANK:]
    state_ps = pair[1]
    z_ps, suffix_ps = pair[1][:, 0:BANK], pair[1][:, BANK:]
    sboT_ps, scores_ps = pair[2][:, 0:BANK], pair[2][:, BANK:]
    merge_ps = pair[3]
    with ExitStack() as ctx:
        sb = lambda n, s, d=F32: ctx.enter_context(nc.sbuf_tensor(n, s, d))
        wret = sb("wret", [P, KD, D])
        wsb = sb("wsb", [P, HEADS, D])
        wout = sb("wout", [P, KD, D])
        gnw = sb("gnw", [P, D])
        dec = sb("dec", [P, DECAY_TABLE.shape[1]])
        C = {**C, **{k: dec[:, a:b] for k, (a, b) in DECAY_AT.items()}}
        g2 = sb("g2", [P, D])
        qk = sb("qk", [P, 1024])
        cs = sb("cs", [P, P])
        rv = sb("rv", [P, D])
        sqkv = sb("sqkv", [P, 3 * BANK])
        rg = sb("rg", [P, D])
        gates = sb("gates", [P, 2 * D])
        x = sb("x", [P, D])
        rot = sb("rot", [P, 1024])
        ra = sb("ra", [P, 1024])
        rb = sb("rb", [P, 1024])
        kd = sb("kd", [P, BANK])
        qT = sb("qT", [P, BANK])
        kT = sb("kT", [P, BANK])
        pT = sb("pT", [P, BANK])
        S = sb("S", [P, HEADS, DV])
        ret = sb("ret", [P, D])
        stats = sb("stats", [P, HEADS, 6])
        mv = sb("mv", [P, HEADS, 2])
        gst = sb("gst", [P, 3, HEADS])
        sqT = sb("sqT", [P, BANK])
        skT = sb("skT", [P, BANK])
        KT = sb("KT", [P, BANK])
        V = sb("V", [P, BANK])
        az = sb("az", [P, BANK])
        sp = sb("sp", [P, BANK])
        spsum = sb("spsum", [P, BANK])
        wT = sb("wT", [P, BANK])
        sboT = sb("sboT", [P, BANK])
        big = sb("big", [P, D])
        turnedT = sb("turnedT", [P, KD, P])
        junk = sb("junk", [P, D])
        n2 = sb("n2", [P, 4])
        retT = sb("retT", [P, KD, P])

        names = ("dve_rot k_used gn_in dec_in dve_merge qk_in rv_in sqkv_in rg_in gates_in x_in k_in v_in cache_in "
                 "s_in s_zero dve act qk_rot "
                 "kd_rdy qk_turned qkT_rdy sq_turned skT_rdy scores_rdy pT_rdy state_mm o_rdy ret_rdy S_new sig_rdy "
                 "var_rdy root_rdy r_rdy z_rdy ln_rdy sp_rdy sp_masked suffix_rdy spsum_rdy w_rdy w_masked pv_done "
                 "sbo_rdy r_turned rT_rdy retb_rdy sbb_rdy mixed_rdy m_turned mT_rdy res_rdy x2_rdy sq2_rdy h2_rdy "
                 "h2_turned h2T_rdy kv_out skT_out x2_out h2_out h2T_out state_out cache_turned cacheT_rdy").split()
        s = {n: sem("b_" + n) for n in names}
        weights_in = [sem(f"b_weights_in{i}") for i in range(3)]

        def block_no(n, j=0):
            return j if first(n) else 2 + (n * (n - 1)) // 2 + j

        def h4(ap, cols=P):
            return ap.rearrange("p (h r) -> p h r", h=HEADS)[:, :, 0:cols]

        def tiles(eng, tile):
            tile(0, SAMPLE, None, None)
            tile(1, P, 0, SAMPLE)
            with eng.Fori(2, TILES) as n:
                tile(n, P, n - 1, P)
            tile(TILES, P, TILES - 1, P)

        def past_blocks(eng, n, block):
            if first(n):
                block(block_no(0, 1), 1)
            elif later(n):
                with eng.Fori(1, n) as j:
                    block(block_no(n) + j, j)

        def past_no(n, j):
            return ((n - 1) * (n - 2)) // 2 + j

        with nc.Block() as block:
            @block.sync
            def _(sy):
                sy.dma_start(dec[:, :], decays).then_inc(s["dec_in"], 16)

                def weights(i):
                    to, what = ((wret, w_ret_o), (wsb, w_sb_o), (wout, w_out))[i]
                    sy.dma_start(to[:], what[0].rearrange("(k p) n -> p k n", p=P)).then_inc(weights_in[i], 16)

                def early(n, rows):
                    r = slice(0, rows)
                    at = bass.ds(token_col(n), rows)
                    pos = bass.ds(PAST if first(n) else token_col(n), rows)
                    if not first(n):
                        hold(sy, s["qk_rot"], n)
                    sy.dma_start(qk[r, :], proj[at, RQ:RV]).then_inc(s["qk_in"], 16)
                    sy.dma_start(cs[r, :], rope[pos, :]).then_inc(s["qk_in"], 16)
                    if not first(n):
                        hold(sy, s["sq_turned"], n)
                        hold(sy, s["kv_out"], 32 * n)
                    sy.dma_start(sqkv[r, :], proj[at, SQ:GT]).then_inc(s["sqkv_in"], 16)
                    if not first(n):
                        hold(sy, s["o_rdy"], n)
                    sy.dma_start(rv[r, :], proj[at, RV:RG]).then_inc(s["rv_in"], 16)

                def keys(m, n, j):
                    key_tile = nc.s_assert_within(n - 1 - j, 0, TILES - 2,
                                                  skip_runtime_bounds_check_because="1 <= j < n")
                    hold(sy, s["k_used"], m)
                    sy.dma_start(KT[:, :], skT_d[bass.ds(key_tile, 1)].rearrange("a p c -> (a p) c"))\
                        .then_inc(s["k_in"], 16)

                def tile(n, rows, m, m_rows):
                    r = slice(0, rows)
                    at = bass.ds(token_col(n), rows)
                    if not first(n):
                        hold(sy, s["r_rdy"], n)
                    sy.dma_start(rg[r, :], proj[at, RG:SQ]).then_inc(s["rg_in"], 16)
                    if first(n):
                        sy.dma_start(gnw[:, :], broadcast_rows(ret_gn_w[0], P)).then_inc(s["gn_in"], 16)
                        sy.dma_start(g2[:, :], broadcast_rows(norm2_w[0], P)).then_inc(s["gn_in"], 16)
                        weights(0)
                    else:
                        hold(sy, s["mixed_rdy"], n)
                    sy.dma_start(gates[r, :], proj[at, GT:IN_W]).then_inc(s["gates_in"], 16)
                    if not final(n):
                        early(n + 1, P)
                    if first(n):
                        weights(1)
                        weights(2)
                    if not first(n):
                        if later(n):
                            hold(sy, s["skT_out"], 16 * (n - 1))
                            past_blocks(sy, n, lambda b, j: keys(b, n, j))
                        store_rows(m, m_rows)
                        hold(sy, s["x2_out"], 16 * n)
                    sy.dma_start(x[r, :], x_sample[0] if first(n) else x_prompt[0, at, :]).then_inc(s["x_in"], 16)

                def store_rows(n, rows):
                    at = bass.ds(token_col(n), rows)
                    hold(sy, s["x2_rdy"], n + 1)
                    sy.dma_start(x2_d[at, :], x[0:rows, :]).then_inc(s["x2_out"], 16)
                    hold(sy, s["h2_rdy"], n + 1)
                    sy.dma_start(h2_d[at, :], big[0:rows, :]).then_inc(s["h2_out"], 16)
                early(0, SAMPLE)
                tiles(sy, tile)
                store_rows(TILES, P)
                for o in ("x2_out", "h2_out"):
                    hold(sy, s[o], 16 * NT)

            @block.gpsimd
            def _(pool):
                pool.dma_start(az[:, :], cache_k[0, 0].rearrange("t h d -> t (h d)")).then_inc(s["cache_in"], 16)
                pool.dma_start(S[:], state_ret[0, 0].rearrange("h k v -> k h v")).then_inc(s["s_in"], 16)

                def tile(n, rows, m, m_rows):
                    r = slice(0, rows)
                    at = bass.ds(token_col(n), rows)
                    k_out, v_out = (sample_k, sample_v) if first(n) else (prompt_k, prompt_v)
                    o_at = slice(0, SAMPLE) if first(n) else at
                    if not first(n):
                        hold(pool, s["pv_done"], block_no(n))
                    pool.dma_start(V[r, :], proj[at, SV:GT]).then_inc(s["v_in"], 16)
                    hold(pool, s["sqkv_in"], 16 * (n + 1))
                    for i, o in ((1, k_out), (2, v_out)):
                        pool.dma_start(o[0, 0, o_at].rearrange("t h d -> t (h d)"),
                                       sqkv[r, i * BANK:(i + 1) * BANK]).then_inc(s["kv_out"], 16)
                    if not first(n):
                        if later(n):
                            hold(pool, s["skT_out"], 16 * (n - 1))
                        hold(pool, s["skT_rdy"], 2 * n + 2)
                        pool.dma_start(skT_d[n - 1], skT[:, :]).then_inc(s["skT_out"], 16)
                    if first(n):
                        hold(pool, s["S_new"], 1)
                        pool.dma_start(sample_state[0, 0].rearrange("h k v -> k h v"), S[:])\
                            .then_inc(s["state_out"], 16)
                        hold(pool, s["state_out"], 16)
                        pool.memset(S[:], 0.0).then_inc(s["s_zero"], 1)
                        hold(pool, s["pv_done"], 1)
                        pool.dma_start(V[:, :], cache_v[0, 0].rearrange("t h d -> t (h d)")).then_inc(s["v_in"], 16)

                    def past(m, j):
                        key_tile = nc.s_assert_within(n - 1 - j, 0, TILES - 2, 
                                                      skip_runtime_bounds_check_because="1 <= j < n")
                        hold(pool, s["pv_done"], m)
                        pool.dma_start(V[:, :], proj[bass.ds(key_tile * P, P), SV:GT]).then_inc(s["v_in"], 16)
                    if not first(n):
                        past_blocks(pool, n, past)
                    if not first(n):
                        store_h2T(m, m_rows)

                def store_h2T(n, rows):
                    hold(pool, s["h2T_rdy"], n + 1)
                    pool.dma_start(h2T_d[bass.ds(n * P, P)].rearrange("p (k c) -> p k c", c=P)[:, :, 0:rows],
                                   turnedT[:, :, 0:rows]).then_inc(s["h2T_out"], 16)
                tiles(pool, tile)
                store_h2T(TILES, P)
                pool.dma_start(prompt_state[0, 0].rearrange("h k v -> k h v"), S[:]).then_inc(s["state_out"], 16)
                hold(pool, s["state_out"], 32)
                hold(pool, s["kv_out"], 32 * NT)
                hold(pool, s["skT_out"], 16 * TILES)
                hold(pool, s["h2T_out"], 16 * NT)

            @block.scalar
            def _(act):
                act.preload_act_table_set(ACT_TABLE)

                def turned(to, rows, done):
                    act.activation(to[:, :, 0:rows], in_blocks(merge_ps[:, :])[:, :, 0:rows], ACT.Copy)\
                        .then_inc(s[done], 1)

                def turned_ret(n, rows):
                    act.wait_ge(s["r_turned"], n + 1)
                    if not first(n):
                        act.wait_ge(s["retb_rdy"], n)
                    turned(retT, rows, "rT_rdy")

                def turned_mixed(n, rows):
                    act.wait_ge(s["m_turned"], n + 1)
                    if not first(n):
                        act.wait_ge(s["h2T_out"], 16 * n)
                    turned(turnedT, rows, "mT_rdy")

                def turned_h2(n, rows):
                    act.wait_ge(s["h2_turned"], n + 1)
                    turned(turnedT, rows, "h2T_rdy")

                def attend(m, k_rows, q_rows, between=None):
                    kr = slice(0, k_rows)
                    a, z = h4(az[kr, :], q_rows), h4(z_ps[kr, :], q_rows)
                    act.wait_ge(s["z_rdy"], m + 1)
                    act.activation(a, z, ACT.Abs).then_inc(s["act"], 1)
                    act.wait_ge(s["act"], m * 2 + 1)
                    act.activation(a, a, ACT.Exp, scale=-1.0).then_inc(s["act"], 1)
                    act.wait_ge(s["act"], m * 2 + 2)
                    act.activation(a, a, ACT.Ln, bias=C["one"][kr]).then_inc(s["ln_rdy"], 1)
                    if between:
                        between()
                    act.wait_ge(s["suffix_rdy"], m + 1)
                    act.activation(h4(wT[kr, :], q_rows), h4(suffix_ps[kr, :], q_rows), ACT.Exp).then_inc(s["w_rdy"], 1)

                def sigmoid(count, out, in_):
                    act.activation(out, in_, ACT.Exp, scale=-1.0).then_inc(s["sig_rdy"], 1)
                    act.wait_ge(s["sig_rdy"], count + 1)
                    act.activation(out, out, ACT.Ln, bias=C["one"][0:out.shape[0]]).then_inc(s["sig_rdy"], 1)
                    act.wait_ge(s["sig_rdy"], count + 2)
                    act.activation(out, out, ACT.Exp, scale=-1.0).then_inc(s["sig_rdy"], 1)

                def square(n, rows):
                    r = slice(0, rows)
                    act.wait_ge(s["x2_rdy"], n + 1)
                    if not first(n):
                        act.wait_ge(s["sq2_rdy"], 3 * n)
                    act.activation(junk[r, :], x[r, :], ACT.Square, accum_out=n2[r, 0:1]).then_inc(s["sq2_rdy"], 1)
                    act.wait_ge(s["sq2_rdy"], 3 * n + 1)
                    rstd_guess(act, s["sq2_rdy"], 3 * n + 1, n2[r, 1:2], n2[r, 0:1], 1.0 / D, C["eps"][r])

                def tile(n, rows, m, m_rows):
                    r = slice(0, rows)
                    if first(n):
                        act.wait_ge(s["cache_turned"], 1)
                        act.activation(KT[:, :], z_ps, ACT.Copy).then_inc(s["cacheT_rdy"], 1)
                    act.wait_ge(s["qk_turned"], n + 1)
                    act.activation(h4(qT[:, :], rows), h4(qT_ps, rows), ACT.Copy).then_inc(s["qkT_rdy"], 1)
                    act.activation(h4(kT[:, :], rows), h4(kT_ps, rows), ACT.Copy).then_inc(s["qkT_rdy"], 1)
                    act.wait_ge(s["rg_in"], 16 * (n + 1))
                    sigmoid(6 * n, rb[r, :], rg[r, :])
                    act.wait_ge(s["o_rdy"], n + 1)
                    for h in range(HEADS):
                        act.activation(ret[r, h * DV:(h + 1) * DV], ret_ps[r, h * DV:(h + 1) * DV], ACT.Copy,
                                       scale=C["inter"][r, h:h + 1]).then_inc(s["ret_rdy"], 1)
                    attend(block_no(n), rows, rows,
                           None if first(n) else lambda: turned_mixed(m, m_rows))
                    act.wait_ge(s["var_rdy"], n + 1)
                    rstd_guess(act, s["root_rdy"], 2 * n, gst[r, 0, :], mv[r, :, 1], 1.0, C["eps"][r])
                    if not first(n):
                        square(m, m_rows)
                    past_blocks(act, n, lambda b, j: attend(b, P, rows))
                    if not first(n):
                        turned_h2(m, m_rows)
                    turned_ret(n, rows)
                    act.wait_ge(s["gates_in"], 16 * (n + 1))
                    sigmoid(6 * n + 3, gates[r, :], gates[r, :])
                tiles(act, tile)
                turned_mixed(TILES, P)
                square(TILES, P)
                turned_h2(TILES, P)

            @block.vector
            def _(dve):
                dve.wait_ge(s["dec_in"], 16)
                ROTARY_STEPS = 4
                STEPS = 3 + 7 + NEWTON_STEPS + 4 + 2
                MERGE_STEPS = 2 + NEWTON_STEPS

                def before(kr, q_rows):
                    a = C["before"][kr, 0:q_rows].rearrange("p (a q) -> p a q", a=1)
                    return a.to_broadcast([kr.stop, HEADS, q_rows])

                def attend(n, m, own, k_rows, q_rows, sum_rows):
                    kr = slice(0, k_rows)
                    dve.wait_ge(s["ln_rdy"], m + 1)
                    if not first(m):
                        dve.wait_ge(s["suffix_rdy"], m)
                        dve.wait_ge(s["spsum_rdy"], m)
                    dve.scalar_tensor_tensor(out=h4(sp[kr, :], q_rows), in0=h4(z_ps[kr, :], q_rows), scalar=0.0,
                                             in1=h4(az[kr, :], q_rows), op0=ALU.max, op1=ALU.add)\
                        .then_inc(s["sp_rdy"], 1)
                    add, to = h4(sp[0:sum_rows, :], q_rows), h4(spsum[0:sum_rows, :], q_rows)
                    if own:
                        dve.wait_ge(s["sp_rdy"], m + 1)
                        dve.tensor_tensor(add, add, before(kr, q_rows), ALU.mult).then_inc(s["sp_masked"], 1)
                        dve.wait_ge(s["sp_masked"], n + 1)
                        dve.tensor_copy(to, add).then_inc(s["spsum_rdy"], 1)
                    else:
                        dve.wait_ge(s["suffix_rdy"], m + 1)
                        dve.wait_ge(s["spsum_rdy"], m)
                        dve.wait_ge(s["sp_rdy"], m + 1)
                        dve.tensor_tensor(to, to, add, ALU.add).then_inc(s["spsum_rdy"], 1)

                def rotary(n, rows):
                    r = slice(0, rows)
                    k_dec = C["k_dec_sample"] if first(n) else C["k_dec"]
                    chain = Chain(dve, s["dve_rot"], n * ROTARY_STEPS)
                    dve.wait_ge(s["qk_in"], 32 * (n + 1))
                    if not first(n):
                        dve.wait_ge(s["qk_turned"], n)
                        dve.wait_ge(s["kd_rdy"], n)
                        if later(n):
                            dve.wait_ge(s["mixed_rdy"], n - 1)
                    half = lambda ap, i: ap[r, :].rearrange("p (h two d) -> p two h d", two=2, d=DK // 2)[:, i]
                    cos = cs[r, 0:64].rearrange("p (a d) -> p a d", a=1)
                    sin = cs[r, 64:128].rearrange("p (a d) -> p a d", a=1)
                    chain.then(dve.tensor_tensor(ra[r, :].rearrange("p (h d) -> p h d", d=64),
                                                 qk[r, :].rearrange("p (h d) -> p h d", d=64),
                                                 cos.to_broadcast([rows, 16, 64]), ALU.mult))
                    chain.then(dve.tensor_tensor(half(rot, 0), half(qk, 1), sin.to_broadcast([rows, 8, 64]), ALU.mult))
                    chain.then(dve.tensor_tensor(half(rot, 1), half(qk, 0), sin.to_broadcast([rows, 8, 64]), ALU.mult))
                    chain.wait()
                    chain.then(dve.tensor_tensor(half(rot, 0), half(ra, 0), half(rot, 0), ALU.subtract))
                    dve.tensor_tensor(half(rot, 1), half(ra, 1), half(rot, 1), ALU.add).then_inc(s["qk_rot"], 1)
                    dve.wait_ge(s["qk_rot"], n + 1)
                    chain.wait()
                    if not first(n):
                        dve.wait_ge(s["state_mm"], n)
                    dve.tensor_tensor(kd[r, :], rot[r, BANK:], k_dec[r], ALU.mult).then_inc(s["kd_rdy"], 1)
                    assert chain.n == ROTARY_STEPS

                def tile(n, rows, m, m_rows):
                    r = slice(0, rows)
                    gamma = gamma_to(rows)
                    chain = Chain(dve, s["dve"], n * STEPS)
                    dve.wait_ge(s["sq_turned"], n + 1)
                    dve.tensor_scalar(h4(sqT[:, :], rows), h4(sqT_ps, rows), SCORE_SCALE, None, ALU.mult)\
                        .then_inc(s["skT_rdy"], 1)
                    if later(n):
                        dve.wait_ge(s["skT_out"], 16 * (n - 1))
                    dve.tensor_copy(h4(skT[:, :], rows), h4(skT_ps, rows)).then_inc(s["skT_rdy"], 1)
                    dve.wait_ge(s["scores_rdy"], n + 1)
                    dve.tensor_tensor(h4(pT[r, :], rows), h4(scores_ps[r, :], rows), h4(C["decay"][r], rows),
                                      ALU.mult).then_inc(s["pT_rdy"], 1)
                    if not first(n):
                        merge_ret(m, m_rows)
                    if first(n):
                        dve.wait_ge(s["s_in"], 16)
                    elif not later(n):
                        dve.wait_ge(s["s_zero"], 1)
                    dve.wait_ge(s["o_rdy"], n + 1)
                    for h in range(HEADS):
                        chain.then(dve.scalar_tensor_tensor(out=S[:, h, :], in0=S[:, h, :], scalar=gamma[h],
                                                            in1=state_ps[:, h * DV:(h + 1) * DV], op0=ALU.mult,
                                                            op1=ALU.add)) if h < HEADS - 1 else \
                            dve.scalar_tensor_tensor(out=S[:, h, :], in0=S[:, h, :], scalar=gamma[h],
                                                     in1=state_ps[:, h * DV:(h + 1) * DV], op0=ALU.mult,
                                                     op1=ALU.add).then_inc(s["S_new"], 1)
                    chain.wait()
                    dve.wait_ge(s["S_new"], n + 1)
                    if not first(n):
                        merge_sb(m, m_rows)
                    attend(n, block_no(n), True, rows, rows, rows)
                    dve.wait_ge(s["ret_rdy"], HEADS * (n + 1))
                    for h in range(HEADS):
                        chain.then(dve.bn_stats(stats[r, h, :], ret[r, h * DV:(h + 1) * DV]))
                    hold(dve, s["dve"], chain.start + chain.n)
                    for h in range(HEADS):
                        ins = dve.bn_aggr(mv[r, h, :], stats[r, h, :])
                        if h < HEADS - 1:
                            chain.then(ins)
                    ins.then_inc(s["var_rdy"], 1)
                    dve.wait_ge(s["w_rdy"], block_no(n) + 1)
                    w = h4(wT[r, :], rows)
                    dve.scalar_tensor_tensor(out=w, in0=w, scalar=1.0, in1=before(r, rows), op0=ALU.min,
                                             op1=ALU.mult).then_inc(s["w_masked"], 1)
                    chain.wait()
                    dve.wait_ge(s["var_rdy"], n + 1)
                    dve.wait_ge(s["root_rdy"], 2 * n + 2)
                    rstd_newton(dve, chain, mv[r, :, 1], gst[r, 0, :], gst[r, 1, :], 1.0)
                    for h in range(HEADS):
                        chain.then(dve.tensor_scalar(ret[r, h * DV:(h + 1) * DV], ret[r, h * DV:(h + 1) * DV],
                                                     mv[r, h, 0:1], gst[r, 0, h:h + 1], ALU.subtract, ALU.mult))
                    dve.wait_ge(s["sig_rdy"], 6 * n + 3)
                    chain.then(dve.tensor_tensor(rb[r, :], rb[r, :], rg[r, :], ALU.mult))
                    chain.wait()
                    if first(n):
                        dve.wait_ge(s["gn_in"], 32)
                    chain.then(dve.tensor_tensor(ret[r, :], ret[r, :], gnw[r, :], ALU.mult))
                    chain.wait()
                    dve.tensor_tensor(ret[r, :], ret[r, :], rb[r, :], ALU.mult).then_inc(s["r_rdy"], 1)
                    assert chain.n == STEPS, chain.n
                    if not final(n):
                        rotary(n + 1, P)
                    if not first(n):
                        merge_end(m, m_rows)
                    past_blocks(dve, n, lambda b, j: attend(n, b, False, P, rows, rows))
                    dve.wait_ge(s["pv_done"], block_no(n + 1) if not first(n) else 2)
                    if not first(n):
                        dve.wait_ge(s["sbb_rdy"], n)
                    dve.tensor_copy(h4(sboT[:, :], rows), h4(sboT_ps, rows)).then_inc(s["sbo_rdy"], 1)

                def merge_ret(n, rows):
                    r = slice(0, rows)
                    chain = Chain(dve, s["dve_merge"], n * MERGE_STEPS)
                    dve.wait_ge(s["sig_rdy"], 6 * n + 6)
                    dve.wait_ge(s["retb_rdy"], n + 1)
                    if not first(n):
                        dve.wait_ge(s["h2_out"], 16 * n)
                        dve.wait_ge(s["h2_turned"], n)
                    chain.then(dve.tensor_tensor(big[r, :], merge_ps[r, :], gates[r, 0:D], ALU.mult))

                def merge_sb(n, rows):
                    r = slice(0, rows)
                    chain = Chain(dve, s["dve_merge"], n * MERGE_STEPS + 1)
                    dve.wait_ge(s["sbb_rdy"], n + 1)
                    chain.then(dve.tensor_tensor(ra[r, :], merge_ps[r, :], gates[r, D:], ALU.mult))
                    chain.wait()
                    dve.tensor_tensor(big[r, :], big[r, :], ra[r, :], ALU.add).then_inc(s["mixed_rdy"], 1)

                def merge_end(n, rows):
                    r = slice(0, rows)
                    chain = Chain(dve, s["dve_merge"], n * MERGE_STEPS + 2)
                    dve.wait_ge(s["x_in"], 16 * (n + 1))
                    dve.wait_ge(s["res_rdy"], n + 1)
                    dve.tensor_tensor(x[r, :], x[r, :], merge_ps[r, :], ALU.add).then_inc(s["x2_rdy"], 1)
                    dve.wait_ge(s["sq2_rdy"], 3 * n + 3)
                    rstd_newton(dve, chain, n2[r, 0:1], n2[r, 1:2], n2[r, 2:3], 1.0 / D)
                    dve.scalar_tensor_tensor(out=big[r, :], in0=x[r, :], scalar=n2[r, 1:2], in1=g2[r, :],
                                             op0=ALU.mult, op1=ALU.mult).then_inc(s["h2_rdy"], 1)
                rotary(0, SAMPLE)
                tiles(dve, tile)
                merge_ret(TILES, P)
                merge_sb(TILES, P)
                merge_end(TILES, P)

            @block.tensor
            def _(pe):
                def attend(n, m, j, KTt, k_rows, q_rows, sum_rows, first_gap=None, second_gap=None):
                    kr = slice(0, k_rows)
                    own = isinstance(j, int) and j == 0

                    def scores(ps):
                        for h in range(HEADS):
                            last = pe.matmul(h4(ps[kr, :], q_rows)[:, h], KTt[:, h * P:h * P + k_rows],
                                             h4(sqT[:, :], q_rows)[:, h], start=(h == 0), stop=True,
                                             skip_group_check=True)
                        return last
                    if own:
                        pe.wait_ge(s["skT_rdy"], 2 * n + 2)
                        pe.wait_ge(s["S_new"], n + 1)
                    else:
                        pe.wait_ge(s["sp_rdy"], m)
                        if first(n):
                            pe.wait_ge(s["cacheT_rdy"], 1)
                        else:
                            pe.wait_ge(s["k_in"], 16 * past_no(n, j))
                    scores(z_ps).then_inc(s["z_rdy"], 1)
                    if not own:
                        pe.wait_ge(s["w_rdy"], m)
                    scores(suffix_ps).then_inc(s["k_used"], 1)
                    if first_gap:
                        first_gap()
                    if own:
                        pe.wait_ge(s["sp_masked"], n + 1)
                    else:
                        pe.wait_ge(s["spsum_rdy"], m)
                        pe.matmul(h4(suffix_ps[kr, :], q_rows), C["neg_ones"][0:sum_rows, kr],
                                  h4(spsum[0:sum_rows, :], q_rows), start=False, stop=True, skip_group_check=True)
                        values(n, m - 1, sum_rows, q_rows)
                        pe.wait_ge(s["sp_rdy"], m + 1)
                    pe.matmul(h4(suffix_ps[kr, :], q_rows), C["neg_tri"][kr, kr], h4(sp[kr, :], q_rows), start=False,
                              stop=True, skip_group_check=True).then_inc(s["suffix_rdy"], 1)
                    if second_gap:
                        second_gap()

                def values(n, m, k_rows, q_rows):
                    kr = slice(0, k_rows)
                    pe.wait_ge(s["w_masked"], n + 1)
                    pe.wait_ge(s["w_rdy"], m + 1)
                    pe.wait_ge(s["v_in"], 16 * (m + 1))
                    for h in range(HEADS):
                        last = pe.matmul(h4(sboT_ps, q_rows)[:, h], V[kr, h * P:(h + 1) * P],
                                         h4(wT[kr, :], q_rows)[:, h], start=False, stop=True,
                                         skip_group_check=True)
                    last.then_inc(s["pv_done"], 1)

                def turn(dst, src, rows, blocks):
                    for k in range(blocks):
                        last = pe.transpose(dst[:, k * P:k * P + rows], src[0:rows, k * P:(k + 1) * P],
                                            C["ident"][0:rows, 0:rows])
                    return last

                def wide(dst, lhsT, rhs, blocks, rows):
                    for half in range(2):
                        c = slice(half * BANK, (half + 1) * BANK)
                        for k in range(blocks):
                            last = pe.matmul(dst[0:rows, c], lhsT(k), rhs[:, k, c], start=(k == 0),
                                             stop=(k == blocks - 1))
                    return last

                def tile(n, rows, m, m_rows):
                    r = slice(0, rows)
                    pe.wait_ge(s["qk_rot"], n + 1)
                    if not first(n):
                        pe.wait_ge(s["ret_rdy"], HEADS * n)
                    turn(pair[0], rot, rows, 8).then_inc(s["qk_turned"], 1)
                    if first(n):
                        pe.wait_ge(s["cache_in"], 16)
                        turn(z_ps, az, P, 4).then_inc(s["cache_turned"], 1)
                        pe.wait_ge(s["cacheT_rdy"], 1)
                    else:
                        pe.wait_ge(s["w_rdy"], block_no(n))
                    pe.wait_ge(s["sqkv_in"], 16 * (n + 1))
                    turn(pair[1], sqkv, rows, 8).then_inc(s["sq_turned"], 1)
                    if not first(n):
                        merge_ret(m, m_rows)
                    pe.wait_ge(s["qkT_rdy"], 2 * n + 2)
                    if not first(n):
                        pe.wait_ge(s["pT_rdy"], n)
                    for h in range(HEADS):
                        last = pe.matmul(h4(scores_ps[r, :], rows)[:, h], kT[:, h * P:h * P + rows],
                                         qT[:, h * P:h * P + rows], start=(h == 0), stop=True, skip_group_check=True)
                    last.then_inc(s["scores_rdy"], 1)
                    pe.wait_ge(s["rv_in"], 16 * (n + 1))
                    pe.wait_ge(s["kd_rdy"], n + 1)
                    pe.wait_ge(s["skT_rdy"], 2 * n + 2)
                    for h in range(HEADS):
                        v = slice(h * DV, (h + 1) * DV)
                        last = pe.matmul(state_ps[:, v], kd[r, h * P:(h + 1) * P], rv[r, v], start=(h % 2 == 0),
                                         stop=True, skip_group_check=True)
                    last.then_inc(s["state_mm"], 1)
                    pe.wait_ge(s["pT_rdy"], n + 1)
                    if first(n):
                        pe.wait_ge(s["s_in"], 16)
                    elif not later(n):
                        pe.wait_ge(s["s_zero"], 1)
                    else:
                        pe.wait_ge(s["S_new"], n)
                    for h in range(HEADS):
                        v = slice(h * DV, (h + 1) * DV)
                        pe.matmul(ret_ps[r, v], pT[r, h * P:h * P + rows], rv[r, v], start=(h % 2 == 0), stop=True,
                                  skip_group_check=True)
                        last = pe.matmul(ret_ps[r, v], qT[:, h * P:h * P + rows], S[:, h, :], start=False, stop=True,
                                         skip_group_check=True)
                    last.then_inc(s["o_rdy"], 1)
                    if not first(n):
                        pe.wait_ge(s["sbo_rdy"], n)
                    pe.matmul(h4(sboT_ps, rows), C["zeros"], h4(C["decay"], rows), start=True, stop=True,
                              skip_group_check=True)
                    if first(n):
                        attend(n, block_no(n), 0, skT, rows, rows, rows)
                    else:
                        merge_sb(m, m_rows)
                        attend(n, block_no(n), 0, skT, rows, rows, rows,
                               lambda: turn_mixed(m, m_rows), lambda: residual(m, m_rows))
                    past_blocks(pe, n, lambda b, j: attend(n, b, j, KT, P, rows, rows))
                    if not first(n):
                        turn_h2(m, m_rows)
                        pe.wait_ge(s["h2T_rdy"], n)
                    pe.wait_ge(s["r_rdy"], n + 1)
                    turn(merge_ps, ret, rows, 8).then_inc(s["r_turned"], 1)
                    values(n, block_no(n + 1) - 1 if not first(n) else 1, P, rows)

                def merge_ret(n, rows):
                    if first(n):
                        pe.wait_ge(weights_in[0], 16)
                    pe.wait_ge(s["rT_rdy"], n + 1)
                    wide(merge_ps, lambda k: retT[:, k, 0:rows], wret, KD, rows).then_inc(s["retb_rdy"], 1)

                def merge_sb(n, rows):
                    if first(n):
                        pe.wait_ge(weights_in[1], 16)
                    pe.wait_ge(s["sbo_rdy"], n + 1)
                    pe.wait_ge(s["dve_merge"], n * (2 + NEWTON_STEPS) + 1)
                    wide(merge_ps, lambda k: sboT[:, k * P:k * P + rows], wsb, HEADS, rows).then_inc(s["sbb_rdy"], 1)

                def turn_mixed(n, rows):
                    pe.wait_ge(s["mixed_rdy"], n + 1)
                    turn(merge_ps, big, rows, 8).then_inc(s["m_turned"], 1)

                def residual(n, rows):
                    if first(n):
                        pe.wait_ge(weights_in[2], 16)
                    pe.wait_ge(s["mT_rdy"], n + 1)
                    wide(merge_ps, lambda k: turnedT[:, k, 0:rows], wout, KD, rows).then_inc(s["res_rdy"], 1)

                def turn_h2(n, rows):
                    pe.wait_ge(s["h2_rdy"], n + 1)
                    turn(merge_ps, big, rows, 8).then_inc(s["h2_turned"], 1)
                tiles(pe, tile)
                for part in (merge_ret, merge_sb, turn_mixed, residual, turn_h2):
                    part(TILES, P)


def experts(nc, sem, hold, pair, C, w_pq, pk_keys, peer_u, peer_v, norm_f_w, x2_d, h2_d, h2T_d, y_prompt, y_sample):
    NT = TILES + 1
    SAMPLE_STEPS = PHEADS // 2
    STEPS = SAMPLE_STEPS + TILES * PHEADS
    CHAIN = 6
    ROUTE_STEPS = 5 * SIDES + 3 + 5 * PHEADS + 14
    HALF = SIDES // 2
    GELU_CUBE, GELU_ROOT = 0.044715, float(np.sqrt(2.0 / np.pi))
    acc, q_ps, s_ps = pair[0], pair[1], pair[2]
    with ExitStack() as ctx:
        sb = lambda n, s, d=F32: ctx.enter_context(nc.sbuf_tensor(n, s, d))
        wpq = sb("wpq", [P, KD, PQ_W])
        pkT = sb("pkT", [P, SIDES, P])
        hT = sb("r_hT", [P, KD, P])
        qT = sb("r_qT", [P, HALF, P])
        sc = sb("sc", [P, SIDES, KEYS])
        sc2 = sb("sc2", [P, SIDES, KEYS])
        top = sb("top", [P, SIDES, TOPK])
        topi = sb("topi", [P, SIDES, TOPK], U32)
        topf = sb("topf", [P, SIDES, TOPK])
        best = sb("best", [P, PHEADS, TOPK])
        besti = sb("besti", [P, PHEADS, TOPK], U32)
        parti = sb("parti", [P, 2, PHEADS, TOPK], U32)
        part = sb("part", [P, 2, PHEADS, TOPK])
        found = sb("found", [P, 2, PHEADS, TOPK])
        sums = sb("sums", [P, PHEADS])
        cand = sc[:].rearrange("p (h two) k -> p h (two k)", two=2)
        cand2 = sc2[:].rearrange("p (h two) k -> p h (two k)", two=2)
        grid = lambda ap: ap.rearrange("p h (a b) -> p h a b", a=TOPK)
        keys = sc
        eidx = sb("eidx", [P, STEPS * TOPK], U32)
        gate = sb("gate", [P, STEPS * TOPK])
        ur = sb("ur", [P, RING, D])
        vr = sb("vr", [P, RING, D])
        idx_u = sb("idx_u", [P, 2, TOPK], U32)
        idx_v = sb("idx_v", [P, 2, TOPK], U32)
        h2 = sb("h2", [P, D])
        x2 = sb("x2t", [P, D])
        x3 = sb("x3", [P, D])
        gf = sb("gf", [P, D])
        dots = sb("dots", [P, 2, TOPK])
        ge = sb("ge", [P, 2, TOPK])
        coef = sb("coef", [P, 2, TOPK])
        diag = sb("diag", [P, TOPK, P])
        n3 = sb("n3", [P, 4])

        names = ("gf_in h2_in x2_in u_staged v_staged u_used v_used gelu norm arg_rdy gelu_exp coef_rdy diag_rdy seeded "
                 "x3_rdy sq3_rdy y_rdy y_out").split()
        s = {n: sem("d_" + n) for n in names}
        s.update({n: sem("c_" + n) for n in ("keys_in h_in keys_turned keysT_rdy q_rdy qT_rdy s_rdy sc_rdy dve "
                                             "best_rdy exp_rdy gates_rdy").split()})
        quarters = [slice(i * PQ_W // 4, (i + 1) * PQ_W // 4) for i in range(4)]
        w_in = [sem(f"c_w_in{i}") for i in range(4)]
        u_in = [sem(f"d_u_in{i}") for i in range(RING)]
        v_in = [sem(f"d_v_in{i}") for i in range(RING)]

        def step_no(n, h=0):
            return h if first(n) else n * PHEADS - SAMPLE_STEPS + h

        def tokens(n):
            return SAMPLE if first(n) else P

        def steps(eng, step, routing=None):
            def tile(n):
                count = SAMPLE_STEPS if first(n) else PHEADS
                for h in range(count):
                    def gap(half):
                        if routing and not (isinstance(n, int) and n == TILES):
                            each = PHEADS // count
                            for i in range(each):
                                part = (2 * h + half) * each + i
                                routing(n + 1, part // 2, part % 2)
                    step(n, h, gap)
            tile(0)
            tile(1)
            with eng.Fori(2, TILES) as n:
                tile(n)
            tile(TILES)

        def route_all(part, n):
            for h in range(PHEADS):
                for half in range(2):
                    part(n, h, half)

        def filled(g, k):
            return 16 * (g * (TOPK // RING) + k // RING + 1)

        with nc.Block() as block:
            @block.sync
            def _(sy):
                sy.dma_start(keys[:].rearrange("k (h two) c -> k two h c", two=2)[:, 0],
                             pk_keys[0, 0].rearrange("h k c -> k h c")).then_inc(s["keys_in"], 16)
                sy.dma_start(keys[:].rearrange("k (h two) c -> k two h c", two=2)[:, 1],
                             pk_keys[0, 1].rearrange("h k c -> k h c")).then_inc(s["keys_in"], 16)

                def load_hT(n):
                    if not first(n):
                        hold(sy, s["q_rdy"], 2 * n)
                    for c in (slice(0, SAMPLE), slice(SAMPLE, P)):
                        from_c = slice(0, SAMPLE) if first(n) else c
                        sy.dma_start(hT[:, :, c], h2T_d[bass.ds(n * P, P)]
                                     .rearrange("p (k c) -> p k c", c=P)[:, :, from_c]).then_inc(s["h_in"], 16)

                def store(n, out):
                    hold(sy, s["y_rdy"], n + 1)
                    sy.dma_start(out, x3[0:tokens(n), :]).then_inc(s["y_out"], 16)

                def tile(n):
                    at = bass.ds(token_col(n), tokens(n))
                    if not first(n):
                        hold(sy, s["u_used"], step_no(n) * TOPK)
                    for c in (slice(0, SAMPLE), slice(SAMPLE, P)):
                        half_at = at if first(n) else bass.ds(token_col(n) + c.start, SAMPLE)
                        sy.dma_start(h2[c, :], h2_d[half_at, :]).then_inc(s["h2_in"], 16)
                    if not (isinstance(n, int) and n == TILES):
                        load_hT(n + 1)
                    if not first(n):
                        hold(sy, s["seeded"], n)
                    sy.dma_start(x2[0:tokens(n), :], x2_d[at, :]).then_inc(s["x2_in"], 16)
                    if not first(n):
                        if isinstance(n, int) and n == 1:
                            store(0, y_sample[0])
                        else:
                            store(n - 1, y_prompt[0, bass.ds((n - 2) * P, P), :])
                load_hT(0)
                for i, c in enumerate(quarters):
                    sy.dma_start(wpq[:, :, c], w_pq[0].rearrange("(k p) n -> p k n", p=P)[:, :, c])\
                        .then_inc(w_in[i], 16)
                sy.dma_start(gf[:, :], broadcast_rows(norm_f_w, P)).then_inc(s["gf_in"], 16)
                tile(0)
                tile(1)
                with sy.Fori(2, TILES) as n:
                    tile(n)
                tile(TILES)
                store(TILES, y_prompt[0, SEQ - P:SEQ, :])
                sy.wait_ge(s["y_out"], 16 * NT)

            @block.gpsimd
            def _(pool):
                def gather(ring, table, idx, k, arrived):
                    pool.indirect_dma_start(ring[:, k % RING, :], None, table,
                                            bass.IndirectOffsetOnAxis(ap=idx[:, k:k + 1], axis=0))\
                        .then_inc(arrived[k % RING], 16)

                def gather_v(g, parity, k):
                    if not (first(g) and k < RING):
                        hold(pool, s["v_used"], g * TOPK + k + 1 - RING)
                    gather(vr, peer_v[0], idx_v[:, parity], k, v_in)

                def stage_v(g, parity):
                    if not isinstance(g, int):
                        hold(pool, s["v_used"], (g - 1) * TOPK)
                    pool.tensor_copy(idx_v[:, parity], eidx[:, bass.ds(g * TOPK, TOPK)])\
                        .then_inc(s["v_staged"], 1)
                    hold(pool, s["v_staged"], g + 1)

                def step(n, h, gap):
                    g, parity = step_no(n, h), h % 2
                    if h == 0:
                        hold(pool, s["gates_rdy"], n + 1)
                    if not isinstance(g, int) or g > 1:
                        hold(pool, s["u_used"], (g - 1) * TOPK)
                    pool.tensor_copy(idx_u[:, parity], eidx[:, bass.ds(g * TOPK, TOPK)])\
                        .then_inc(s["u_staged"], 1)
                    hold(pool, s["u_staged"], g + 1)
                    if not first(g):
                        stage_v(g - 1, 1 - parity)
                    for k in range(TOPK):
                        if not (first(g) and k < RING):
                            hold(pool, s["u_used"], g * TOPK + k + 1 - RING)
                        gather(ur, peer_u[0], idx_u[:, parity], k, u_in)
                        if not first(g):
                            gather_v(g - 1, 1 - parity, k)
                steps(pool, step)
                last = STEPS - 1
                pool.wait_ge(s["v_used"], (last - 1) * TOPK)
                pool.tensor_copy(idx_v[:, 1], eidx[:, last * TOPK:]).then_inc(s["v_staged"], 1)
                pool.wait_ge(s["v_staged"], last + 1)
                for k in range(TOPK):
                    gather_v(last, 1, k)

            @block.scalar
            def _(act):
                act.preload_act_table_set(ACT_TABLE)
                for half in range(2):
                    act.wait_ge(s["keys_turned"], half + 1)
                    act.activation(pkT[:, half * 8:half * 8 + 8, :], in_blocks(pair[half + 1][:, :]), ACT.Copy)\
                        .then_inc(s["keysT_rdy"], 1)

                def q_copy(n, i):
                    act.wait_ge(s["q_rdy"], 2 * n + i + 1)
                    if not (first(n) and i == 0):
                        act.wait_ge(s["s_rdy"], 2 * n + i)
                    act.activation(qT[:], in_blocks(q_ps[:, :]), ACT.Copy).then_inc(s["qT_rdy"], 1)

                def s_copy(n, i):
                    act.wait_ge(s["s_rdy"], 2 * n + i + 1)
                    if not first(n):
                        act.wait_ge(s["gates_rdy"], n)
                    act.activation(sc[:, i * HALF:(i + 1) * HALF, :], in_blocks(s_ps[:, :]), ACT.Copy)\
                        .then_inc(s["sc_rdy"], 1)

                def routing(n, h, half):
                    if half == 0:
                        return
                    if h == 0:
                        q_copy(n, 0)
                    elif h == 1:
                        s_copy(n, 0)
                    elif h == 2:
                        q_copy(n, 1)
                    elif h == 3:
                        s_copy(n, 1)
                    elif h == 5:
                        act.wait_ge(s["best_rdy"], n + 1)
                        act.activation(best[:], best[:], ACT.Exp).then_inc(s["exp_rdy"], 1)

                def finish(n):
                    r = slice(0, tokens(n))
                    act.wait_ge(s["v_used"], step_no(n + 1) * TOPK)
                    if not first(n):
                        act.wait_ge(s["y_out"], 16 * n)
                    act.activation(x3[r, :], acc[r, :], ACT.Copy).then_inc(s["x3_rdy"], 1)
                    act.wait_ge(s["x3_rdy"], n + 1)
                    act.activation(acc[r, :], x3[r, :], ACT.Square, accum_out=n3[r, 0:1]).then_inc(s["sq3_rdy"], 1)
                    act.wait_ge(s["sq3_rdy"], 3 * n + 1)
                    rstd_guess(act, s["sq3_rdy"], 3 * n + 1, n3[r, 1:2], n3[r, 0:1], 1.0 / D, C["eps"][r])

                def step(n, h, gap):
                    g, parity = step_no(n, h), h % 2
                    act.wait_ge(s["arg_rdy"], g + 1)
                    act.activation(ge[:, parity], ge[:, parity], ACT.Exp, scale=-2.0 * GELU_ROOT)\
                        .then_inc(s["gelu_exp"], 1)
                    if h == 0 and not first(n):
                        finish(0 if isinstance(n, int) and n == 1 else n - 1)
                    act.wait_ge(s["coef_rdy"], g + 1)
                    for k in range(TOPK):
                        if not first(g):
                            act.wait_ge(s["v_used"], (g - 1) * TOPK + k + 1)
                        act.activation(diag[:, k, :], C["fold" if first(n) else "ident"], ACT.Copy,
                                       scale=coef[:, parity, k:k + 1])\
                            .then_inc(s["diag_rdy"], 1)
                    gap(0)
                    gap(1)
                route_all(routing, 0)
                steps(act, step, routing)
                finish(TILES)

            @block.vector
            def _(dve):
                dve.wait_ge(s["gf_in"], 16)

                def top16(chain, values, spare, out, out_i, count, r):
                    for i in range(count):
                        chain.then(dve.max(out[r, i, 0:8], values[r, i]))
                    chain.hold(hold)
                    for i in range(count):
                        chain.then(dve.max_index(out_i[r, i, 0:8], out[r, i, 0:8], values[r, i]))
                    for i in range(count):
                        chain.then(dve.match_replace(spare[r, i], out[r, i, 0:8], values[r, i], LOWEST))
                    chain.hold(hold)
                    for i in range(count):
                        chain.then(dve.max(out[r, i, 8:16], spare[r, i]))
                    chain.hold(hold)
                    for i in range(count):
                        chain.then(dve.max_index(out_i[r, i, 8:16], out[r, i, 8:16], spare[r, i]))
                    chain.hold(hold)

                def routing(n, h, half):
                    r, rows = slice(0, P), P
                    side = lambda ap, i: ap[r].rearrange("p (h two) k -> p two h k", two=2)[:, i]
                    full = [rows, PHEADS, TOPK, TOPK]
                    over_b = lambda ap: ap.rearrange("p h (k a) -> p h k a", a=1).to_broadcast(full)
                    over_a = lambda ap: ap.rearrange("p h (a k) -> p h a k", a=1).to_broadcast(full)

                    def ranked_keys(chain, i):
                        hot = grid((cand, cand2)[i])[r]
                        iota = C["iota16"][r].rearrange("p (a b k) -> p a b k", a=1, b=1).to_broadcast(full)
                        chain.then(dve.tensor_tensor(hot, over_b(part[r, i]), iota, ALU.is_equal))
                        chain.wait()
                        chain.then(dve.tensor_tensor(hot, hot, over_a(side(topf, i)), ALU.mult))
                        chain.wait()
                        chain.then(dve.tensor_reduce(found[r, i], hot, AX_X, ALU.add))
                        chain.wait()

                    count = HALF // 2
                    if (h, half) in ((2, 1), (3, 0), (4, 0), (4, 1)):
                        i = ((2, 1), (3, 0), (4, 0), (4, 1)).index((h, half))
                        chain = Chain(dve, s["dve"], n * ROUTE_STEPS + i * 5 * count)
                        v = slice(i * count, (i + 1) * count)
                        hold(dve, s["sc_rdy"], 2 * n + i // 2 + 1)
                        top16(chain, sc[:, v], sc2[:, v], top[:, v], topi[:, v], count, r)
                    elif h == 5 and half == 0:
                        chain = Chain(dve, s["dve"], n * ROUTE_STEPS + 5 * SIDES)
                        chain.then(dve.tensor_tensor(grid(cand)[r], over_b(side(top, 0)), over_a(side(top, 1)), ALU.add))
                        chain.then(dve.tensor_copy(topf[r], topi[r]))
                        chain.hold(hold)
                        v = slice(0, count)
                        top16(chain, cand[:, v], cand2[:, v], best[:, v], besti[:, v], count, r)
                    elif h == 5:
                        chain = Chain(dve, s["dve"], n * ROUTE_STEPS + 5 * SIDES + 2 + 5 * count)
                        v = slice(count, PHEADS)
                        top16(chain, cand[:, v], cand2[:, v], best[:, v], besti[:, v], count, r)
                        peak = best[r, :, 0:1].to_broadcast([rows, PHEADS, TOPK])
                        chain.then(dve.tensor_copy(part[r, 0, :, :], peak))
                        chain.wait()
                        dve.tensor_tensor(best[r], best[r], part[r, 0], ALU.subtract).then_inc(s["best_rdy"], 1)
                    elif h == 6 and half == 0:
                        chain = Chain(dve, s["dve"], n * ROUTE_STEPS + 5 * SIDES + 5 * PHEADS + 3)
                        chain.then(dve.tensor_scalar(parti[r, 0], besti[r], 4, None, ALU.logical_shift_right))
                        chain.then(dve.tensor_scalar(parti[r, 1], besti[r], 15, None, ALU.bitwise_and))
                        chain.wait()
                        dve.wait_ge(s["best_rdy"], n + 1)
                        chain.then(dve.tensor_copy(part[r], parti[r]))
                        chain.wait()
                        ranked_keys(chain, 0)
                    elif h == 6:
                        chain = Chain(dve, s["dve"], n * ROUTE_STEPS + 5 * SIDES + 5 * PHEADS + 3 + 6)
                        ranked_keys(chain, 1)
                        chain.then(dve.scalar_tensor_tensor(out=part[r, 0], in0=found[r, 0], scalar=float(KEYS),
                                                            in1=found[r, 1], op0=ALU.mult, op1=ALU.add))
                        chain.wait()
                        by_step = lambda ap: ap.rearrange("p (h k) -> p h k", k=TOPK)
                        if first(n):
                            parts = [(slice(i * SAMPLE, (i + 1) * SAMPLE), slice(0, SAMPLE_STEPS * TOPK),
                                      lambda ap, i=i: ap.rearrange("p (h two) k -> p two h k", two=2)[:, i])
                                     for i in range(2)]
                        else:
                            parts = [(slice(0, P), bass.ds(step_no(n) * TOPK, SLOTS), lambda ap: ap)]
                        for rs, slot, pick in parts:
                            last = dve.tensor_copy(by_step(eidx[rs, slot]), pick(part[rs, 0]))
                        chain.then(last)
                        dve.wait_ge(s["exp_rdy"], n + 1)
                        chain.then(dve.tensor_reduce(sums[r, :], best[r], AX_X, ALU.add))
                        chain.wait()
                        chain.then(dve.reciprocal(sums[r, :], sums[r, :]))
                        chain.wait()
                        chain.then(dve.tensor_copy(part[r, 1], sums[r, :].rearrange("p (h a) -> p h a", a=1)
                                                   .to_broadcast([rows, PHEADS, TOPK])))
                        chain.wait()
                        for rs, slot, pick in parts:
                            last = dve.tensor_tensor(by_step(gate[rs, slot]), pick(best[rs]), pick(part[rs, 1]),
                                                     ALU.mult)
                        last.then_inc(s["gates_rdy"], 1)
                        assert 5 * SIDES + 5 * PHEADS + 9 + chain.n == ROUTE_STEPS, chain.n

                def finish(n):
                    r = slice(0, tokens(n))
                    chain = Chain(dve, s["norm"], n * NEWTON_STEPS)
                    dve.wait_ge(s["sq3_rdy"], 3 * n + 3)
                    rstd_newton(dve, chain, n3[r, 0:1], n3[r, 1:2], n3[r, 2:3], 1.0 / D)
                    dve.scalar_tensor_tensor(out=x3[r, :], in0=x3[r, :], scalar=n3[r, 1:2], in1=gf[r, :],
                                             op0=ALU.mult, op1=ALU.mult).then_inc(s["y_rdy"], 1)

                def step(n, h, gap):
                    r = slice(0, P)
                    g, parity = step_no(n, h), h % 2
                    if h == 0:
                        hold(dve, s["h2_in"], 32 * (n + 1))
                    if not isinstance(g, int) or g > 1:
                        hold(dve, s["coef_rdy"], g - 1)
                    for k in range(TOPK):
                        dve.wait_ge(u_in[k % RING], filled(g, k))
                        dve.tensor_tensor_reduce(ur[r, k % RING, :], ur[r, k % RING, :], h2[r, :], 1.0, 0.0,
                                                 ALU.mult, ALU.add, dots[r, parity, k:k + 1])\
                            .then_inc(s["u_used"], 1)
                        if k == TOPK // 2 - 1:
                            if h == 1 and not first(n):
                                finish(0 if isinstance(n, int) and n == 1 else n - 1)
                            gap(0)
                    chain = Chain(dve, s["gelu"], g * CHAIN)
                    d, t = dots[r, parity], ge[r, parity]
                    dve.wait_ge(s["u_used"], (g + 1) * TOPK)
                    chain.then(dve.tensor_tensor(t, d, d, ALU.mult))
                    chain.wait()
                    chain.then(dve.tensor_scalar(t, t, GELU_CUBE, 1.0, ALU.mult, ALU.add))
                    chain.wait()
                    chain.then(dve.tensor_tensor(t, t, d, ALU.mult))
                    chain.wait()
                    dve.tensor_scalar(t, t, -50.0, None, ALU.max).then_inc(s["arg_rdy"], 1)
                    dve.wait_ge(s["gelu_exp"], g + 1)
                    chain.then(dve.tensor_scalar(t, t, 1.0, None, ALU.add))
                    chain.wait()
                    chain.then(dve.reciprocal(t, t))
                    chain.wait()
                    chain.then(dve.tensor_tensor(t, t, d, ALU.mult))
                    chain.wait()
                    if not isinstance(g, int) or g > 1:
                        dve.wait_ge(s["diag_rdy"], (g - 1) * TOPK)
                    dve.tensor_tensor(coef[r, parity], t, gate[r, bass.ds(g * TOPK, TOPK)], ALU.mult)\
                        .then_inc(s["coef_rdy"], 1)
                    gap(1)
                route_all(routing, 0)
                steps(dve, step, routing)
                finish(TILES)

            @block.tensor
            def _(pe):
                pe.wait_ge(s["keys_in"], 32)
                for half in range(2):
                    for i in range(8):
                        last = pe.transpose(pair[half + 1][:, i * P:(i + 1) * P], keys[:, half * 8 + i, :], C["ident"])
                    last.then_inc(s["keys_turned"], 1)
                pe.wait_ge(s["keysT_rdy"], 2)

                def queries(n, quarter):
                    i = quarter // 2
                    if quarter % 2 == 0:
                        pe.wait_ge(s["h_in"], 32 * (n + 1))
                        if not (first(n) and i == 0):
                            pe.wait_ge(s["qT_rdy"], 2 * n + i)
                    if first(n):
                        pe.wait_ge(w_in[quarter], 16)
                    for j in range(quarter * HALF // 2, (quarter + 1) * HALF // 2):
                        for k in range(KD):
                            last = pe.matmul(q_ps[:, j % HALF * P:(j % HALF + 1) * P],
                                             wpq[:, k, j * P:(j + 1) * P], hT[:, k, :],
                                             start=(k == 0), stop=(k == KD - 1))
                    if quarter % 2:
                        last.then_inc(s["q_rdy"], 1)

                def key_scores(n, i):
                    pe.wait_ge(s["qT_rdy"], 2 * n + i + 1)
                    if not (first(n) and i == 0):
                        pe.wait_ge(s["sc_rdy"], 2 * n + i)
                    for j in range(HALF):
                        last = pe.matmul(s_ps[:, j * P:(j + 1) * P], qT[:, j, :], pkT[:, i * HALF + j, :],
                                         start=True, stop=True)
                    last.then_inc(s["s_rdy"], 1)

                def routing(n, h, half):
                    if (h, half) in ((0, 0), (0, 1), (1, 1), (2, 0)):
                        queries(n, ((0, 0), (0, 1), (1, 1), (2, 0)).index((h, half)))
                    elif (h, half) in ((1, 0), (3, 0)):
                        key_scores(n, h // 2)

                def weigh(g, gap=None):
                    for k in range(TOPK):
                        pe.wait_ge(s["diag_rdy"], g * TOPK + k + 1)
                        pe.wait_ge(v_in[k % RING], filled(g, k))
                        for c in (slice(0, BANK), slice(BANK, 2 * BANK)):
                            last = pe.matmul(acc[:, c], diag[:, k, :], vr[:, k % RING, c], start=False, stop=True,
                                             skip_group_check=True)
                        last.then_inc(s["v_used"], 1)
                        if gap and k == TOPK // 2 - 1:
                            gap(0)
                    if gap:
                        gap(1)

                def step(n, h, gap):
                    r = slice(0, tokens(n))
                    g = step_no(n, h)
                    if h == 1:
                        pe.wait_ge(s["x2_in"], 16 * (n + 1))
                        if not first(n):
                            pe.wait_ge(s["sq3_rdy"], 3 * n - 2)
                        for c in (slice(0, BANK), slice(BANK, 2 * BANK)):
                            last = pe.matmul(acc[:, c], C["ident"][r, :], x2[r, c], start=True, stop=True,
                                             skip_group_check=True)
                        last.then_inc(s["seeded"], 1)
                    if not first(g):
                        weigh(g - 1, gap)
                    else:
                        gap(0)
                        gap(1)
                route_all(routing, 0)
                steps(pe, step, routing)
                weigh(STEPS - 1)


_INS = ["x_prompt", "x_sample", "cache_sb_k", "cache_sb_v", "state_ret", "norm1_w", "w_in", "ret_gn_w", "w_ret_o",
        "w_sb_o", "w_out", "norm2_w", "w_pq", "pk_keys", "peer_u", "peer_v", "norm_f_w"]
_OUTS = [(1, SEQ, D), (1, SAMPLE, D), (1, 1, SEQ, HEADS, DK), (1, 1, SEQ, HEADS, DK), (1, 1, HEADS, DK, DV),
         (1, 1, SAMPLE, HEADS, DK), (1, 1, SAMPLE, HEADS, DK), (1, 1, HEADS, DK, DV)]


def kernel(**inputs):
    import concourse.bacc as bacc
    from concourse.bass_utils import run_bass_kernel_spmd

    nc = bacc.Bacc("TRN2", target_bir_lowering=False, num_devices=1)
    arrays = {name: np.ascontiguousarray(inputs[name]) for name in _INS}
    arrays["consts"] = CONST_TABLE
    arrays["decays"] = DECAY_TABLE
    arrays["rope"] = ROPE_TABLE
    args = [nc.dram_tensor(f"in_{n}", a.shape, mybir.dt.from_np(a.dtype), kind="ExternalInput").ap()
            for n, a in arrays.items()]
    outs = [nc.dram_tensor(f"out_{i}", s, F32, kind="ExternalOutput").ap() for i, s in enumerate(_OUTS)]
    build(nc, *args, *outs)
    got = run_bass_kernel_spmd(nc, [{f"in_{n}": a for n, a in arrays.items()}], core_ids=[0])
    return tuple(got.results[0][f"out_{i}"] for i in range(len(_OUTS)))
```
